# Optimizing a Trainium2 kernel written in Bass

```python
import math
import jax, jax.numpy as jnp
from jax import lax
import numpy as np

D_MODEL = 1024
BATCH = 1
SEQ = 512
DEPTH = 1

EPS = 1e-6
POOL_WINDOWS = (2, 4, 8, 16)
POOL_GROUPS = 4
POOL_WIDTH = D_MODEL // 2
POOL_GROUP_DIM = POOL_WIDTH // POOL_GROUPS
DN_HEADS = 8
DN_HEAD_DIM = 128
DN_WIDTH = DN_HEADS * DN_HEAD_DIM
CONV_WIDTH = 4
CHUNK = 64
PEER_HEADS = 8
N_KEYS = 128
N_EXPERTS = N_KEYS * N_KEYS
PEER_TOPK = 16
PEER_HALF = 128
PEER_QUERY_DIM = 2 * PEER_HALF
PEER_BLOCK = 64
SPLIT_POINTS = (
    POOL_WIDTH,
    POOL_WIDTH + 3 * DN_WIDTH,
    POOL_WIDTH + 4 * DN_WIDTH,
    POOL_WIDTH + 4 * DN_WIDTH + DN_HEADS,
    POOL_WIDTH + 4 * DN_WIDTH + 2 * DN_HEADS,
    POOL_WIDTH + 4 * DN_WIDTH + 2 * DN_HEADS + D_MODEL,
)
IN_COLS = POOL_WIDTH + 4 * DN_WIDTH + 2 * DN_HEADS + 2 * D_MODEL


def rmsnorm(x, w):
    xf = x.astype(jnp.float32)
    y = xf * lax.rsqrt(jnp.mean(xf * xf, axis=-1, keepdims=True) + EPS)
    return (y * w.astype(jnp.float32)).astype(x.dtype)

def l2norm(x):
    return x * lax.rsqrt(jnp.sum(x * x, axis=-1, keepdims=True) + EPS)

def pool_mixer(xa, pool_w, pool_scale):
    b, s, _ = xa.shape
    xf = xa.astype(jnp.float32)
    csum = jnp.cumsum(xf, axis=1)
    count = jnp.arange(1, s + 1, dtype=jnp.float32)[None, :, None]
    groups = []
    for g, win in enumerate(POOL_WINDOWS):
        sl = slice(g * POOL_GROUP_DIM, (g + 1) * POOL_GROUP_DIM)
        c = csum[..., sl]
        c_lag = jnp.pad(c, ((0, 0), (win, 0), (0, 0)))[:, :s]
        mean = (c - c_lag) / jnp.minimum(count, float(win))
        groups.append(mean - xf[..., sl])
    pooled = jnp.stack(groups, axis=2)
    y = jnp.einsum("bsgc,gcd->bsgd", pooled, pool_w.astype(jnp.float32))
    y = y.reshape(b, s, POOL_WIDTH) * pool_scale.astype(jnp.float32)
    return y.astype(xa.dtype)

def causal_dwconv(x, w):
    s = x.shape[1]
    k = w.shape[0]
    xp = jnp.pad(x, ((0, 0), (k - 1, 0), (0, 0)))
    y = xp[:, 0:s] * w[0]
    for j in range(1, k):
        y = y + xp[:, j:j + s] * w[j]
    return y

def gated_delta_rule(q, k, v, g, beta):
    b, h, s, dk = q.shape
    dv = v.shape[-1]
    nc = s // CHUNK
    q = q * (dk ** -0.5)
    k_beta = k * beta[..., None]
    v_beta = v * beta[..., None]

    def chunks(t):
        return t.reshape(b, h, nc, CHUNK, t.shape[-1])

    q, k, k_beta, v_beta = chunks(q), chunks(k), chunks(k_beta), chunks(v_beta)
    gc = jnp.cumsum(g.reshape(b, h, nc, CHUNK), axis=-1)
    tril = jnp.tril(jnp.ones((CHUNK, CHUNK), dtype=bool))
    strict = jnp.tril(jnp.ones((CHUNK, CHUNK), dtype=bool), -1)
    diff = gc[..., :, None] - gc[..., None, :]
    decay = jnp.where(tril, jnp.exp(jnp.where(tril, diff, 0.0)), 0.0)
    lower = jnp.where(strict, jnp.einsum("bhnid,bhnjd->bhnij", k_beta, k) * decay, 0.0)
    eye = jnp.eye(CHUNK, dtype=jnp.float32)
    t_inv = lax.linalg.triangular_solve(eye + lower, jnp.broadcast_to(eye, lower.shape),
                                        left_side=True, lower=True, unit_diagonal=True)
    u = jnp.einsum("bhnij,bhnjd->bhnid", t_inv, v_beta)
    w = jnp.einsum("bhnij,bhnjd->bhnid", t_inv, k_beta * jnp.exp(gc)[..., None])
    attn = jnp.where(tril, jnp.einsum("bhnid,bhnjd->bhnij", q, k) * decay, 0.0)

    def step(state, inp):
        q_i, k_i, u_i, w_i, a_i, g_i = inp
        v_new = u_i - jnp.einsum("bhcd,bhde->bhce", w_i, state)
        o = (jnp.einsum("bhcd,bhde->bhce", q_i * jnp.exp(g_i)[..., None], state)
             + jnp.einsum("bhij,bhje->bhie", a_i, v_new))
        g_last = g_i[..., -1]
        k_dec = k_i * jnp.exp(g_last[..., None] - g_i)[..., None]
        state = state * jnp.exp(g_last)[..., None, None] + jnp.einsum("bhcd,bhce->bhde", k_dec, v_new)
        return state, o

    xs = tuple(jnp.moveaxis(t, 2, 0) for t in (q, k, u, w, attn, gc))
    state0 = jnp.zeros((b, h, dk, dv), dtype=jnp.float32)
    _, o = lax.scan(step, state0, xs)
    return jnp.moveaxis(o, 0, 2).reshape(b, h, s, dv)

def deltanet_branch(qkv, z, beta_logit, a_logit, conv_w, a_log, dt_bias, dn_norm_w):
    b, s, _ = qkv.shape
    out_dtype = qkv.dtype
    f32 = jnp.float32
    qkv = jax.nn.silu(causal_dwconv(qkv.astype(f32), conv_w.astype(f32)))
    q, k, v = jnp.split(qkv, 3, axis=-1)

    def heads(t):
        return t.reshape(b, s, DN_HEADS, DN_HEAD_DIM).transpose(0, 2, 1, 3)

    q = l2norm(heads(q))
    k = l2norm(heads(k))
    v = heads(v)
    beta = jax.nn.sigmoid(beta_logit.astype(f32)).transpose(0, 2, 1)
    g = (-jnp.exp(a_log.astype(f32))
         * jax.nn.softplus(a_logit.astype(f32) + dt_bias.astype(f32))).transpose(0, 2, 1)
    o = gated_delta_rule(q, k, v, g, beta).transpose(0, 2, 1, 3)
    zf = z.astype(f32).reshape(b, s, DN_HEADS, DN_HEAD_DIM)
    o = rmsnorm(o, dn_norm_w) * jax.nn.silu(zf)
    return o.reshape(b, s, DN_WIDTH).astype(out_dtype)

def peer_ffn(x, w_query, keys_1, keys_2, expert_down, expert_up):
    b, s, d = x.shape
    f32 = jnp.float32
    q = (x @ w_query).astype(f32).reshape(b, s, PEER_HEADS, 2, PEER_HALF)
    s1 = jnp.einsum("bshc,hkc->bshk", q[..., 0, :], keys_1.astype(f32))
    s2 = jnp.einsum("bshc,hkc->bshk", q[..., 1, :], keys_2.astype(f32))
    v1, i1 = lax.top_k(s1, PEER_TOPK)
    v2, i2 = lax.top_k(s2, PEER_TOPK)
    cand_score = (v1[..., :, None] + v2[..., None, :]).reshape(b, s, PEER_HEADS, PEER_TOPK * PEER_TOPK)
    cand_idx = (i1[..., :, None] * N_KEYS + i2[..., None, :]).reshape(b, s, PEER_HEADS, PEER_TOPK * PEER_TOPK)
    top_score, pos = lax.top_k(cand_score, PEER_TOPK)
    experts = jnp.take_along_axis(cand_idx, pos, axis=-1)
    gates = jax.nn.softmax(top_score, axis=-1)

    nb = s // PEER_BLOCK
    xb = x.reshape(b, nb, PEER_BLOCK, d).transpose(1, 0, 2, 3)
    eb = experts.reshape(b, nb, PEER_BLOCK, PEER_HEADS, PEER_TOPK).transpose(1, 0, 2, 3, 4)
    gb = gates.reshape(b, nb, PEER_BLOCK, PEER_HEADS, PEER_TOPK).transpose(1, 0, 2, 3, 4)

    def block(args):
        xi, ei, gi = args
        u = jnp.take(expert_down, ei, axis=0)
        act = jax.nn.gelu(jnp.einsum("btd,bthkd->bthk", xi, u).astype(f32), approximate=False)
        vv = jnp.take(expert_up, ei, axis=0)
        return jnp.einsum("bthk,bthkd->btd", (gi * act).astype(x.dtype), vv)

    y = lax.map(block, (xb, eb, gb))
    return y.transpose(1, 0, 2, 3).reshape(b, s, d)

def first_inputs(seed: int = 0) -> dict:
    key = jax.random.key(seed)
    ks = jax.random.split(key, 20)
    f32 = jnp.float32

    def nrm(k, shape, scale):
        return scale * jax.random.normal(k, shape, f32)

    def gain(k, shape):
        return 1.0 + 0.05 * jax.random.normal(k, shape, f32)

    dt = jnp.exp(jax.random.uniform(ks[7], (DEPTH, DN_HEADS), f32, math.log(1e-3), math.log(1e-1)))
    dt_bias = dt + jnp.log(-jnp.expm1(-dt))
    a_log = jnp.log(jax.random.uniform(ks[8], (DEPTH, DN_HEADS), f32, 1.0, 16.0))
    return {
        "x": jax.random.normal(ks[0], (BATCH, SEQ, D_MODEL), f32),
        "mix_norm_w": gain(ks[1], (DEPTH, D_MODEL)),
        "w_in": nrm(ks[2], (DEPTH, D_MODEL, IN_COLS), D_MODEL ** -0.5),
        "pool_w": nrm(ks[3], (DEPTH, POOL_GROUPS, POOL_GROUP_DIM, POOL_GROUP_DIM), POOL_GROUP_DIM ** -0.5),
        "pool_scale": 1.0 + 0.1 * jax.random.normal(ks[4], (DEPTH, POOL_WIDTH), f32),
        "conv_w": nrm(ks[5], (DEPTH, CONV_WIDTH, 3 * DN_WIDTH), CONV_WIDTH ** -0.5),
        "a_log": a_log,
        "dt_bias": dt_bias,
        "dn_norm_w": gain(ks[6], (DEPTH, DN_HEAD_DIM)),
        "w_pool_up": nrm(ks[9], (DEPTH, POOL_WIDTH, D_MODEL), POOL_WIDTH ** -0.5),
        "w_dn_up": nrm(ks[10], (DEPTH, DN_WIDTH, D_MODEL), DN_WIDTH ** -0.5),
        "w_mix_out": nrm(ks[11], (DEPTH, D_MODEL, D_MODEL), D_MODEL ** -0.5),
        "ffn_norm_w": gain(ks[12], (DEPTH, D_MODEL)),
        "peer_w_query": nrm(ks[13], (DEPTH, D_MODEL, PEER_HEADS * PEER_QUERY_DIM), D_MODEL ** -0.5),
        "peer_keys_1": nrm(ks[14], (DEPTH, PEER_HEADS, N_KEYS, PEER_HALF), PEER_HALF ** -0.5),
        "peer_keys_2": nrm(ks[15], (DEPTH, PEER_HEADS, N_KEYS, PEER_HALF), PEER_HALF ** -0.5),
        "peer_down": nrm(ks[16], (DEPTH, N_EXPERTS, D_MODEL), D_MODEL ** -0.5),
        "peer_up": nrm(ks[17], (DEPTH, N_EXPERTS, D_MODEL), PEER_HEADS ** -0.5),
        "final_norm_w": gain(ks[18], (D_MODEL,)),
    }

def first_block(x, mix_norm_w, w_in, pool_w, pool_scale, conv_w, a_log, dt_bias, dn_norm_w,
              w_pool_up, w_dn_up, w_mix_out, ffn_norm_w, peer_w_query, peer_keys_1,
              peer_keys_2, peer_down, peer_up, final_norm_w):
    h = x
    for l in range(DEPTH):
        xn = rmsnorm(h, mix_norm_w[l])
        proj = xn @ w_in[l]
        xa, qkv, z, beta_logit, a_logit, gate_a, gate_b = jnp.split(proj, SPLIT_POINTS, axis=-1)
        y_a = pool_mixer(xa, pool_w[l], pool_scale[l]) @ w_pool_up[l]
        y_b = deltanet_branch(qkv, z, beta_logit, a_logit, conv_w[l], a_log[l], dt_bias[l],
                              dn_norm_w[l]) @ w_dn_up[l]
        merged = jax.nn.sigmoid(gate_a) * y_a + jax.nn.sigmoid(gate_b) * y_b
        h = h + merged @ w_mix_out[l]
        h = h + peer_ffn(rmsnorm(h, ffn_norm_w[l]), peer_w_query[l], peer_keys_1[l],
                         peer_keys_2[l], peer_down[l], peer_up[l])
    return rmsnorm(h, final_norm_w)


SSD_HEADS = 16
SSD_HEAD_DIM = 64
SSD_INNER = SSD_HEADS * SSD_HEAD_DIM
SSD_GROUPS = 2
SSD_STATE = 128
SSD_CONV = 4
SSD_SCAN_CHUNK = CHUNK
CONV_DIM = SSD_INNER + 2 * SSD_GROUPS * SSD_STATE
SB_HEADS = 16
SB_HEAD_DIM = 64
SB_INNER = SB_HEADS * SB_HEAD_DIM
SB_BLOCK = 128
N_BRANCH = 2
IN_SIZES = (SSD_INNER, CONV_DIM, SSD_HEADS, SB_INNER, SB_INNER, SB_INNER, SB_INNER, N_BRANCH * D_MODEL)
IN_COLS_2 = sum(IN_SIZES)


def _split_points():
    pts, acc = [], 0
    for s in IN_SIZES[:-1]:
        acc += s
        pts.append(acc)
    return pts

def rmsnorm_2(x, w):
    xf = x.astype(jnp.float32)
    y = xf * lax.rsqrt(jnp.mean(xf * xf, axis=-1, keepdims=True) + EPS)
    return (y * w.astype(jnp.float32)).astype(x.dtype)

def gated_group_rmsnorm(y, z, w, groups):
    g = (y.astype(jnp.float32) * jax.nn.silu(z.astype(jnp.float32)))
    g = g.reshape(y.shape[:-1] + (groups, y.shape[-1] // groups))
    g = g * lax.rsqrt(jnp.mean(g * g, axis=-1, keepdims=True) + EPS)
    return (g.reshape(y.shape) * w.astype(jnp.float32)).astype(y.dtype)

def ssd_scan(xh, dt, a, bmat, cmat, d_skip):
    bsz, L, H, P = xh.shape
    G, N = bmat.shape[2], bmat.shape[3]
    R = H // G
    T = SSD_SCAN_CHUNK
    NC = L // T
    x_dt = (xh * dt[..., None]).reshape(bsz, NC, T, G, R, P)
    a_dt = jnp.transpose((dt * a).reshape(bsz, NC, T, G, R), (0, 3, 4, 1, 2))
    a_cs = jnp.cumsum(a_dt, axis=-1)
    bc = bmat.reshape(bsz, NC, T, G, N)
    cc = cmat.reshape(bsz, NC, T, G, N)
    seg = a_cs[..., :, None] - a_cs[..., None, :]
    causal = jnp.tril(jnp.ones((T, T), dtype=bool))
    decay = jnp.exp(jnp.where(causal, seg, -jnp.inf))
    scores = jnp.einsum('bclgn,bcsgn->bgcls', cc, bc)
    attn = scores[:, :, None] * decay
    y_diag = jnp.einsum('bgrcls,bcsgrp->bclgrp', attn, x_dt)
    decay_states = jnp.exp(a_cs[..., -1:] - a_cs)
    states = jnp.einsum('bclgn,bgrcl,bclgrp->bcgrpn', bc, decay_states, x_dt)
    chunk_decay = jnp.exp(a_cs[..., -1])

    def step(carry, inp):
        st, dec = inp
        new = carry * dec[..., None, None] + st
        return new, carry

    init = jnp.zeros((bsz, G, R, P, N), dtype=xh.dtype)
    _, prev = lax.scan(step, init, (jnp.moveaxis(states, 1, 0), jnp.moveaxis(chunk_decay, -1, 0)))
    prev = jnp.moveaxis(prev, 0, 1)
    y_off = jnp.einsum('bclgn,bcgrpn,bgrcl->bclgrp', cc, prev, jnp.exp(a_cs))
    y = (y_diag + y_off).reshape(bsz, L, H, P)
    return y + xh * d_skip[:, None]

def stick_breaking(q, k, v):
    bsz, L, H, Dh = q.shape
    scale = Dh ** -0.5
    outs = []
    for blk in range(L // SB_BLOCK):
        q0 = blk * SB_BLOCK
        kend = q0 + SB_BLOCK
        logits = jnp.einsum('bqhd,bkhd->bhqk', q[:, q0:kend], k[:, :kend]).astype(jnp.float32) * scale
        qi = q0 + jnp.arange(SB_BLOCK)[:, None]
        ki = jnp.arange(kend)[None, :]
        mask = ki < qi
        log_fail = jnp.where(mask, jax.nn.log_sigmoid(-logits), 0.0)
        between = lax.cumsum(log_fail, axis=3, reverse=True) - log_fail
        w = jnp.where(mask, jnp.exp(jax.nn.log_sigmoid(logits) + between), 0.0)
        outs.append(jnp.einsum('bhqk,bkhd->bqhd', w.astype(v.dtype), v[:, :kend]))
    return jnp.concatenate(outs, axis=1)

def hybrid_layer(x, norm_pre, w_in, b_gate, conv_w, conv_b, dt_bias, a_log, d_skip,
                 ssd_norm, w_ssd_proj, w_sb_proj, w_out, norm_post):
    bsz, L, _ = x.shape
    h = rmsnorm_2(x, norm_pre)
    proj = jnp.einsum('bld,de->ble', h, w_in)
    z_ssd, xbc, dt_raw, q, k, v, z_sb, gates = jnp.split(proj, _split_points(), axis=-1)

    xbc = lax.conv_general_dilated(
        xbc, conv_w[:, None, :], window_strides=(1,), padding=[(SSD_CONV - 1, 0)],
        dimension_numbers=('NWC', 'WIO', 'NWC'), feature_group_count=CONV_DIM) + conv_b
    xbc = jax.nn.silu(xbc)
    xs, bm, cm = jnp.split(xbc, [SSD_INNER, SSD_INNER + SSD_GROUPS * SSD_STATE], axis=-1)
    dt = jax.nn.softplus(dt_raw.astype(jnp.float32) + dt_bias.astype(jnp.float32))
    a = -jnp.exp(a_log.astype(jnp.float32))
    y = ssd_scan(xs.reshape(bsz, L, SSD_HEADS, SSD_HEAD_DIM).astype(jnp.float32), dt, a,
                 bm.reshape(bsz, L, SSD_GROUPS, SSD_STATE).astype(jnp.float32),
                 cm.reshape(bsz, L, SSD_GROUPS, SSD_STATE).astype(jnp.float32),
                 d_skip.astype(jnp.float32))
    y = y.reshape(bsz, L, SSD_INNER).astype(x.dtype)
    y = gated_group_rmsnorm(y, z_ssd, ssd_norm, SSD_GROUPS)
    y_ssd = jnp.einsum('ble,ed->bld', y, w_ssd_proj)

    o = stick_breaking(q.reshape(bsz, L, SB_HEADS, SB_HEAD_DIM),
                       k.reshape(bsz, L, SB_HEADS, SB_HEAD_DIM),
                       v.reshape(bsz, L, SB_HEADS, SB_HEAD_DIM)).reshape(bsz, L, SB_INNER)
    y_sb = jnp.einsum('ble,ed->bld', o * jax.nn.silu(z_sb), w_sb_proj)

    g = jax.nn.sigmoid(gates + b_gate)
    g_ssd, g_sb = jnp.split(g, [D_MODEL], axis=-1)
    merged = g_ssd * y_ssd + g_sb * y_sb
    out = jnp.einsum('bld,de->ble', merged, w_out)
    return x + rmsnorm_2(out, norm_post)

def second_inputs(seed: int = 0) -> dict:
    key = jax.random.key(seed)
    ks = jax.random.split(key, 16)
    f32 = jnp.float32
    x = jax.random.normal(ks[0], (BATCH, SEQ, D_MODEL), f32)
    norm_pre = 1.0 + 0.05 * jax.random.normal(ks[1], (DEPTH, D_MODEL), f32)
    w_in = jax.random.normal(ks[2], (DEPTH, D_MODEL, IN_COLS_2), f32) * D_MODEL ** -0.5
    b_gate = 0.02 * jax.random.normal(ks[3], (DEPTH, N_BRANCH * D_MODEL), f32)
    conv_w = jax.random.normal(ks[4], (DEPTH, SSD_CONV, CONV_DIM), f32) * SSD_CONV ** -0.5
    conv_b = 0.02 * jax.random.normal(ks[5], (DEPTH, CONV_DIM), f32)
    u = jax.random.uniform(ks[6], (DEPTH, SSD_HEADS), f32)
    dt0 = jnp.exp(u * (math.log(0.1) - math.log(0.001)) + math.log(0.001))
    dt_bias = dt0 + jnp.log(-jnp.expm1(-dt0))
    a_log = jnp.log(jax.random.uniform(ks[7], (DEPTH, SSD_HEADS), f32, 1.0, 16.0))
    d_skip = 1.0 + 0.05 * jax.random.normal(ks[8], (DEPTH, SSD_HEADS), f32)
    ssd_norm = 1.0 + 0.05 * jax.random.normal(ks[9], (DEPTH, SSD_INNER), f32)
    w_ssd_proj = jax.random.normal(ks[10], (DEPTH, SSD_INNER, D_MODEL), f32) * SSD_INNER ** -0.5
    w_sb_proj = jax.random.normal(ks[11], (DEPTH, SB_INNER, D_MODEL), f32) * SB_INNER ** -0.5
    w_out = jax.random.normal(ks[12], (DEPTH, D_MODEL, D_MODEL), f32) * D_MODEL ** -0.5
    norm_post = 1.0 + 0.05 * jax.random.normal(ks[13], (DEPTH, D_MODEL), f32)
    return {"x": x, "norm_pre": norm_pre, "w_in": w_in, "b_gate": b_gate,
            "conv_w": conv_w, "conv_b": conv_b, "dt_bias": dt_bias, "a_log": a_log,
            "d_skip": d_skip, "ssd_norm": ssd_norm, "w_ssd_proj": w_ssd_proj,
            "w_sb_proj": w_sb_proj, "w_out": w_out, "norm_post": norm_post}

def second_block(x, norm_pre, w_in, b_gate, conv_w, conv_b, dt_bias, a_log, d_skip,
              ssd_norm, w_ssd_proj, w_sb_proj, w_out, norm_post):
    for layer in range(DEPTH):
        x = hybrid_layer(x, norm_pre[layer], w_in[layer], b_gate[layer], conv_w[layer],
                         conv_b[layer], dt_bias[layer], a_log[layer], d_skip[layer],
                         ssd_norm[layer], w_ssd_proj[layer], w_sb_proj[layer],
                         w_out[layer], norm_post[layer])
    return x


def setup_inputs(seed=0):
    out = dict(first_inputs(seed))
    for name, value in second_inputs(seed + 1).items():
        if name != "x":
            out[name + "_2"] = value
    return out


def reference(
    x, mix_norm_w, w_in, pool_w, pool_scale, conv_w, a_log, dt_bias, dn_norm_w, w_pool_up,
    w_dn_up, w_mix_out, ffn_norm_w, peer_w_query, peer_keys_1, peer_keys_2, peer_down, peer_up,
    final_norm_w, norm_pre_2, w_in_2, b_gate_2, conv_w_2, conv_b_2, dt_bias_2, a_log_2,
    d_skip_2, ssd_norm_2, w_ssd_proj_2, w_sb_proj_2, w_out_2, norm_post_2,
):
    x = first_block(
        x, mix_norm_w, w_in, pool_w, pool_scale, conv_w, a_log, dt_bias, dn_norm_w, w_pool_up,
        w_dn_up, w_mix_out, ffn_norm_w, peer_w_query, peer_keys_1, peer_keys_2, peer_down,
        peer_up, final_norm_w,
    )
    return second_block(
        x, norm_pre_2, w_in_2, b_gate_2, conv_w_2, conv_b_2, dt_bias_2, a_log_2, d_skip_2,
        ssd_norm_2, w_ssd_proj_2, w_sb_proj_2, w_out_2, norm_post_2,
    )


_drawn_inputs = setup_inputs


def setup_inputs(seed=0):
    import zlib

    import numpy as np

    out = dict(_drawn_inputs(seed))
    spreads = {}
    factors = {'b_gate_2': 8.0, 'conv_b_2': 3.309}
    for name, (base, spread) in spreads.items():
        noise = np.random.default_rng([zlib.crc32(name.encode()), seed]).standard_normal(out[name].shape)
        drawn = base * np.exp(spread * noise) if base else spread * noise
        out[name] = __import__('jax').numpy.asarray(drawn.astype(out[name].dtype))
    for name, factor in factors.items():
        out[name] = (out[name] * factor).astype(out[name].dtype)
    return out
```

```python
from contextlib import ExitStack, contextmanager

import numpy as np

import concourse.bass as bass
from concourse import mybir

ALU = mybir.AluOpType
ACT = mybir.ActivationFunctionType
AX = mybir.AxisListType
F32 = mybir.dt.float32
F32R = mybir.dt.float32r
U32 = mybir.dt.uint32

P = 128
D = 1024
S = 512
DC = D // P
TT = S // P
EPS = 1e-6
RAW = 4
TILE = 1024

POOL_WINDOWS = (2, 4, 8, 16)
HEADS = 8
TAPS = 4
TOPK = 16
N_KEYS = 128
SSD_HEADS = 16
SB_HEADS = 16
LEVELS = 7

N_PROJ1 = 36
N_MERGE = 32
N_OUT = 8
N_QUERY = 16
N_PEER = 2 * N_KEYS
N_PROJ2A = 20
N_PROJ2B = 32
N_TILES = N_PROJ1 + N_MERGE + N_OUT + N_QUERY + N_PEER + N_PROJ2A + N_PROJ2B + N_MERGE + N_OUT

COLS = {}


def _col(name, n):
    COLS[name] = (sum(w for _, w in COLS.values()), n)


for _name, _n in (("mix_norm", 8), ("ffn_norm", 8), ("pre2", 8), ("pool_scale", 4), ("conv1", 24 * TAPS),
                  ("dn_norm", 1), ("conv2", 12 * TAPS), ("conv2_b", 12), ("ssd_norm", 8), ("gate2_b", 16),
                  ("d_skip", 8)):
    _col(_name, _n)
N_COLS = sum(w for _, w in COLS.values())


PAGE = 2048
SBUF_FROM = 16512
MISC, RAW_AT, SPLIT_AT, X_AT, R = 0, 6, 14, 22, 38
H_AT = R + 57
N_PAGES = R + 65


class Program:

    def __init__(self, nc, io):
        self.nc, self.io = nc, io
        self.base = 0
        self.total = io["stream"].shape[0]
        self.names = 0
        self.consts_end = 0

    def at(self, name, page, shape, dt=F32):
        self.names += 1
        assert page + int(np.prod(shape[1:])) * 4 / PAGE <= N_PAGES, (name, page, shape)
        return self.nc.alloc_sbuf_tensor_at(f"{name}_{self.names}", list(shape), dt,
                                            offset=SBUF_FROM + int(page * PAGE))

    def const(self, name, shape, dt=F32):
        at = self.consts_end
        self.consts_end += -(-int(np.prod(shape[1:])) * 4 // 32) * 32
        assert self.consts_end <= RAW_AT * PAGE, self.consts_end
        return self.at(name, MISC + at / PAGE, shape, dt)

    def banks(self, stack, n, name="bank"):
        self.names += 1
        return [stack.enter_context(self.nc.psum_tensor(f"{name}{b}_{self.names}", [P, 512], F32)) for b in range(n)]

    def sem(self, name):
        self.names += 1
        return self.nc.alloc_semaphore(f"{name}_{self.names}")

    def run(self, stage, *args, **kw):
        before = self.nc.snapshot_sems()
        result = stage(self, *args, **kw)
        self.nc.clear_and_free_semaphores(self.nc.allocated_since(before))
        self.nc.all_engine_barrier()
        return result

    def col(self, name, i=0):
        at = COLS[name][0] + i
        return self.cols[:, at:at + 1]


@contextmanager
def steps(eng, start, end, step):
    with eng.Fori(start // step, end // step) as k:
        yield k * step



def stream_load(g, sp, n):
    base = g.base
    n = min(n, g.total - RAW - base)
    if n <= 0:
        return
    with steps(sp, 0, n, RAW) as i:
        for j in range(RAW):
            sp.wait_ge(g.high_split, i + (base + j + 1))
            sp.wait_ge(g.low_split, i + (base + j + 1))
            sp.dma_start(g.raw[:, j, :], g.io["stream"][i + (base + RAW + j)]).then_inc(g.raw_loaded[j], 16)


def split_high(g, act, i, j, slots=2):
    t = g.base + j
    act.wait_ge(g.raw_loaded[t % RAW], 4 * i + 16 * (t // RAW + 1))
    act.wait_ge(g.tile_used, i + (t + 3 - slots))
    act.activation(g.high[t % slots], g.raw[:, t % RAW, :], ACT.Copy).then_inc(g.high_split, 1)


def split_low(g, dve, i, j, slots=2):
    t = g.base + j
    dve.wait_ge(g.raw_loaded[t % RAW], 4 * i + 16 * (t // RAW + 1))
    dve.wait_ge(g.high_split, i + (t + 1))
    dve.tensor_tensor(g.low[t % slots], g.raw[:, t % RAW, :], g.high[t % slots], ALU.subtract).then_inc(g.low_split, 1)


def tile_done(g, eng, i, j):
    eng.wait_ge(g.tile_used, i + (g.base + j + 3))


def mm_columns(g, pe, t, out, chunks=DC, x=None):
    xh, xl = x or (g.xh, g.xl)
    hi, lo = g.high[t % 2], g.low[t % 2]
    for c in range(chunks):
        w = slice(c * P, c * P + P)
        pe.matmul(out, hi[:, w], xh[:, c, :], start=(c == 0), stop=False)
        pe.matmul(out, hi[:, w], xl[:, c, :], start=False, stop=False)
        last = pe.matmul(out, lo[:, w], xh[:, c, :], start=False, stop=(c == chunks - 1))
    return last


def setup(g):
    nc, io = g.nc, g.io
    g.h = g.at("h", H_AT, [P, TT, D])
    g.xh = g.at("xh", X_AT, [P, DC, S], F32R)
    g.xl = g.at("xl", X_AT + 8, [P, DC, S], F32R)
    g.raw = g.at("raw", RAW_AT, [P, RAW, TILE])
    hl = g.at("split", SPLIT_AT, [P, 2, 2, TILE], F32R)
    g.high = [hl[:, s, 0, :] for s in range(2)]
    g.low = [hl[:, s, 1, :] for s in range(2)]
    g.cols = g.const("cols", [P, N_COLS])
    g.heads = g.const("heads", [SSD_HEADS, 4])
    g.ident = g.const("ident", [P, P])
    g.ones = g.const("ones", [P, P])
    g.upto = g.const("upto", [P, P])
    g.neg_from = g.const("neg_from", [P, P])
    g.neg_ones = g.const("neg_ones", [P, P])
    g.last_row = g.const("last_row", [P, P])
    g.to_row = g.const("to_row", [P, HEADS, 32])
    g.head_mask = g.const("head_mask", [P, SSD_HEADS])
    g.level = g.const("level", [P, LEVELS, P])
    g.raw_loaded = [g.sem(f"raw_loaded{j}") for j in range(RAW)]
    g.high_split = g.sem("high_split")
    g.low_split = g.sem("low_split")
    g.tile_used = g.sem("tile_used")
    cols_loaded, heads_loaded = g.sem("cols_loaded"), g.sem("heads_loaded")
    rows_loaded = g.sem("rows_loaded")
    consts = g.sem("consts")
    with nc.Block() as block:
        @block.sync
        def _(sp):
            sp.dma_start(g.h[:, :, :], io["x"].rearrange("(t p) d -> p t d", p=P)).then_inc(rows_loaded, 16)
            for j in range(RAW):
                sp.dma_start(g.raw[:, j, :], io["stream"][j]).then_inc(g.raw_loaded[j], 16)
            sp.wait_ge(rows_loaded, 16)

        @block.scalar
        def _(act):
            act.dma_start(g.cols[:, :], io["cols"]).then_inc(cols_loaded, 16)
            act.dma_start(g.heads[:, :], io["heads"]).then_inc(heads_loaded, 16)
            act.sem_inc(g.tile_used, 2)
            for j in range(2):
                split_high(g, act, 0, j)
            act.wait_ge(cols_loaded, 16)
            act.wait_ge(heads_loaded, 16)

        @block.vector
        def _(dve):
            for j in range(2):
                split_low(g, dve, 0, j)

        @block.gpsimd
        def _(pool):
            for b, v in ((g.ident, 0.0), (g.ones, 1.0), (g.upto, 1.0), (g.neg_from, -1.0), (g.neg_ones, -1.0),
                         (g.last_row, 1.0)):
                pool.memset(b[:, :], v).then_inc(consts, 1)
            pool.memset(g.to_row[:, :, :], 0.0).then_inc(consts, 1)
            pool.memset(g.head_mask[:, :], 0.0).then_inc(consts, 1)
            pool.memset(g.level[:, :, :], 0.0).then_inc(consts, 1)
            pool.wait_ge(consts, 9)
            for h in range(HEADS):
                pool.memset(g.to_row[:, h, h:h + 1], 1.0)
            for lv in range(LEVELS):
                w = 1 << lv
                pool.memset(g.level[:, lv, :].rearrange("p (b r) -> p b r", r=2 * w)[:, :, w:], 1.0).then_inc(consts, 1)
            n = 9 + LEVELS
            pool.wait_ge(consts, n)

            def select(view, compare, fill, base, pattern, mult):
                nonlocal n
                pool.affine_select(out=view, in_=view, compare_op=compare, fill=fill, base=base, pattern=pattern,
                                   channel_multiplier=mult).then_inc(consts, 1)
                n += 1

            select(g.ident[:, :], ALU.not_equal, 1.0, 0, [[-1, P]], 1)
            select(g.upto[:, :], ALU.is_ge, 0.0, 0, [[1, P]], -1)
            select(g.neg_from[:, :], ALU.is_ge, 0.0, 0, [[-1, P]], 1)
            select(g.last_row[:, :], ALU.is_ge, 0.0, 1 - P, [[0, P]], 1)
            for lv in range(LEVELS):
                w = 1 << lv
                v = g.level[:, lv, :].rearrange("p (b r) -> p b r", r=2 * w)
                select(v, ALU.is_ge, 0.0, 0, [[-2 * w, P // (2 * w)], [0, 2 * w]], 1)
                pool.wait_ge(consts, n)
                select(v, ALU.is_ge, 0.0, w - 1, [[2 * w, P // (2 * w)], [0, 2 * w]], -1)
            for q in range(4):
                pool.wait_ge(consts, n)
                select(g.head_mask[:, :], ALU.not_equal, 1.0, -32 * q, [[-1, SSD_HEADS]], 1)
            pool.wait_ge(consts, n)


def refine_root(dve, r, v, t, done, n):
    dve.tensor_tensor(t, r, r, ALU.mult).then_inc(done, 1)
    dve.wait_ge(done, n + 1)
    dve.tensor_tensor(t, t, v, ALU.mult).then_inc(done, 1)
    dve.wait_ge(done, n + 2)
    dve.tensor_scalar(t, t, -0.5, 1.5, ALU.mult, ALU.add).then_inc(done, 1)
    dve.wait_ge(done, n + 3)
    dve.tensor_tensor(r, r, t, ALU.mult).then_inc(done, 1)
    return n + 4


def normed_columns(g, weight, small=None, first_weight=None, rows_to=None):
    nc = g.nc
    with ExitStack() as stack:
        junk = g.at("junk", R, [P, D])
        rows = g.at("rows", R + 2, [P, TT, D])
        col = g.at("col", R + 10, [P, 2, S])
        wn = g.at("wn", R + 12, [P, D])
        ws = g.at("ws", R + 14, [P, DC, 64])
        ss = g.at("ss", R + 15, [P, 2, TT])
        rs = g.at("rs", R + 15.25, [P, 2, TT])
        var = g.at("var", R + 15.5, [P, 2, TT])
        tmp = g.at("tmp", R + 15.75, [P, 2, TT])
        turned_ps = g.banks(stack, 4, "turned")
        m = small[0].shape[2] if small else 0
        small_loaded, norm_loaded = g.sem("small_loaded"), g.sem("norm_loaded")
        summed, rooted, scaled, turned, columned, high, low = (
            g.sem(x) for x in ("summed", "rooted", "scaled", "turned", "columned", "x_high", "x_low"))
        small_used, vv = g.sem("small_used"), g.sem("vector_step")
        rounds = 2 if first_weight is not None else 1
        with nc.Block() as block:
            @block.sync
            def _(sp):
                if first_weight is not None:
                    sp.dma_start(wn[:, :], first_weight).then_inc(norm_loaded, 16)
                if rows_to is not None:
                    sp.wait_ge(scaled, TT)
                    sp.dma_start(rows_to.rearrange("(t p) d -> p t d", p=P), g.h[:, :, :]).then_inc(norm_loaded, 16)
                    sp.wait_ge(norm_loaded, 32)
                if small:
                    sp.dma_start(ws[:, :, 0:m], small[0]).then_inc(small_loaded, 16)

            @block.scalar
            def _(act):
                for r in range(rounds):
                    for t in range(TT):
                        if r == 1:
                            act.wait_ge(scaled, t + 1)
                        act.activation(junk[:, :], g.h[:, t, :], ACT.Square,
                                       accum_out=ss[:, r, t:t + 1]).then_inc(summed, 1)
                        act.wait_ge(summed, TT * r + t + 1)
                    act.wait_ge(rooted, 7 * r + 2)
                    act.activation(rs[:, r, :], rs[:, r, :], ACT.Sqrt).then_inc(rooted, 1)
                for c in range(DC):
                    act.wait_ge(columned, c + 1)
                    act.activation(g.xh[:, c, :], col[:, c % 2, :], ACT.Copy).then_inc(high, 1)

            @block.vector
            def _(dve):
                for r in range(rounds):
                    dve.wait_ge(summed, TT * (r + 1))
                    dve.tensor_scalar(var[:, r, :], ss[:, r, :], 1.0 / D, EPS, ALU.mult, ALU.add).then_inc(rooted, 1)
                    dve.wait_ge(rooted, 7 * r + 1)
                    dve.reciprocal(rs[:, r, :], var[:, r, :]).then_inc(rooted, 1)
                    dve.wait_ge(rooted, 7 * r + 3)
                    n = refine_root(dve, rs[:, r, :], var[:, r, :], tmp[:, r, :], rooted, 7 * r + 3)
                    dve.wait_ge(rooted, n)
                    if r == 0 and first_weight is not None:
                        dve.wait_ge(norm_loaded, 16)
                        for t in range(TT):
                            dve.scalar_tensor_tensor(out=g.h[:, t, :], in0=g.h[:, t, :], scalar=rs[:, 0, t:t + 1],
                                                     in1=wn[:, :], op0=ALU.mult, op1=ALU.mult).then_inc(scaled, 1)
                        dve.wait_ge(scaled, TT)
                for t in range(TT):
                    dve.tensor_scalar(rows[:, t, :], g.h[:, t, :], rs[:, rounds - 1, t:t + 1], None,
                                      ALU.mult).then_inc(scaled, 1)
                for c in range(DC):
                    dve.wait_ge(turned, c + 1)
                    if c >= 2:
                        dve.wait_ge(high, c - 1)
                        dve.wait_ge(low, c - 1)
                        if small:
                            dve.wait_ge(small_used, c - 1)
                    dve.tensor_scalar(col[:, c % 2, :], turned_ps[c % 4][:, :], g.col(weight, c), None,
                                      ALU.mult).then_inc(columned, 1)
                    dve.wait_ge(high, c + 1)
                    dve.tensor_tensor(g.xl[:, c, :], col[:, c % 2, :], g.xh[:, c, :], ALU.subtract).then_inc(low, 1)

            @block.tensor
            def _(pe):
                def narrow(c):
                    pe.wait_ge(columned, c + 1)
                    pe.matmul(small[1], ws[:, c, 0:m], col[:, c % 2, :], start=(c == 0),
                              stop=(c == DC - 1)).then_inc(small_used, 1)

                pe.wait_ge(scaled, TT * rounds)
                if small:
                    pe.wait_ge(small_loaded, 16)
                for c in range(DC):
                    if c >= 4:
                        pe.wait_ge(columned, c - 3)
                    for t in range(TT):
                        last = pe.transpose(turned_ps[c % 4][:, t * P:t * P + P], rows[:, t, c * P:c * P + P],
                                            g.ident[:, :])
                    last.then_inc(turned, 1)
                    if small and c >= 1:
                        narrow(c - 1)
                if small:
                    narrow(DC - 1)


def project(g, act_buf, n_tiles, plain, conv=None, conv_bias=None):
    nc = g.nc
    with ExitStack() as stack:
        out = g.banks(stack, 4, "proj")
        pre = g.at("pre", R + 40, [P, 2, 3 + S])
        mixed = g.at("conv", R + 43, [P, 2, S])
        read, summed, done = (g.sem(x) for x in ("bank_read", "conv_step", "conv_out"))
        cleared, silu = g.sem("pad_cleared"), g.sem("silu_done")
        base = g.base
        n_plain = sum(n for n, _, _ in plain)
        with nc.Block() as block:
            @block.sync
            def _(sp):
                stream_load(g, sp, n_tiles)

            @block.tensor
            def _(pe):
                with steps(pe, 0, n_tiles, 4) as i:
                    for j in range(4):
                        pe.wait_ge(g.low_split, i + (base + j + 1))
                        pe.wait_ge(read, i + j)
                        mm_columns(g, pe, base + j, out[j][:, :]).then_inc(g.tile_used, 1)

            @block.scalar
            def _(act):
                act.sem_inc(read, 3)
                at = 0
                for n, func, scale in plain:
                    with steps(act, at, at + n, 4) as i:
                        for j in range(4):
                            split_high(g, act, i, j + 2)
                            tile_done(g, act, i, j)
                            act.activation(act_buf[:, i + j, :], out[j][:, :], func, scale=scale).then_inc(read, 1)
                    at += n
                if n_tiles > n_plain:
                    act.wait_ge(cleared, 1)
                    with steps(act, n_plain, n_tiles, 4) as i:
                        for j in range(4):
                            split_high(g, act, i, j + 2)
                            tile_done(g, act, i, j)
                            act.wait_ge(done, i + (j + 1 - n_plain))
                            act.activation(pre[:, j % 2, 3:], out[j][:, :], ACT.Copy).then_inc(read, 1)
                            act.wait_ge(done, i + (j + 3 - n_plain))
                            b = 0.0
                            if conv_bias:
                                b = g.cols[:, bass.ds(i + (COLS[conv_bias][0] + j - n_plain), 1)]
                            act.activation(act_buf[:, i + j, :], mixed[:, j % 2, :], ACT.Silu, bias=b)\
                               .then_inc(silu, 1)

            @block.vector
            def _(dve):
                with steps(dve, 0, n_plain, 4) as i:
                    for j in range(4):
                        split_low(g, dve, i, j + 2)
                if n_tiles > n_plain:
                    dve.memset(pre[:, :, 0:3], 0.0).then_inc(cleared, 1)
                    dve.sem_inc(done, 2)
                    with steps(dve, n_plain, n_tiles, 4) as i:
                        for j in range(4):
                            split_low(g, dve, i, j + 2)
                            w = COLS[conv][0]
                            dve.wait_ge(read, i + (j + 4))
                            b = j % 2
                            for k in range(TAPS):
                                tap = g.cols[:, bass.ds(4 * i + (w + 4 * (j - n_plain) + k), 1)]
                                if k == 0:
                                    if j >= 2:
                                        dve.wait_ge(silu, i + (j - 1 - n_plain))
                                    ins = dve.tensor_scalar(mixed[:, b, :], pre[:, b, 0:S], tap, None, ALU.mult)
                                else:
                                    dve.wait_ge(summed, 3 * i + (3 * (j - n_plain) + k))
                                    ins = dve.scalar_tensor_tensor(out=mixed[:, b, :], in0=pre[:, b, k:k + S],
                                                                   scalar=tap, in1=mixed[:, b, :], op0=ALU.mult,
                                                                   op1=ALU.add)
                                ins.then_inc(summed if k < 3 else done, 1)
    g.base += n_tiles


XA, Z, Q, K, V = 0, 4, 12, 20, 28


def delta_rows(g, act_buf, rows_ps):
    nc = g.nc
    g.rows = g.at("rows", R + 62, [P, S])
    v = g.at("v", R + 58, [P, S])
    t = g.at("t", R + 59, [P, S])
    u = g.at("u", R + 60, [P, S])
    sq = g.at("sq", R + 56, [P, 2, S])
    neg_a = g.const("neg_a", [P, 1])
    g.sum_c = g.const("sum_c", [P, HEADS, TT])
    g.beta_c = g.const("beta_c", [P, HEADS, TT])
    g.nbeg_c = g.const("nbeg_c", [P, HEADS, TT])
    g.left_c = g.const("left_c", [P, HEADS, TT])
    g.last_c = g.const("last_c", [P, HEADS, TT])
    eg = g.const("eg", [P, HEADS, TT])
    cleared, squared, summed, root, soft, turned, copied, spread, tail = (g.sem(x) for x in (
        "rows_cleared", "squared", "norms_summed", "root", "softplus", "rows_turned", "turned_read", "last_spread",
        "scalars"))
    with ExitStack() as stack:
        cols_ps = g.banks(stack, 1, "cols")[0]
        last_ps = g.banks(stack, 1, "last")[0]
        with nc.Block() as block:
            @block.scalar
            def _(act):
                act.wait_ge(soft, 1)
                act.activation(t[0:8, :], v[0:8, :], ACT.Abs).then_inc(soft, 1)
                act.wait_ge(soft, 2)
                act.activation(t[0:8, :], t[0:8, :], ACT.Exp, scale=-1.0).then_inc(soft, 1)
                act.activation(neg_a[0:8, :], g.heads[0:8, 0:1], ACT.Exp)
                act.wait_ge(soft, 3)
                act.activation(t[0:8, :], t[0:8, :], ACT.Ln, bias=1.0).then_inc(soft, 1)
                act.wait_ge(cleared, 1)
                act.activation(g.rows[32:40, :], rows_ps[32:40, :], ACT.Sigmoid).then_inc(soft, 1)
                for n in range(2 * HEADS):
                    if n >= 2:
                        act.wait_ge(summed, n - 1)
                    act.activation(sq[:, n % 2, :], act_buf[:, (K if n < HEADS else Q) + n % HEADS, :],
                                   ACT.Square).then_inc(squared, 1)
                act.wait_ge(root, 2)
                act.activation(g.rows[64:, :], t[64:, :], ACT.Sqrt).then_inc(root, 1)
                act.wait_ge(tail, 2)
                act.activation(eg[:, :, :], g.sum_c[:, :, :], ACT.Exp).then_inc(tail, 1)
                act.wait_ge(spread, 1)
                act.activation(g.last_c[:, :, :], last_ps[:, 0:32].rearrange("p (h c) -> p h c", c=TT),
                               ACT.Exp).then_inc(tail, 1)
                act.wait_ge(tail, 5)
                act.activation(g.left_c[:, :, :], g.left_c[:, :, :], ACT.Exp).then_inc(tail, 1)

            @block.tensor
            def _(pe):
                for n in range(2 * HEADS):
                    pe.wait_ge(squared, n + 1)
                    q = 64 if n < HEADS else 96
                    pe.matmul(rows_ps[q:q + 32, :], g.to_row[:, n % HEADS, :], sq[:, n % 2, :],
                              start=(n % HEADS == 0), stop=(n % HEADS == HEADS - 1)).then_inc(summed, 1)
                pe.wait_ge(soft, 11)
                for c in range(TT):
                    pe.transpose(cols_ps[:, c * P:c * P + 64], g.rows[0:64, c * P:c * P + P], g.ident[0:64, 0:64])\
                      .then_inc(turned, 1)
                pe.wait_ge(tail, 2)
                pe.matmul(last_ps[:, 0:32], g.last_row[:, :], g.sum_c[:, :, :].rearrange("p h c -> p (h c)"),
                          start=True, stop=True).then_inc(spread, 1)

            @block.vector
            def _(dve):
                dve.tensor_scalar(v[0:8, :], rows_ps[0:8, :], g.heads[0:8, 1:2], None, ALU.add).then_inc(soft, 1)
                dve.memset(g.rows[:, :], 0.0).then_inc(cleared, 1)
                dve.wait_ge(soft, 5)
                dve.scalar_tensor_tensor(out=u[0:8, :], in0=v[0:8, :], scalar=0.0, in1=t[0:8, :], op0=ALU.max,
                                         op1=ALU.add).then_inc(soft, 1)
                dve.wait_ge(soft, 6)
                dve.tensor_scalar(u[0:8, :], u[0:8, :], neg_a[0:8, :], -1.0, ALU.mult, ALU.mult).then_inc(soft, 1)
                dve.wait_ge(soft, 7)
                for c in range(TT):
                    w = slice(c * P, c * P + P)
                    dve.tensor_tensor_scan(out=g.rows[0:8, w], data0=g.ones[0:8, :], data1=u[0:8, w], initial=0.0,
                                           op0=ALU.mult, op1=ALU.add).then_inc(soft, 1)
                dve.wait_ge(summed, 2 * HEADS)
                dve.tensor_scalar(v[64:, :], rows_ps[64:, :], EPS, None, ALU.add).then_inc(root, 1)
                dve.wait_ge(root, 1)
                dve.reciprocal(t[64:, :], v[64:, :]).then_inc(root, 1)
                dve.wait_ge(root, 3)
                n = refine_root(dve, g.rows[64:, :], v[64:, :], t[64:, :], root, 3)
                dve.wait_ge(root, n)
                dve.tensor_scalar(g.rows[96:, :], g.rows[96:, :], P ** -0.5, None, ALU.mult).then_inc(root, 1)
                dve.wait_ge(turned, TT)
                cols = cols_ps[:, :].rearrange("p (c n) -> p n c", n=P)
                dve.tensor_copy(g.sum_c[:, :, :], cols[:, 0:8, :]).then_inc(tail, 1)
                dve.tensor_copy(g.beta_c[:, :, :], cols[:, 32:40, :]).then_inc(tail, 1)
                dve.wait_ge(tail, 3)
                dve.scalar_tensor_tensor(out=g.nbeg_c[:, :, :], in0=eg[:, :, :], scalar=-1.0, in1=g.beta_c[:, :, :],
                                         op0=ALU.mult, op1=ALU.mult)
                dve.wait_ge(spread, 1)
                dve.wait_ge(tail, 4)
                dve.tensor_tensor(g.left_c[:, :, :], last_ps[:, 0:32].rearrange("p (h c) -> p h c", c=TT),
                                  g.sum_c[:, :, :], ALU.subtract).then_inc(tail, 1)
                dve.wait_ge(root, n + 1)


SLOTS = 2


def nth(i, s, per, k=0):
    return per * i + (SLOTS * k + s + 1)


def delta_rule(g, act_buf):
    nc = g.nc

    def tile(name, page):
        return g.at(name, page, [P, TT, P])

    bufs = []
    for s in range(SLOTS):
        a = R + 36 + 13 * s
        b = {n: tile(n, a + k) for k, n in enumerate(
            ("kn", "qn", "dec", "db", "d", "attn", "x", "kb", "kd", "qg", "sel", "vb"))}
        b["inv"], b["inv_t"], b["part"], b["w"] = b["kn"], b["qn"], b["db"], b["sel"]
        b["vn"] = g.at("vn", a + 12, [P, P])
        b["st"] = g.at("st", a + 12.25, [P, P])
        bufs.append(b)
    names = ("selected", "spread", "k_normed", "q_normed", "diffed", "decayed", "masked", "grown", "betad", "grams",
             "lowered", "attended", "v_copied", "rows_turned", "v_scaled", "k_scaled", "k_left", "q_scaled",
             "part_made", "first_t", "crossed", "cross_read", "product_made", "inv_made", "inv_t_made",
             "w_made", "w_read", "new_made", "new_read", "out_made", "state_made", "state_added", "head_done")
    m = {n: g.sem(n) for n in names}

    def per(b):
        return b[:, :, :].rearrange("p c n -> p (c n)")

    with ExitStack() as stack:
        banks = [g.banks(stack, 4, "delta") for _ in range(SLOTS)]

        def ps(s, k):
            return banks[s][k][:, :].rearrange("p (c n) -> p c n", n=P)

        with nc.Block() as block:
            @block.tensor
            def _(pe):
                with steps(pe, 0, HEADS, SLOTS) as i:
                    for s in range(SLOTS):
                        b = bufs[s]
                        pe.wait_ge(m["selected"], i + (s + 1))
                        for q in range(4):
                            last = pe.matmul(banks[s][q][:, :], g.ones[32 * q:32 * q + 32, :],
                                             per(b["sel"])[32 * q:32 * q + 32, :], start=True, stop=True)
                        last.then_inc(m["spread"], 1)
                    for s in range(SLOTS):
                        b = bufs[s]
                        pe.wait_ge(m["k_normed"], i + (s + 1))
                        pe.wait_ge(m["q_normed"], i + (s + 1))
                        for c in range(TT):
                            pe.matmul(ps(s, 2)[:, c, :], b["kn"][:, c, :], b["kn"][:, c, :], start=True, stop=True)
                        for c in range(TT):
                            last = pe.matmul(ps(s, 3)[:, c, :], b["kn"][:, c, :], b["qn"][:, c, :], start=True,
                                             stop=True)
                        last.then_inc(m["grams"], 1)
                    for s in range(SLOTS):
                        b = bufs[s]
                        pe.wait_ge(m["v_copied"], i + (s + 1))
                        pe.wait_ge(m["grown"], i + (s + 1))
                        pe.wait_ge(m["diffed"], i + (s + 1))
                        pe.wait_ge(m["betad"], i + (s + 1))
                        for c in range(TT):
                            pe.transpose(ps(s, 0)[:, c, :], b["kn"][:, c, :], g.ident[:, :])
                        for c in range(TT):
                            last = pe.transpose(ps(s, 1)[:, c, :], b["x"][:, c, :], g.ident[:, :])
                        last.then_inc(m["rows_turned"], 1)
                    for s in range(SLOTS):
                        b = bufs[s]
                        pe.wait_ge(m["part_made"], nth(i, s, LEVELS))
                        pe.wait_ge(m["lowered"], i + (s + 1))
                        for c in range(TT):
                            last = pe.matmul(ps(s, 2)[:, c, :], b["part"][:, c, :], g.ident[:, :], start=True,
                                             stop=True)
                        last.then_inc(m["first_t"], 1)
                    for lv in range(1, LEVELS):
                        for s in range(SLOTS):
                            b = bufs[s]
                            pe.wait_ge(m["part_made"], nth(i, s, LEVELS, lv))
                            pe.wait_ge(m["inv_made"], nth(i, s, LEVELS - 1, lv - 1))
                            for c in range(TT):
                                last = pe.matmul(ps(s, 2)[:, c, :], b["part"][:, c, :], b["inv"][:, c, :],
                                                 start=True, stop=True)
                            last.then_inc(m["crossed"], 1)
                        for s in range(SLOTS):
                            b = bufs[s]
                            pe.wait_ge(m["cross_read"], nth(i, s, LEVELS - 1, lv - 1))
                            pe.wait_ge(m["inv_t_made"], nth(i, s, LEVELS, lv - 1))
                            if lv == 1:
                                pe.wait_ge(m["attended"], i + (s + 1))
                                pe.wait_ge(m["k_left"], i + (s + 1))
                            if lv < LEVELS - 1:
                                for c in range(TT):
                                    pe.matmul(ps(s, 3)[:, c, :], b["inv_t"][:, c, :], b["x"][:, c, :],
                                              start=True, stop=True)
                            for c in range(TT):
                                last = pe.matmul(ps(s, 0)[:, c, :], b["x"][:, c, :], b["inv_t"][:, c, :],
                                                 start=True, stop=True)
                            last.then_inc(m["product_made"], 1)
                    for s in range(SLOTS):
                        b = bufs[s]
                        pe.wait_ge(m["inv_t_made"], nth(i, s, LEVELS, LEVELS - 1))
                        pe.wait_ge(m["k_scaled"], i + (s + 1))
                        for c in range(TT):
                            last = pe.matmul(ps(s, 2)[:, c, :], b["kb"][:, c, :], b["inv_t"][:, c, :], start=True,
                                             stop=True)
                        last.then_inc(m["w_made"], 1)
                    for c in range(TT):
                        for s in range(SLOTS):
                            b = bufs[s]
                            if c == 0:
                                pe.wait_ge(m["v_scaled"], i + (s + 1))
                                pe.wait_ge(m["w_read"], i + (s + 1))
                            else:
                                pe.wait_ge(m["state_added"], nth(i, s, TT - 1, c - 1))
                            last = pe.matmul(ps(s, 3)[:, c, :], b["inv_t"][:, c, :], b["vb"][:, c, :], start=True,
                                             stop=(c == 0))
                            if c:
                                last = pe.matmul(ps(s, 3)[:, c, :], b["w"][:, c, :], b["st"][:, :], start=False,
                                                 stop=True)
                            last.then_inc(m["new_made"], 1)
                        for s in range(SLOTS):
                            b = bufs[s]
                            pe.wait_ge(m["new_read"], nth(i, s, TT, c))
                            if c == 0:
                                pe.wait_ge(m["q_scaled"], i + (s + 1))
                            if c < TT - 1:
                                pe.matmul(ps(s, 0)[:, c, :], b["kd"][:, c, :], b["vn"][:, :], start=True,
                                          stop=True).then_inc(m["state_made"], 1)
                            if c:
                                pe.matmul(ps(s, 1)[:, c, :], b["st"][:, :], b["qg"][:, c, :], start=True, stop=False)
                            pe.matmul(ps(s, 1)[:, c, :], b["vn"][:, :], b["attn"][:, c, :], start=(c == 0),
                                      stop=True).then_inc(m["out_made"], 1)

            @block.scalar
            def _(act):
                act.sem_inc(m["head_done"], SLOTS)
                with steps(act, 0, HEADS, SLOTS) as i:
                    for s in range(SLOTS):
                        b = bufs[s]
                        act.wait_ge(m["spread"], i + (s + 1))
                        act.activation(per(b["qg"]), banks[s][0][:, :], ACT.Exp).then_inc(m["grown"], 1)
                        act.activation(per(b["x"]), act_buf[:, i + (V + s), :], ACT.Copy).then_inc(m["v_copied"], 1)
                        act.wait_ge(m["diffed"], i + (s + 1))
                        act.activation(per(b["dec"]), per(b["dec"]), ACT.Exp).then_inc(m["decayed"], 1)
                    for lv in range(1, LEVELS):
                        for s in range(SLOTS):
                            b = bufs[s]
                            act.wait_ge(m["crossed"], nth(i, s, LEVELS - 1, lv - 1))
                            act.activation(per(b["x"]), banks[s][2][:, :], ACT.Copy).then_inc(m["cross_read"], 1)
                    for s in range(SLOTS):
                        b = bufs[s]
                        act.wait_ge(m["w_made"], i + (s + 1))
                        act.activation(per(b["w"]), banks[s][2][:, :], ACT.Copy).then_inc(m["w_read"], 1)
                    for c in range(TT):
                        for s in range(SLOTS):
                            b = bufs[s]
                            act.wait_ge(m["new_made"], nth(i, s, TT, c))
                            act.activation(b["vn"][:, :], ps(s, 3)[:, c, :], ACT.Copy).then_inc(m["new_read"], 1)
                    for s in range(SLOTS):
                        act.wait_ge(m["out_made"], nth(i, s, TT, TT - 1))
                        act.activation(act_buf[:, i + (Q + s), :], banks[s][1][:, :],
                                       ACT.Copy).then_inc(m["head_done"], 1)

            @block.gpsimd
            def _(pool):
                with steps(pool, 0, HEADS, SLOTS) as i:
                    for s in range(SLOTS):
                        b = bufs[s]
                        pool.wait_ge(m["decayed"], i + (s + 1))
                        pool.tensor_tensor(b["dec"][:, :, :], b["dec"][:, :, :],
                                           g.upto[:, :].unsqueeze(1).to_broadcast([P, TT, P]),
                                           ALU.mult).then_inc(m["masked"], 1)
                    for lv in range(LEVELS):
                        for s in range(SLOTS):
                            b = bufs[s]
                            if lv == 0:
                                pool.wait_ge(m["lowered"], i + (s + 1))
                            elif lv == 1:
                                pool.wait_ge(m["first_t"], i + (s + 1))
                                pool.wait_ge(m["inv_t_made"], nth(i, s, LEVELS))
                            else:
                                pool.wait_ge(m["crossed"], nth(i, s, LEVELS - 1, lv - 2))
                            pool.tensor_tensor(b["part"][:, :, :], b["d"][:, :, :],
                                               g.level[:, lv, :].unsqueeze(1).to_broadcast([P, TT, P]),
                                               ALU.mult).then_inc(m["part_made"], 1)

            @block.vector
            def _(dve):
                def scaled(out, src, cols, h, sem):
                    dve.tensor_tensor(out[:, :, :], src, cols[:, bass.ds(h, 1), :].rearrange("p o c -> p (o c)")
                                      .unsqueeze(2).to_broadcast([P, TT, P]), ALU.mult).then_inc(sem, 1)

                with steps(dve, 0, HEADS, SLOTS) as i:
                    for s in range(SLOTS):
                        b = bufs[s]
                        dve.wait_ge(m["head_done"], i + (s + 1))
                        dve.tensor_scalar(per(b["sel"]), g.rows[:, :], g.head_mask[:, bass.ds(i + s, 1)], None,
                                          ALU.mult).then_inc(m["selected"], 1)
                    for s in range(SLOTS):
                        b = bufs[s]
                        h = i + s
                        dve.wait_ge(m["grown"], i + (s + 1))
                        for c in range(TT):
                            ins = dve.tensor_scalar(b["dec"][:, c, :], ps(s, 0)[:, c, :],
                                                    g.sum_c[:, bass.ds(h, 1), c], 0.0, ALU.subtract, ALU.min)
                        ins.then_inc(m["diffed"], 1)
                        dve.tensor_tensor(per(b["kn"]), act_buf[:, i + (K + s), :], banks[s][2][:, :],
                                          ALU.mult).then_inc(m["k_normed"], 1)
                        dve.tensor_tensor(per(b["qn"]), act_buf[:, i + (Q + s), :], banks[s][3][:, :],
                                          ALU.mult).then_inc(m["q_normed"], 1)
                        dve.wait_ge(m["grown"], i + (s + 1))
                        dve.wait_ge(m["q_normed"], i + (s + 1))
                        dve.tensor_tensor(per(b["qg"]), per(b["qg"]), per(b["qn"]), ALU.mult).then_inc(m["q_scaled"], 1)
                    for s in range(SLOTS):
                        b = bufs[s]
                        dve.wait_ge(m["masked"], i + (s + 1))
                        dve.tensor_tensor(per(b["db"]), per(b["dec"]), banks[s][1][:, :],
                                          ALU.mult).then_inc(m["betad"], 1)
                        dve.wait_ge(m["grams"], i + (s + 1))
                        dve.wait_ge(m["betad"], i + (s + 1))
                        dve.tensor_tensor(per(b["d"]), banks[s][2][:, :], per(b["db"]),
                                          ALU.mult).then_inc(m["lowered"], 1)
                        dve.tensor_tensor(per(b["attn"]), banks[s][3][:, :], per(b["dec"]),
                                          ALU.mult).then_inc(m["attended"], 1)
                    ident = g.ident[:, :].unsqueeze(1).to_broadcast([P, TT, P])
                    for s in range(SLOTS):
                        b = bufs[s]
                        h = i + s
                        dve.wait_ge(m["rows_turned"], i + (s + 1))
                        scaled(b["vb"], ps(s, 1), g.beta_c, h, m["v_scaled"])
                        scaled(b["kb"], ps(s, 0), g.nbeg_c, h, m["k_scaled"])
                        scaled(b["kd"], ps(s, 0), g.left_c, h, m["k_left"])
                    for s in range(SLOTS):
                        b = bufs[s]
                        dve.wait_ge(m["part_made"], nth(i, s, LEVELS))
                        dve.tensor_tensor(b["inv_t"][:, :, :], ident, b["part"][:, :, :],
                                          ALU.subtract).then_inc(m["inv_t_made"], 1)
                        dve.wait_ge(m["first_t"], i + (s + 1))
                        dve.tensor_tensor(b["inv"][:, :, :], ident, ps(s, 2),
                                          ALU.subtract).then_inc(m["inv_made"], 1)
                    for lv in range(1, LEVELS):
                        for s in range(SLOTS):
                            b = bufs[s]
                            dve.wait_ge(m["product_made"], nth(i, s, LEVELS - 1, lv - 1))
                            if lv < LEVELS - 1:
                                dve.wait_ge(m["inv_made"], nth(i, s, LEVELS - 1, lv - 1))
                                dve.tensor_tensor(per(b["inv"]), per(b["inv"]), banks[s][3][:, :],
                                                  ALU.subtract).then_inc(m["inv_made"], 1)
                            dve.wait_ge(m["inv_t_made"], nth(i, s, LEVELS, lv - 1))
                            dve.tensor_tensor(per(b["inv_t"]), per(b["inv_t"]), banks[s][0][:, :],
                                              ALU.subtract).then_inc(m["inv_t_made"], 1)
                    for c in range(TT - 1):
                        for s in range(SLOTS):
                            b = bufs[s]
                            dve.wait_ge(m["state_made"], nth(i, s, TT - 1, c))
                            if c == 0:
                                dve.tensor_copy(b["st"][:, :], ps(s, 0)[:, c, :]).then_inc(m["state_added"], 1)
                            else:
                                dve.wait_ge(m["out_made"], nth(i, s, TT, c))
                                dve.scalar_tensor_tensor(
                                    out=b["st"][:, :], in0=b["st"][:, :], scalar=g.last_c[:, bass.ds(i + s, 1), c],
                                    in1=ps(s, 0)[:, c, :], op0=ALU.mult, op1=ALU.add).then_inc(m["state_added"], 1)


def delta_norm(g, act_buf):
    nc = g.nc
    g.yh = g.at("yh", R + 36, [P, HEADS, S], F32R)
    g.yl = g.at("yl", R + 44, [P, HEADS, S], F32R)
    sq = g.at("sq", R + 52, [P, 2, S])
    v = g.at("v", R + 54, [32, S])
    t = g.at("t", R + 55, [32, S])
    rr = g.at("rr", R + 56, [32, S])
    sel = g.at("sel", R + 57, [32, 2, S])
    y = g.at("y", R + 59, [P, 2, S])
    squared, summed, root, selected, spread, normed, gated, high, low = (g.sem(x) for x in (
        "squared", "summed", "root", "selected", "spread", "normed", "gated", "y_high", "y_low"))
    with ExitStack() as stack:
        rows_ps = g.banks(stack, 1, "rows")[0]
        wide = g.banks(stack, 2, "wide")
        with nc.Block() as block:
            @block.scalar
            def _(act):
                for h in range(HEADS):
                    if h >= 2:
                        act.wait_ge(summed, h - 1)
                    act.activation(sq[:, h % 2, :], act_buf[:, Q + h, :], ACT.Square).then_inc(squared, 1)
                act.wait_ge(root, 2)
                act.activation(rr[:, :], t[:, :], ACT.Sqrt).then_inc(root, 1)
                with steps(act, 0, HEADS, 2) as i:
                    for s in range(2):
                        act.wait_ge(gated, i + (s + 1))
                        act.activation(g.yh[:, i + s, :], y[:, s, :], ACT.Copy).then_inc(high, 1)

            @block.tensor
            def _(pe):
                for h in range(HEADS):
                    pe.wait_ge(squared, h + 1)
                    pe.matmul(rows_ps[0:32, :], g.to_row[:, h, :], sq[:, h % 2, :], start=(h == 0),
                              stop=(h == HEADS - 1)).then_inc(summed, 1)
                with steps(pe, 0, HEADS, 2) as i:
                    for s in range(2):
                        pe.wait_ge(selected, i + (s + 1))
                        pe.matmul(wide[s][:, :], g.ones[0:32, :], sel[:, s, :], start=True, stop=True)\
                          .then_inc(spread, 1)

            @block.vector
            def _(dve):
                dve.wait_ge(summed, HEADS)
                dve.tensor_scalar(v[:, :], rows_ps[0:32, :], 1.0 / P, EPS, ALU.mult, ALU.add).then_inc(root, 1)
                dve.wait_ge(root, 1)
                dve.reciprocal(t[:, :], v[:, :]).then_inc(root, 1)
                dve.wait_ge(root, 3)
                n = refine_root(dve, rr[:, :], v[:, :], t[:, :], root, 3)
                dve.wait_ge(root, n)
                dve.sem_inc(normed, 2)
                dve.sem_inc(low, 2)
                with steps(dve, 0, HEADS, 2) as i:
                    for s in range(2):
                        dve.wait_ge(normed, i + (s + 1))
                        dve.tensor_scalar(sel[:, s, :], rr[:, :], g.head_mask[0:32, bass.ds(i + s, 1)], None,
                                          ALU.mult).then_inc(selected, 1)
                    for s in range(2):
                        dve.wait_ge(spread, i + (s + 1))
                        dve.wait_ge(low, i + (s + 1))
                        dve.tensor_tensor(y[:, s, :], act_buf[:, i + (Q + s), :], wide[s][:, :],
                                          ALU.mult).then_inc(normed, 1)
                    for s in range(2):
                        dve.wait_ge(normed, i + (s + 3))
                        dve.scalar_tensor_tensor(out=y[:, s, :], in0=y[:, s, :], scalar=g.col("dn_norm"),
                                                 in1=act_buf[:, i + (Z + s), :], op0=ALU.mult,
                                                 op1=ALU.mult).then_inc(gated, 1)
                    for s in range(2):
                        dve.wait_ge(high, i + (s + 1))
                        dve.tensor_tensor(g.yl[:, i + s, :], y[:, s, :], g.yh[:, i + s, :],
                                          ALU.subtract).then_inc(low, 1)


def pool_mix(g, act_buf):
    nc = g.nc
    n_groups = len(POOL_WINDOWS)
    pad = max(POOL_WINDOWS)
    g.ph = g.at("ph", R + 12, [P, n_groups, S], F32R)
    g.pl = g.at("pl", R + 16, [P, n_groups, S], F32R)
    a = g.at("win_a", R + 20, [P, pad + S])
    b = g.at("win_b", R + 22, [P, pad + S])
    pooled = g.at("pooled", R + 24, [P, n_groups, S])
    y = g.at("pool_y", R + 28, [P, n_groups, S])
    w = g.at("pool_w", R + 32, [P, n_groups, P])
    count = g.at("count", R + 33, [P, 2, pad])
    head = g.at("head", R + 34, [P, pad])
    loaded, counted, step, mixed, scaled, high, low = (g.sem(x) for x in (
        "pool_w_loaded", "counted", "window_step", "mixed", "pool_scaled", "p_high", "p_low"))
    pooled_done = g.sem("pooled")
    with ExitStack() as stack:
        banks = g.banks(stack, n_groups, "mixed")
        with nc.Block() as block:
            @block.sync
            def _(sp):
                sp.dma_start(w[:, :, :], g.io["pool_w"]).then_inc(loaded, 16)

            @block.gpsimd
            def _(pool):
                pool.iota(count[:, 0, :], pattern=[[1, pad]], base=1, channel_multiplier=0,
                          allow_small_or_imprecise_dtypes=True).then_inc(counted, 1)

            @block.vector
            def _(dve):
                n = 0

                def did(ins):
                    nonlocal n
                    ins.then_inc(step, 1)
                    n += 1
                    dve.wait_ge(step, n)

                dve.wait_ge(counted, 1)
                did(dve.reciprocal(count[:, 1, :], count[:, 0, :]))
                did(dve.memset(a[:, 0:pad], 0.0))
                did(dve.memset(b[:, 0:pad], 0.0))
                for q, win in enumerate(POOL_WINDOWS):
                    x = act_buf[:, XA + q, :]
                    did(dve.tensor_copy(a[:, pad:], x))
                    src, dst, lag = a, b, 1
                    while lag < win:
                        did(dve.tensor_tensor(dst[:, pad:], src[:, pad:], src[:, pad - lag:pad - lag + S], ALU.add))
                        src, dst, lag = dst, src, 2 * lag
                    did(dve.scalar_tensor_tensor(out=pooled[:, q, :], in0=src[:, pad:], scalar=1.0 / win, in1=x,
                                                 op0=ALU.mult, op1=ALU.subtract))
                    did(dve.tensor_tensor(head[:, 0:win], src[:, pad:pad + win], count[:, 1, 0:win], ALU.mult))
                    did(dve.tensor_tensor(pooled[:, q, 0:win], head[:, 0:win], x[:, 0:win], ALU.subtract))
                    dve.sem_inc(pooled_done, 1)
                for q in range(n_groups):
                    dve.wait_ge(mixed, q + 1)
                    dve.tensor_scalar(y[:, q, :], banks[q][:, :], g.col("pool_scale", q), None,
                                      ALU.mult).then_inc(scaled, 1)
                for q in range(n_groups):
                    dve.wait_ge(high, q + 1)
                    dve.tensor_tensor(g.pl[:, q, :], y[:, q, :], g.ph[:, q, :], ALU.subtract).then_inc(low, 1)

            @block.tensor
            def _(pe):
                pe.wait_ge(loaded, 16)
                for q in range(n_groups):
                    pe.wait_ge(pooled_done, q + 1)
                    pe.matmul(banks[q][:, :], w[:, q, :], pooled[:, q, :], start=True, stop=True).then_inc(mixed, 1)

            @block.scalar
            def _(act):
                for q in range(n_groups):
                    act.wait_ge(scaled, q + 1)
                    act.activation(g.ph[:, q, :], y[:, q, :], ACT.Copy).then_inc(high, 1)


def merge(g, a, a_chunks, b, rows_from, bias=None):
    nc, base = g.nc, g.base
    g.mh = g.at("mh", R + 20, [P, DC, S], F32R)
    g.ml = g.at("ml", R + 28, [P, DC, S], F32R)
    gate = g.at("gate", R + 52, [P, 2, S])
    m = g.at("merged", R + 54, [P, 3, S])
    gated, first, second, both, high, low = (g.sem(x) for x in (
        "gated", "a_gated", "b_gated", "merged", "m_high", "m_low"))
    rows = g.sem("rows_loaded")
    with ExitStack() as stack:
        banks = g.banks(stack, 4, "merge")
        with nc.Block() as block:
            @block.sync
            def _(sp):
                sp.dma_start(g.h[:, :, :], rows_from.rearrange("(t p) d -> p t d", p=P)).then_inc(rows, 16)
                stream_load(g, sp, N_MERGE)
                sp.wait_ge(rows, 16)

            @block.tensor
            def _(pe):
                with steps(pe, 0, N_MERGE, 4) as i:
                    for j, (x, chunks) in enumerate(((None, DC), (a, a_chunks), (None, DC), (b, DC))):
                        pe.wait_ge(g.low_split, i + (base + j + 1))
                        if j % 2 == 0:
                            pe.wait_ge(gated, i // 2 + (j // 2 + 1))
                        else:
                            pe.wait_ge(first if j == 1 else second, i // 4 + 1)
                        mm_columns(g, pe, base + j, banks[j][:, :], chunks, x).then_inc(g.tile_used, 1)

            @block.scalar
            def _(act):
                act.sem_inc(gated, 2)
                with steps(act, 0, N_MERGE, 4) as i:
                    for j in range(4):
                        split_high(g, act, i, j + 2)
                        if j % 2 == 0:
                            tile_done(g, act, i, j)
                            act.wait_ge(first if j == 0 else second, i // 4 + 1)
                            b = 0.0
                            if bias:
                                b = g.cols[:, bass.ds(i // 4 + (COLS[bias][0] + DC * (j // 2)), 1)]
                            act.activation(gate[:, j // 2, :], banks[j][:, :], ACT.Sigmoid, bias=b).then_inc(gated, 1)
                    act.wait_ge(both, i // 4 + 1)
                    act.activation(g.mh[:, i // 4, :], m[:, 2, :], ACT.Copy).then_inc(high, 1)

            @block.vector
            def _(dve):
                dve.sem_inc(first, 1)
                dve.sem_inc(second, 1)
                with steps(dve, 0, N_MERGE, 4) as i:
                    for j in range(4):
                        split_low(g, dve, i, j + 2)
                        if j % 2:
                            dve.wait_ge(gated, i // 2 + (j // 2 + 3))
                            tile_done(g, dve, i, j)
                            dve.tensor_tensor(m[:, j // 2, :], gate[:, j // 2, :], banks[j][:, :],
                                              ALU.mult).then_inc(first if j == 1 else second, 1)
                    dve.wait_ge(first, i // 4 + 2)
                    dve.wait_ge(second, i // 4 + 2)
                    dve.tensor_tensor(m[:, 2, :], m[:, 0, :], m[:, 1, :], ALU.add).then_inc(both, 1)
                    dve.wait_ge(high, i // 4 + 1)
                    dve.tensor_tensor(g.ml[:, i // 4, :], m[:, 2, :], g.mh[:, i // 4, :],
                                      ALU.subtract).then_inc(low, 1)
    g.base += N_MERGE


def mm_rows(g, pe, hi, lo, bank, xh, xl, half, start, stop):
    w = slice(half * 512, half * 512 + 512)
    pe.matmul(bank, xh, hi[:, w], start=start, stop=False, skip_group_check=True)
    pe.matmul(bank, xh, lo[:, w], start=False, stop=False, skip_group_check=True)
    return pe.matmul(bank, xl, hi[:, w], start=False, stop=stop, skip_group_check=True)


def mix_out(g, stack):
    nc, base = g.nc, g.base
    banks = g.banks(stack, 2 * TT, "out")
    last = base + N_OUT == g.total
    done = g.sem("out_done")
    added = g.sem("rows_added")
    with nc.Block() as block:
        @block.sync
        def _(sp):
            stream_load(g, sp, N_OUT)

        @block.tensor
        def _(pe):
            for c in range(N_OUT):
                t = base + c
                pe.wait_ge(g.low_split, t + 1)
                for q in range(2 * TT):
                    w = slice(q // 2 * P, q // 2 * P + P)
                    ins = mm_rows(g, pe, g.high[t % 2], g.low[t % 2], banks[q][:, :], g.mh[:, c, w], g.ml[:, c, w],
                                  q % 2, c == 0, c == N_OUT - 1)
                    if c == N_OUT - 1:
                        ins.then_inc(done, 1)
                if c < N_OUT - 1:
                    ins.then_inc(g.tile_used, 1)
            pe.wait_ge(done, 2 * TT)
            pe.sem_inc(g.tile_used, 1)

        @block.scalar
        def _(act):
            for c in range(N_OUT - 2 * last):
                split_high(g, act, 0, c + 2)

        @block.vector
        def _(dve):
            for c in range(N_OUT - 2 * last):
                split_low(g, dve, 0, c + 2)
            if not last:
                for q in range(2 * TT):
                    dve.wait_ge(done, q + 1)
                    rows = g.h[:, q // 2, q % 2 * 512:q % 2 * 512 + 512]
                    dve.tensor_tensor(rows, rows, banks[q][:, :], ALU.add).then_inc(added, 1)
    g.base += N_OUT
    return banks


def past(eng, sem, count, passed):
    eng.wait_ge(sem, count)
    eng.sem_inc(passed, 1)


def top16(dve, n, values, work, best, at, picked, passed, count):
    for r in range(n):
        dve.max(best[:, r, 0:8], values(r)).then_inc(picked, 1)
    count += n
    past(dve, picked, count, passed)
    for r in range(n):
        dve.match_replace(work(r), best[:, r, 0:8], values(r), -3.0e38).then_inc(picked, 1)
        dve.max_index(at[:, r, 0:8], best[:, r, 0:8], values(r)).then_inc(picked, 1)
    count += 2 * n
    past(dve, picked, count, passed)
    for r in range(n):
        dve.max(best[:, r, 8:16], work(r)).then_inc(picked, 1)
    count += n
    past(dve, picked, count, passed)
    for r in range(n):
        dve.max_index(at[:, r, 8:16], best[:, r, 8:16], work(r)).then_inc(picked, 1)
    return count + n


def peer_scores(g):
    nc, base = g.nc, g.base
    n_halves = 2 * HEADS
    keys = g.at("keys", R, [P, n_halves, N_KEYS])
    query = g.at("query", R + 4, [P, 2, S])
    score = g.at("score", R + 6, [P, 2, TT, N_KEYS])
    work = g.at("work", R + 8, [P, TT, N_KEYS])
    g.vals = g.at("vals", R + 10, [P, TT, n_halves, TOPK])
    g.keyno = g.at("keyno", R + 12, [P, TT, n_halves, TOPK])
    best = g.at("best", R + 14, [P, 2, TT, TOPK])
    where = g.at("where", R + 15, [P, 2, TT, TOPK], U32)
    per_tile = 5 * TT
    passed = g.sem("passed")
    keys_loaded, q_read, scored, s_read, picked, kept = (g.sem(x) for x in (
        "keys_loaded", "query_read", "scored", "score_read", "picked", "kept"))
    with ExitStack() as stack:
        qb = g.banks(stack, 4, "query")
        sb = g.banks(stack, 4, "score")
        with nc.Block() as block:
            @block.sync
            def _(sp):
                sp.dma_start(keys[:, :, :], g.io["keys"]).then_inc(keys_loaded, 16)
                stream_load(g, sp, N_QUERY)

            @block.tensor
            def _(pe):
                def score_tile(i, j):
                    pe.wait_ge(q_read, i + (j + 1))
                    pe.wait_ge(s_read, i + j)
                    for t in range(TT):
                        last = pe.matmul(sb[j][:, t * P:t * P + P], query[:, j % 2, t * P:t * P + P],
                                         keys[:, bass.ds(i + j, 1), :].rearrange("p o k -> p (o k)"),
                                         start=True, stop=True)
                    last.then_inc(scored, 1)

                pe.wait_ge(keys_loaded, 16)
                with steps(pe, 0, N_QUERY, 4) as i:
                    for j in range(4):
                        pe.wait_ge(g.low_split, i + (base + j + 1))
                        mm_columns(g, pe, base + j, qb[j][:, :]).then_inc(g.tile_used, 1)
                        if j:
                            score_tile(i, j - 1)
                    score_tile(i, 3)

            @block.scalar
            def _(act):
                act.sem_inc(s_read, 3)
                with steps(act, 0, N_QUERY, 4) as i:
                    for j in range(4):
                        split_high(g, act, i, j + 2)
                        tile_done(g, act, i, j)
                        act.wait_ge(scored, i + (j + 1))
                        act.activation(query[:, j % 2, :], qb[j][:, :], ACT.Copy).then_inc(q_read, 1)

            @block.vector
            def _(dve):
                dve.sem_inc(scored, 2)
                with steps(dve, 0, N_QUERY, 4) as i:
                    for j in range(4):
                        split_low(g, dve, i, j + 2)
                        s = j % 2
                        dve.wait_ge(scored, i + (j + 3))
                        if j < 2:
                            dve.wait_ge(kept, 2 * i + 2 * j)
                        else:
                            dve.wait_ge(kept, 2 * i + 2 * (j - 1))
                        dve.tensor_copy(score[:, s, :, :].rearrange("p t k -> p (t k)"), sb[j][:, :])\
                           .then_inc(s_read, 1)
                        past(dve, s_read, i + (j + 4), passed)
                        top16(dve, TT, lambda r: score[:, s, r, :], lambda r: work[:, r, :], best[:, s, :, :],
                              where[:, s, :, :], picked, passed, per_tile * i + per_tile * j)
                        dve.wait_ge(picked, per_tile * i + per_tile * (j + 1))
                        dve.tensor_copy(g.vals[:, :, bass.ds(i + j, 1), :].rearrange("p t o k -> p t (o k)"),
                                        best[:, s, :, :]).then_inc(kept, 1)
                        dve.tensor_copy(g.keyno[:, :, bass.ds(i + j, 1), :].rearrange("p t o k -> p t (o k)"),
                                        where[:, s, :, :]).then_inc(kept, 1)
    g.base += N_QUERY


def peer_pick(g):
    nc = g.nc
    hk = HEADS * TOPK
    g.first = g.at("first", R + 17, [P, S])
    g.second = g.at("second", R + 18, [P, S])
    g.gate = g.at("gate", R + 19, [P, S])
    g.count = g.at("count", R + 20, [P, N_KEYS])
    cand = g.at("cand", R + 21, [P, HEADS, TOPK, TOPK])
    work = g.at("work", R + 25, [P, HEADS, TOPK, TOPK])
    hot = g.at("hot", R + 29, [P, 2, HEADS, TOPK, TOPK])
    best = g.at("best", R + 37, [P, HEADS, TOPK])
    where = g.at("where", R + 37.25, [P, HEADS, TOPK], U32)
    part = g.at("part", R + 37.5, [P, 2, hk], U32)
    partf = g.at("partf", R + 38, [P, 2, hk])
    res = g.at("res", R + 38.5, [P, 3, hk])
    total = g.at("total", R + 39.5, [P, 2, HEADS])
    passed = g.sem("passed")
    ready, counted, picked, step, grown, turned, kept, hot_made = (g.sem(x) for x in (
        "summed", "counted", "picked", "pick_step", "exp_done", "turned", "kept", "hot_made"))
    per_pick = 5 * HEADS

    def wide(v, axis):
        return v.unsqueeze(axis).to_broadcast([P, HEADS, TOPK, TOPK])

    def heads(v):
        return v.rearrange("p (h k) -> p h k", k=TOPK)

    with ExitStack() as stack:
        bank = g.banks(stack, 1, "turned")[0]
        with nc.Block() as block:
            @block.gpsimd
            def _(pool):
                pool.iota(g.count[:, :], pattern=[[1, N_KEYS]], base=0, channel_multiplier=0,
                          allow_small_or_imprecise_dtypes=True).then_inc(counted, 1)

            @block.scalar
            def _(act):
                with steps(act, 0, TT, 1) as t:
                    act.wait_ge(step, 10 * t + 6)
                    act.activation(res[:, 2, :], res[:, 2, :], ACT.Exp).then_inc(grown, 1)

            @block.tensor
            def _(pe):
                with steps(pe, 0, TT, 1) as t:
                    pe.wait_ge(step, 10 * t + 10)
                    for r in range(3):
                        last = pe.transpose(bank[:, r * P:r * P + P], res[:, r, :], g.ident[:, :])
                    last.then_inc(turned, 1)

            @block.vector
            def _(dve):
                dve.wait_ge(counted, 1)
                with steps(dve, 0, TT, 1) as t:
                    def halves(buf, half):
                        return buf[:, bass.ds(t, 1), half::2, :].rearrange("p o h k -> p (o h) k")

                    dve.wait_ge(kept, 3 * t)
                    dve.tensor_tensor(cand[:, :, :, :], wide(halves(g.vals, 0), 3), wide(halves(g.vals, 1), 2),
                                      ALU.add).then_inc(ready, 1)
                    past(dve, ready, t + 1, passed)
                    top16(dve, HEADS, lambda h: cand[:, h, :, :].rearrange("p a b -> p (a b)"),
                          lambda h: work[:, h, :, :].rearrange("p a b -> p (a b)"), best, where, picked,
                          passed, per_pick * t)
                    dve.wait_ge(picked, per_pick * t + per_pick)
                    flat = where[:, :, :].rearrange("p h k -> p (h k)")
                    dve.tensor_scalar(part[:, 0, :], flat, 4, None, ALU.logical_shift_right).then_inc(step, 1)
                    dve.tensor_scalar(part[:, 1, :], flat, TOPK - 1, None, ALU.bitwise_and).then_inc(step, 1)
                    dve.wait_ge(step, 10 * t + 2)
                    dve.tensor_copy(partf[:, :, :], part[:, :, :]).then_inc(step, 1)
                    dve.wait_ge(step, 10 * t + 3)
                    for k in range(2):
                        dve.tensor_tensor(hot[:, k, :, :, :], wide(heads(partf[:, k, :]), 3),
                                          g.count[:, 0:TOPK].unsqueeze(1).unsqueeze(1)
                                          .to_broadcast([P, HEADS, TOPK, TOPK]), ALU.is_equal).then_inc(step, 1)
                    dve.tensor_tensor(heads(res[:, 2, :]), best[:, :, :],
                                      best[:, :, 0:1].to_broadcast([P, HEADS, TOPK]), ALU.subtract).then_inc(step, 1)
                    dve.wait_ge(step, 10 * t + 6)
                    for k in range(2):
                        dve.tensor_tensor(hot[:, k, :, :, :], hot[:, k, :, :, :], wide(halves(g.keyno, k), 2),
                                          ALU.mult).then_inc(hot_made, 1)
                    dve.wait_ge(grown, t + 1)
                    dve.tensor_reduce(total[:, 0, :], heads(res[:, 2, :]), AX.X, ALU.add).then_inc(step, 1)
                    for k in range(2):
                        dve.wait_ge(hot_made, 2 * t + (k + 1))
                        ins = dve.tensor_reduce(heads(res[:, k, :]), hot[:, k, :, :, :], AX.X, ALU.add)
                    ins.then_inc(step, 1)
                    dve.wait_ge(step, 10 * t + 8)
                    dve.reciprocal(total[:, 1, :], total[:, 0, :]).then_inc(step, 1)
                    dve.wait_ge(step, 10 * t + 9)
                    dve.tensor_tensor(heads(res[:, 2, :]), heads(res[:, 2, :]),
                                      total[:, 1, :].unsqueeze(2).to_broadcast([P, HEADS, TOPK]),
                                      ALU.mult).then_inc(step, 1)
                    dve.wait_ge(turned, t + 1)
                    for r, out in enumerate((g.first, g.second, g.gate)):
                        dve.tensor_copy(out[:, bass.ds(t * P, P)], bank[:, r * P:r * P + P]).then_inc(kept, 1)


GROUP = 64


def peer_gates(g):
    nc = g.nc
    QUAD = 4
    BY_POOL = 2
    n_groups = S // GROUP
    g.gates = nc.dram_tensor("gates", [n_groups, P, N_KEYS, GROUP], F32, kind="Internal").ap()
    hot2 = g.at("hot2", R + 21, [P, 4, QUAD, N_KEYS])
    hot1 = g.at("hot1", R + 25, [P, 4, QUAD, N_KEYS])
    now = g.at("now", R + 28.5 + 16.5, [P, 4 * QUAD])
    now_read, passed = g.sem("now_read"), g.sem("passed")
    stage = [g.at(f"stage{s}", R + (0 if s == 0 else 29), [P, N_KEYS, GROUP]) for s in range(2)]
    second_made, first_made, product, read = (g.sem(x) for x in ("second_hot", "first_hot", "product", "read"))
    stored = [g.sem(f"stored{s}") for s in range(2)]
    quads = GROUP // QUAD
    with ExitStack() as stack:
        banks = g.banks(stack, 4, "gates")

        with nc.Block() as block:
            @block.gpsimd
            def _(pool):
                pool.sem_inc(product, 4)
                with steps(pool, 0, S // QUAD, 4) as i:
                    pool.wait_ge(second_made, i)
                    pool.tensor_copy(now[:, :], g.second[:, bass.ds(i * QUAD, 4 * QUAD)]).then_inc(now_read, 1)
                    pool.wait_ge(now_read, i // 4 + 1)
                    for j in range(4):
                        pool.wait_ge(product, i + (j + 1))
                        pool.sem_inc(passed, 1)
                        for k in range(BY_POOL):
                            n = j * QUAD + k
                            ins = pool.tensor_scalar(hot2[:, j, k, :], g.count[:, :], now[:, n:n + 1], None,
                                                     ALU.is_equal)
                        ins.then_inc(second_made, 1)

            @block.vector
            def _(dve):
                with steps(dve, 0, S // QUAD, 4) as i:
                    for j in range(4):
                        dve.wait_ge(product, i + (j + 1))
                        for k in range(QUAD):
                            t = i * QUAD + (j * QUAD + k)
                            ins = dve.tensor_scalar(hot1[:, j, k, :], g.count[:, :], g.first[:, bass.ds(t, 1)],
                                                    g.gate[:, bass.ds(t, 1)], ALU.is_equal, ALU.mult)
                        for k in range(BY_POOL, QUAD):
                            t = i * QUAD + (j * QUAD + k)
                            ins = dve.tensor_scalar(hot2[:, j, k, :], g.count[:, :], g.second[:, bass.ds(t, 1)],
                                                    None, ALU.is_equal)
                        ins.then_inc(first_made, 1)

            @block.tensor
            def _(pe):
                with steps(pe, 0, S // QUAD, 4) as i:
                    for j in range(4):
                        pe.wait_ge(second_made, i + (j + 1))
                        pe.wait_ge(first_made, i + (j + 1))
                        pe.wait_ge(read, i + (j + 1))
                        for k in range(QUAD):
                            ins = pe.matmul(banks[j][:, k * P:k * P + P], hot2[:, j, k, :], hot1[:, j, k, :],
                                            start=True, stop=True)
                        ins.then_inc(product, 1)

            @block.scalar
            def _(act):
                act.sem_inc(read, 4)
                with steps(act, 0, n_groups, 2) as i:
                    for s in range(2):
                        act.wait_ge(stored[s], 8 * i)
                        with steps(act, 0, quads, 4) as q:
                            for j in range(4):
                                n = i * quads + q
                                act.wait_ge(product, n + (s * quads + j + 5))
                                act.activation(
                                    stage[s][:, :, bass.ds(q * QUAD + j * QUAD, QUAD)],
                                    banks[j][:, :].rearrange("p (t e) -> p e t", e=N_KEYS), ACT.Copy).then_inc(read, 1)

            @block.sync
            def _(sp):
                with steps(sp, 0, n_groups, 2) as i:
                    for s in range(2):
                        sp.wait_ge(read, i * quads + ((s + 1) * quads + 4))
                        sp.dma_start(g.gates[i + s], stage[s][:, :, :]).then_inc(stored[s], 16)
                for s in range(2):
                    sp.wait_ge(stored[s], 16 * n_groups // 2)


def peer_experts(g):
    nc, base = g.nc, g.base
    SL, B, UP = 4, 4, 6
    gate = g.at("gate", R, [P, S // GROUP, B, GROUP])
    more = g.at("split2", R + 4, [P, 2, 2, TILE], F32R)
    gelu = g.at("gelu", R + 12, [P, 2, S])
    w = g.at("weight", R + 14, [P, 2, S])
    wh = g.at("weight_high", R + 16, [P, B, S], F32R)
    wl = g.at("weight_low", R + 20, [P, B, S], F32R)
    high, low = list(g.high), list(g.low)
    g.high += [more[:, s, 0, :] for s in range(2)]
    g.low += [more[:, s, 1, :] for s in range(2)]
    gates_loaded, activated, weighed, w_high, w_low, up_done, added = (g.sem(x) for x in (
        "gates_loaded", "activated", "weighed", "w_high", "w_low", "up_done", "added"))
    per = 2 * B
    adds = 2 * 2 * TT

    def up_free(n):
        before = n - UP if n >= UP else max(m for m in range(adds) if m % UP == n) - adds
        return UP + before + 1

    with ExitStack() as stack:
        down = g.banks(stack, 2, "down")
        up = g.banks(stack, UP, "up")
        with nc.Block() as block:
            @block.sync
            def _(sp):
                with steps(sp, 0, N_PEER, per) as i:
                    for j in range(per):
                        if j == 0:
                            sp.wait_ge(weighed, i // 2)
                            sp.dma_start(gate[:, :, :, :], g.gates[:, :, bass.ds(i // 2, B), :]
                                         .rearrange("n p e t -> p n e t")).then_inc(gates_loaded, 16)
                        sp.wait_ge(g.high_split, i + (base + j + 1))
                        sp.wait_ge(g.low_split, i + (base + j + 1))
                        sp.dma_start(g.raw[:, j % RAW, :], g.io["stream"][i + (base + RAW + j)])\
                          .then_inc(g.raw_loaded[j % RAW], 16)

            @block.tensor
            def _(pe):
                with steps(pe, 0, N_PEER, per) as i:
                    for j in range(B):
                        pe.wait_ge(g.low_split, i + (base + j + 1))
                        pe.wait_ge(activated, i // 2 + (j + 1))
                        hi, lo = g.high[j], g.low[j]
                        for c in range(DC):
                            k = slice(c * P, c * P + P)
                            pe.matmul(down[j % 2][:, :], hi[:, k], g.xh[:, c, :], start=(c == 0), stop=False)
                            pe.matmul(down[j % 2][:, :], hi[:, k], g.xl[:, c, :], start=False, stop=False)
                            last = pe.matmul(down[j % 2][:, :], lo[:, k], g.xh[:, c, :], start=False,
                                             stop=(c == DC - 1))
                        last.then_inc(g.tile_used, 1)
                    for pair in range(2):
                        pe.wait_ge(g.low_split, i + (base + B + 2 * pair + 2))
                        pe.wait_ge(w_low, i // 2 + (2 * pair + 2))
                        for q in range(2 * TT):
                            n = 8 * pair + q
                            pe.wait_ge(added, 2 * i + up_free(n))
                            for k in range(2):
                                e = 2 * pair + k
                                rows = slice(q // 2 * P, q // 2 * P + P)
                                last = mm_rows(g, pe, g.high[e], g.low[e], up[n % UP][:, :], wh[:, e, rows],
                                               wl[:, e, rows], q % 2, k == 0, k == 1)
                            if q < 2 * TT - 1:
                                last.then_inc(up_done, 1)
                            else:
                                last.then_inc(g.tile_used, 2)

            @block.scalar
            def _(act):
                act.sem_inc(activated, 2)
                with steps(act, 0, N_PEER, per) as i:
                    for j in range(B):
                        for t in ((2, 3), (4,), (5,), ())[j]:
                            split_high(g, act, i, t, SL)
                        tile_done(g, act, i, j)
                        act.wait_ge(weighed, i // 2 + (j + 1))
                        act.activation(gelu[:, j % 2, :], down[j % 2][:, :], ACT.Gelu).then_inc(activated, 1)
                        act.wait_ge(weighed, i // 2 + (j + 3))
                        act.wait_ge(g.tile_used, i + (base + 2))
                        act.activation(wh[:, j, :], w[:, j % 2, :], ACT.Copy).then_inc(w_high, 1)
                    for t in (6, 7, 8, 9):
                        split_high(g, act, i, t, SL)

            @block.vector
            def _(dve):
                dve.sem_inc(weighed, 2)
                dve.sem_inc(added, UP)
                with steps(dve, 0, N_PEER, per) as i:
                    dve.wait_ge(gates_loaded, 2 * i + 16)
                    for j in range(B):
                        for t in ((2, 3), (4,), (5,), ())[j]:
                            split_low(g, dve, i, t, SL)
                        dve.wait_ge(activated, i // 2 + (j + 3))
                        dve.tensor_tensor(w[:, j % 2, :].rearrange("p (n t) -> p n t", t=GROUP),
                                          gelu[:, j % 2, :].rearrange("p (n t) -> p n t", t=GROUP),
                                          gate[:, :, j, :], ALU.mult).then_inc(weighed, 1)
                        dve.wait_ge(w_high, i // 2 + (j + 1))
                        dve.tensor_tensor(wl[:, j, :], w[:, j % 2, :], wh[:, j, :], ALU.subtract).then_inc(w_low, 1)
                    for pair in range(2):
                        for t in ((6, 7), (8, 9))[pair]:
                            split_low(g, dve, i, t, SL)
                        for q in range(2 * TT):
                            n = 8 * pair + q
                            if q < 2 * TT - 1:
                                dve.wait_ge(up_done, 14 * (i // 8) + (7 * pair + q + 1))
                            else:
                                tile_done(g, dve, i, B + 2 * pair + 1)
                            rows = g.h[:, q // 2, q % 2 * 512:q % 2 * 512 + 512]
                            dve.tensor_tensor(rows, rows, up[n % UP][:, :], ALU.add).then_inc(added, 1)
    g.high, g.low = high, low
    g.base += N_PEER


SZ, SX, SB_, SC = 0, 8, 16, 18
AQ, AK, AV, AZ = 0, 8, 16, 24
SSD_GROUPS = 2


def ssd_rows(g, rows_ps):
    nc = g.nc
    nh = SSD_HEADS
    g.rows = g.at("ssd_rows", R + 20, [64, S])
    v = g.at("v", R + 21, [nh, S])
    t = g.at("t", R + 22, [nh, S])
    dt = g.at("dt", R + 23, [nh, S])
    da = g.at("da", R + 24, [nh, S])
    neg_a = g.at("neg_a", R + 25, [nh, 1])
    g.sum_c = g.at("ssd_sum", R + 25.25, [P, nh, TT])
    g.dt_c = g.at("ssd_dt", R + 25.5, [P, nh, TT])
    g.left_c = g.at("ssd_left", R + 25.75, [P, nh, TT])
    g.last_c = g.at("ssd_last", R + 26, [P, nh, TT])
    soft, turned, tail, spread, rate = (g.sem(x) for x in ("softplus", "turned", "scalars", "last_spread", "rate"))
    with ExitStack() as stack:
        cols_ps = g.banks(stack, 1, "cols")[0]
        last_ps = g.banks(stack, 1, "last")[0]
        with nc.Block() as block:
            @block.scalar
            def _(act):
                act.activation(neg_a[:, :], g.heads[:, 2:3], ACT.Exp).then_inc(rate, 1)
                act.wait_ge(soft, 2)
                act.activation(t[:, :], v[:, :], ACT.Abs).then_inc(soft, 1)
                act.wait_ge(soft, 3)
                act.activation(t[:, :], t[:, :], ACT.Exp, scale=-1.0).then_inc(soft, 1)
                act.wait_ge(soft, 4)
                act.activation(t[:, :], t[:, :], ACT.Ln, bias=1.0).then_inc(soft, 1)
                act.wait_ge(spread, 1)
                act.activation(g.last_c[:, :, :], last_ps[:, 0:TT * nh].rearrange("p (h c) -> p h c", c=TT),
                               ACT.Exp).then_inc(tail, 1)
                act.wait_ge(tail, 4)
                act.activation(g.left_c[:, :, :], g.left_c[:, :, :], ACT.Exp).then_inc(tail, 1)

            @block.tensor
            def _(pe):
                pe.wait_ge(soft, 12)
                for c in range(TT):
                    pe.transpose(cols_ps[:, c * P:c * P + 64], g.rows[:, c * P:c * P + P], g.ident[0:64, 0:64])\
                      .then_inc(turned, 1)
                pe.wait_ge(tail, 2)
                pe.matmul(last_ps[:, 0:TT * nh], g.last_row[:, :], g.sum_c[:, :, :].rearrange("p h c -> p (h c)"),
                          start=True, stop=True).then_inc(spread, 1)

            @block.vector
            def _(dve):
                dve.memset(g.rows[:, :], 0.0).then_inc(soft, 1)
                dve.tensor_scalar(v[:, :], rows_ps[0:nh, :], g.heads[:, 3:4], None, ALU.add).then_inc(soft, 1)
                dve.wait_ge(soft, 5)
                dve.scalar_tensor_tensor(out=dt[:, :], in0=v[:, :], scalar=0.0, in1=t[:, :], op0=ALU.max,
                                         op1=ALU.add).then_inc(soft, 1)
                dve.wait_ge(soft, 6)
                dve.wait_ge(rate, 1)
                dve.tensor_scalar(da[:, :], dt[:, :], neg_a[:, :], -1.0, ALU.mult, ALU.mult).then_inc(soft, 1)
                dve.tensor_copy(g.rows[32:32 + nh, :], dt[:, :]).then_inc(soft, 1)
                dve.wait_ge(soft, 8)
                for c in range(TT):
                    w = slice(c * P, c * P + P)
                    dve.tensor_tensor_scan(out=g.rows[0:nh, w], data0=g.ones[0:nh, :], data1=da[:, w], initial=0.0,
                                           op0=ALU.mult, op1=ALU.add).then_inc(soft, 1)
                dve.wait_ge(turned, TT)
                cols = cols_ps[:, :].rearrange("p (c n) -> p n c", n=P)
                dve.tensor_copy(g.sum_c[:, :, :], cols[:, 0:nh, :]).then_inc(tail, 1)
                dve.tensor_copy(g.dt_c[:, :, :], cols[:, 32:32 + nh, :]).then_inc(tail, 1)
                dve.wait_ge(tail, 3)
                dve.tensor_tensor(g.left_c[:, :, :], last_ps[:, 0:TT * nh].rearrange("p (h c) -> p h c", c=TT),
                                  g.sum_c[:, :, :], ALU.subtract).then_inc(tail, 1)
                dve.wait_ge(tail, 5)
                dve.tensor_tensor(g.left_c[:, :, :], g.left_c[:, :, :], g.dt_c[:, :, :], ALU.mult).then_inc(tail, 1)
                dve.wait_ge(tail, 6)


def ssd(g, act_buf):
    nc = g.nc

    def tile(name, page):
        return g.at(name, R + page, [P, TT, P])

    def flat(b):
        return b[:, :, :].rearrange("p c n -> p (c n)")

    sel = [g.at(f"sel{s}", R + 27 + s, [SSD_HEADS, S]) for s in range(2)]
    grown = [tile(f"grown{s}", 29 + s) for s in range(2)]
    dec = [tile(f"dec{s}", 31 + s) for s in range(2)]
    attn = [tile(f"attn{s}", 33 + s) for s in range(2)]
    cg = [tile(f"cg{s}", 35 + s) for s in range(2)]
    x = tile("x", 37)
    xdt, xleft = tile("xdt", 38), tile("xleft", 39)
    st = g.at("st", R + 40, [P, TT - 1, P])
    y = g.at("y", R + 41, [P, S])
    scores = [tile(f"scores{q}", 42 + q) for q in range(SSD_GROUPS)]
    b_rows = [tile(f"b_rows{q}", 44 + q) for q in range(SSD_GROUPS)]
    m = {n: g.sem(n) for n in ("prepared", "scores_read", "b_read", "selected", "spread", "exp_made", "x_copied",
                               "diffed", "decayed", "masked", "attended", "c_scaled", "x_turned", "x_scaled",
                               "states_made", "states_added", "y_made", "y_read", "y_done")}
    pairs = SSD_HEADS // 2 // SSD_GROUPS
    with ExitStack() as stack:
        wide = g.banks(stack, 2, "wide")
        prep = g.banks(stack, 2, "prep")
        xb, sb, yb = g.banks(stack, 3, "ssd")

        def chunks(b):
            return b[:, :].rearrange("p (c n) -> p c n", n=P)

        with nc.Block() as block:
            @block.tensor
            def _(pe):
                for q in range(SSD_GROUPS):
                    if q:
                        pe.wait_ge(m["scores_read"], q)
                        pe.wait_ge(m["b_read"], q)
                    for c in range(TT):
                        w = slice(c * P, c * P + P)
                        pe.matmul(prep[0][:, w], act_buf[:, SB_ + q, w], act_buf[:, SC + q, w], start=True, stop=True)
                    for c in range(TT):
                        w = slice(c * P, c * P + P)
                        last = pe.transpose(prep[1][:, w], act_buf[:, SB_ + q, w], g.ident[:, :])
                    last.then_inc(m["prepared"], 1)
                for q in range(SSD_GROUPS):
                    pe.wait_ge(m["b_read"], q + 1)
                    with steps(pe, 0, pairs, 1) as i:
                        n = i + q * pairs
                        pe.wait_ge(m["selected"], 2 * n + 2)
                        pe.wait_ge(m["diffed"], 2 * n)
                        for s in range(2):
                            pe.matmul(wide[s][:, :], g.ones[0:SSD_HEADS, :], sel[s][:, :], start=True,
                                      stop=True).then_inc(m["spread"], 1)
                        pe.wait_ge(m["x_copied"], n + 1)
                        pe.wait_ge(m["x_scaled"], 2 * n)
                        for c in range(TT):
                            last = pe.transpose(chunks(xb)[:, c, :], x[:, c, :], g.ident[:, :])
                        last.then_inc(m["x_turned"], 1)
                        pe.wait_ge(m["x_scaled"], 2 * n + 2)
                        for c in range(TT - 1):
                            last = pe.matmul(chunks(sb)[:, c, :], b_rows[q][:, c, :], xleft[:, c, :], start=True,
                                             stop=True)
                        last.then_inc(m["states_made"], 1)
                        pe.wait_ge(m["states_added"], 5 * n + 5)
                        pe.wait_ge(m["attended"], 2 * n + 2)
                        pe.wait_ge(m["c_scaled"], 2 * n + 2)
                        pe.wait_ge(m["y_read"], n)
                        for s in range(2):
                            half = slice(64 * s, 64 * s + 64)
                            for c in range(TT):
                                last = pe.matmul(chunks(yb)[half, c, :], xdt[:, c, half], attn[s][:, c, :],
                                                 start=True, stop=(c == 0))
                                if c:
                                    last = pe.matmul(chunks(yb)[half, c, :], st[:, c - 1, half], cg[s][:, c, :],
                                                     start=False, stop=True)
                        last.then_inc(m["y_made"], 1)

            @block.scalar
            def _(act):
                for q in range(SSD_GROUPS):
                    act.wait_ge(m["prepared"], q + 1)
                    act.activation(flat(scores[q]), prep[0][:, :], ACT.Copy).then_inc(m["scores_read"], 1)
                    act.activation(flat(b_rows[q]), prep[1][:, :], ACT.Copy).then_inc(m["b_read"], 1)
                with steps(act, 0, pairs * SSD_GROUPS, 1) as n:
                    act.wait_ge(m["x_turned"], n)
                    act.activation(flat(x), act_buf[:, n + SX, :], ACT.Copy).then_inc(m["x_copied"], 1)
                    act.wait_ge(m["c_scaled"], 2 * n)
                    act.wait_ge(m["spread"], 2 * n + 2)
                    for s in range(2):
                        act.activation(flat(grown[s]), wide[s][:, :], ACT.Exp).then_inc(m["exp_made"], 1)
                    for s in range(2):
                        act.wait_ge(m["diffed"], 2 * n + (s + 1))
                        act.activation(flat(dec[s]), flat(dec[s]), ACT.Exp).then_inc(m["decayed"], 1)

            @block.gpsimd
            def _(pool):
                with steps(pool, 0, pairs * SSD_GROUPS, 1) as n:
                    for s in range(2):
                        pool.wait_ge(m["decayed"], 2 * n + (s + 1))
                        pool.tensor_tensor(dec[s][:, :, :], dec[s][:, :, :],
                                           g.upto[:, :].unsqueeze(1).to_broadcast([P, TT, P]),
                                           ALU.mult).then_inc(m["masked"], 1)

            @block.vector
            def _(dve):
                for q in range(SSD_GROUPS):
                    dve.wait_ge(m["scores_read"], q + 1)
                    with steps(dve, 0, pairs, 1) as i:
                        n = i + q * pairs

                        def heads(b):
                            return b[:, :, :].rearrange("p c (h d) -> p c h d", d=64)

                        def scalars(cols):
                            return cols[:, bass.ds(2 * n, 2), :].rearrange("p h c -> p c h").unsqueeze(3)\
                                .to_broadcast([P, TT, 2, 64])

                        for s in range(2):
                            dve.tensor_scalar(sel[s][:, :], g.rows[0:SSD_HEADS, :],
                                              g.head_mask[0:SSD_HEADS, bass.ds(2 * n + s, 1)], None,
                                              ALU.mult).then_inc(m["selected"], 1)
                        for s in range(2):
                            dve.wait_ge(m["exp_made"], 2 * n + (s + 1))
                            for c in range(TT):
                                ins = dve.tensor_scalar(dec[s][:, c, :], chunks(wide[s])[:, c, :],
                                                        g.sum_c[:, bass.ds(2 * n + s, 1), c], 0.0, ALU.subtract,
                                                        ALU.min)
                            ins.then_inc(m["diffed"], 1)
                        dve.wait_ge(m["x_turned"], n + 1)
                        for out, cols in ((xdt, g.dt_c), (xleft, g.left_c)):
                            for s in range(2):
                                src = xb[:, :].rearrange("p (c h d) -> p h c d", h=2, d=64)[:, s, :, :]
                                dst = out[:, :, :].rearrange("p c (h d) -> p h c d", d=64)[:, s, :, :]
                                ins = dve.tensor_tensor(
                                    dst, src, cols[:, bass.ds(2 * n + s, 1), :].rearrange("p o c -> p (o c)")
                                    .unsqueeze(2).to_broadcast([P, TT, 64]), ALU.mult)
                            ins.then_inc(m["x_scaled"], 1)
                        for s in range(2):
                            dve.wait_ge(m["exp_made"], 2 * n + (s + 1))
                            dve.tensor_tensor(flat(cg[s]), flat(grown[s]), act_buf[:, SC + q, :],
                                              ALU.mult).then_inc(m["c_scaled"], 1)
                        dve.wait_ge(m["states_made"], n + 1)
                        dve.tensor_copy(st[:, 0, :], chunks(sb)[:, 0, :]).then_inc(m["states_added"], 1)
                        for c in range(1, TT - 1):
                            dve.wait_ge(m["states_added"], 5 * n + (2 * c - 1))
                            for s in range(2):
                                half = slice(64 * s, 64 * s + 64)
                                dve.scalar_tensor_tensor(
                                    out=st[:, c, half], in0=st[:, c - 1, half],
                                    scalar=g.last_c[:, bass.ds(2 * n + s, 1), c], in1=chunks(sb)[:, c, half],
                                    op0=ALU.mult, op1=ALU.add).then_inc(m["states_added"], 1)
                        for s in range(2):
                            dve.wait_ge(m["masked"], 2 * n + (s + 1))
                            dve.tensor_tensor(flat(attn[s]), flat(dec[s]), flat(scores[q]),
                                              ALU.mult).then_inc(m["attended"], 1)
                        dve.wait_ge(m["y_made"], n + 1)
                        dve.scalar_tensor_tensor(out=y[:, :], in0=act_buf[:, n + SX, :],
                                                 scalar=g.cols[:, bass.ds(n + COLS["d_skip"][0], 1)], in1=yb[:, :],
                                                 op0=ALU.mult, op1=ALU.add).then_inc(m["y_read"], 1)
                        dve.wait_ge(m["y_read"], n + 1)
                        dve.tensor_tensor(act_buf[:, n + SZ, :], y[:, :], act_buf[:, n + SZ, :],
                                          ALU.mult).then_inc(m["y_done"], 1)


def ssd_norm(g, act_buf):
    nc = g.nc
    g.yh = g.at("yh", R + 36, [P, DC, S], F32R)
    g.yl = g.at("yl", R + 44, [P, DC, S], F32R)
    sq = g.at("sq", R + 20, [P, 2, S])
    v = g.at("v", R + 22, [P, SSD_GROUPS, S])
    t = g.at("t", R + 24, [P, SSD_GROUPS, S])
    r = g.at("r", R + 26, [P, SSD_GROUPS, S])
    y = g.at("y", R + 28, [P, 2, S])
    squared, summed, root, scaled, high, low = (g.sem(x) for x in (
        "squared", "summed", "root", "scaled", "y_high", "y_low"))
    per = DC // SSD_GROUPS
    with ExitStack() as stack:
        banks = g.banks(stack, SSD_GROUPS, "mean")
        with nc.Block() as block:
            @block.scalar
            def _(act):
                for n in range(DC):
                    if n >= 2:
                        act.wait_ge(summed, n - 1)
                    act.activation(sq[:, n % 2, :], act_buf[:, SZ + n, :], ACT.Square).then_inc(squared, 1)
                act.wait_ge(root, 3)
                act.activation(r[:, :, :], t[:, :, :], ACT.Sqrt).then_inc(root, 1)
                for n in range(DC):
                    act.wait_ge(scaled, n + 1)
                    act.activation(g.yh[:, n, :], y[:, n % 2, :], ACT.Copy).then_inc(high, 1)

            @block.tensor
            def _(pe):
                for n in range(DC):
                    pe.wait_ge(squared, n + 1)
                    pe.matmul(banks[n // per][:, :], g.ones[:, :], sq[:, n % 2, :], start=(n % per == 0),
                              stop=(n % per == per - 1)).then_inc(summed, 1)

            @block.vector
            def _(dve):
                for q in range(SSD_GROUPS):
                    dve.wait_ge(summed, per * (q + 1))
                    dve.tensor_scalar(v[:, q, :], banks[q][:, :], 1.0 / (per * P), EPS, ALU.mult,
                                      ALU.add).then_inc(root, 1)
                dve.wait_ge(root, 2)
                dve.reciprocal(t[:, :, :], v[:, :, :]).then_inc(root, 1)
                dve.wait_ge(root, 4)
                n = refine_root(dve, r[:, :, :], v[:, :, :], t[:, :, :], root, 4)
                dve.wait_ge(root, n)
                for n in range(DC):
                    if n >= 2:
                        dve.wait_ge(low, n - 1)
                    dve.scalar_tensor_tensor(out=y[:, n % 2, :], in0=act_buf[:, SZ + n, :],
                                             scalar=g.col("ssd_norm", n), in1=r[:, n // per, :], op0=ALU.mult,
                                             op1=ALU.mult).then_inc(scaled, 1)
                    dve.wait_ge(high, n + 1)
                    dve.tensor_tensor(g.yl[:, n, :], y[:, n % 2, :], g.yh[:, n, :], ALU.subtract).then_inc(low, 1)


def stick_breaking(g, act_buf):
    nc = g.nc
    OFF = (0, 512, 1024, 896)
    WIDE = 1280
    g.oh = g.at("oh", R + AQ, [P, DC, S], F32R)
    g.ol = g.at("ol", R + AK, [P, DC, S], F32R)
    soft = [g.at(f"soft{s}", R + 52 + 2.5 * s, [P, WIDE]) for s in range(2)]
    tmp = [g.at(f"tmp{s}", R + 57 + 2.5 * s, [P, WIDE]) for s in range(2)]
    ks, qs, vs = (g.at(n, R + 32 + k, [P, S]) for k, n in enumerate(("ks", "qs", "vs")))
    vr = g.at("v_rows", R + 35, [P, TT, P])
    o = g.at("o", R + 62, [P, S])
    m = {n: g.sem(n) for n in ("copied", "v_turned", "v_read", "logits", "abs_made", "exp_made", "log_made", "softened",
                               "soft_masked", "summed", "weights", "masked", "out_made", "out_gated", "o_high", "o_low",
                               "pool_passed", "act_passed")}
    with ExitStack() as stack:
        lg = [stack.enter_context(nc.psum_tensor(f"logits{s}", [P, 3 * 512], F32)) for s in range(2)]
        vb, ob = g.banks(stack, 2, "attn")
        pairs = SB_HEADS // 2

        def kb_of(buf, kb, qb=None):
            qb = kb if qb is None else qb
            return buf[:, OFF[kb] + (qb - kb) * P:OFF[kb] + (TT - kb) * P]

        with nc.Block() as block:
            @block.tensor
            def _(pe):
                with steps(pe, 0, pairs, 1) as n:
                    pe.wait_ge(m["copied"], 3 * n + 3)
                    for s in range(2):
                        pe.wait_ge(m["weights"], 2 * n)
                        half = slice(64 * s, 64 * s + 64)
                        for kb in (0, 1, 3, 2):
                            last = pe.matmul(kb_of(lg[s], kb), ks[half, kb * P:kb * P + P], qs[half, kb * P:],
                                             start=(kb != 3), stop=True, skip_group_check=True)
                        last.then_inc(m["logits"], 1)
                    pe.wait_ge(m["v_read"], n)
                    for c in range(TT):
                        last = pe.transpose(vb[:, c * P:c * P + P], vs[:, c * P:c * P + P], g.ident[:, :])
                    last.then_inc(m["v_turned"], 1)
                    for s in range(2):
                        pe.wait_ge(m["soft_masked"], 2 * n + (s + 1))
                        for kb in range(TT):
                            for k2 in range(kb, TT):
                                last = pe.matmul(kb_of(lg[s], kb, k2), (g.neg_from if k2 == kb else g.neg_ones)[:, :],
                                                 kb_of(soft[s], k2), start=False, stop=True, skip_group_check=True)
                        last.then_inc(m["summed"], 1)
                    pe.wait_ge(m["v_read"], n + 1)
                    pe.wait_ge(m["out_gated"], n)
                    for s in range(2):
                        pe.wait_ge(m["masked"], 2 * n + (s + 1))
                        half = slice(64 * s, 64 * s + 64)
                        for kb in range(TT):
                            last = pe.matmul(ob[half, kb * P:], vr[:, kb, half], kb_of(soft[s], kb),
                                             start=(kb == 0), stop=(kb == TT - 1), skip_group_check=True)
                    last.then_inc(m["out_made"], 1)

            @block.scalar
            def _(act):
                with steps(act, 0, pairs, 1) as n:
                    act.wait_ge(m["v_turned"], n)
                    past(act, m["logits"], 2 * n, m["act_passed"])
                    for dst, src in ((ks, AK), (qs, AQ), (vs, AV)):
                        act.activation(dst[:, :], act_buf[:, n + src, :], ACT.Copy).then_inc(m["copied"], 1)
                    for s in range(2):
                        act.wait_ge(m["logits"], 2 * n + (s + 1))
                        act.activation(tmp[s][:, :], lg[s][:, 0:WIDE], ACT.Abs).then_inc(m["abs_made"], 1)
                        act.wait_ge(m["abs_made"], 2 * n + (s + 1))
                        act.activation(tmp[s][:, :], tmp[s][:, :], ACT.Exp, scale=-1.0).then_inc(m["exp_made"], 1)
                        act.wait_ge(m["exp_made"], 2 * n + (s + 1))
                        act.activation(tmp[s][:, :], tmp[s][:, :], ACT.Ln, bias=1.0).then_inc(m["log_made"], 1)
                    act.wait_ge(m["v_turned"], n + 1)
                    act.activation(vr[:, :, :].rearrange("p c n -> p (c n)"), vb[:, :], ACT.Copy)\
                       .then_inc(m["v_read"], 1)
                    for s in range(2):
                        act.wait_ge(m["summed"], 2 * n + (s + 1))
                        act.activation(soft[s][:, :], lg[s][:, 0:WIDE], ACT.Exp).then_inc(m["weights"], 1)
                    past(act, m["out_gated"], n + 1, m["act_passed"])
                    act.activation(g.oh[:, n, :], o[:, :], ACT.Copy).then_inc(m["o_high"], 1)

            @block.gpsimd
            def _(pool):
                def mask(buf, sem):
                    for kb in range(TT):
                        v = buf[:, OFF[kb]:OFF[kb] + P]
                        ins = pool.affine_select(out=v, in_=v, compare_op=ALU.is_gt, fill=0.0, base=0,
                                                 pattern=[[1, P]], channel_multiplier=-1)
                    ins.then_inc(sem, 1)

                with steps(pool, 0, pairs, 1) as n:
                    for s in range(2):
                        pool.wait_ge(m["softened"], 2 * n + (s + 1))
                        pool.sem_inc(m["pool_passed"], 1)
                        mask(soft[s], m["soft_masked"])
                    for s in range(2):
                        pool.wait_ge(m["weights"], 2 * n + (s + 1))
                        pool.sem_inc(m["pool_passed"], 1)
                        mask(soft[s], m["masked"])

            @block.vector
            def _(dve):
                with steps(dve, 0, pairs, 1) as n:
                    for s in range(2):
                        dve.wait_ge(m["log_made"], 2 * n + (s + 1))
                        dve.wait_ge(m["out_made"], n)
                        dve.scalar_tensor_tensor(out=soft[s][:, :], in0=lg[s][:, 0:WIDE], scalar=0.0,
                                                 in1=tmp[s][:, :], op0=ALU.max,
                                                 op1=ALU.add).then_inc(m["softened"], 1)
                    dve.wait_ge(m["out_made"], n + 1)
                    dve.wait_ge(m["o_low"], n)
                    dve.tensor_tensor(o[:, :], ob[:, :], act_buf[:, n + AZ, :], ALU.mult).then_inc(m["out_gated"], 1)
                    dve.wait_ge(m["o_high"], n + 1)
                    dve.tensor_tensor(g.ol[:, n, :], o[:, :], g.oh[:, n, :], ALU.subtract).then_inc(m["o_low"], 1)


def finish(g, banks):
    nc = g.nc
    wp = g.at("norm_post", R, [P, D])
    junk = g.at("junk", R + 2, [P, 512])
    res = g.at("res", R + 3, [P, TT, D])
    ss = g.at("ss", R + 11, [P, TT, 2])
    st = g.at("stats", R + 11.5, [P, 4, TT])
    loaded, summed, root, scaled, added = (g.sem(x) for x in ("post_loaded", "summed", "root", "scaled", "added"))
    stored = g.sem("stored")
    with nc.Block() as block:
        @block.sync
        def _(sp):
            sp.dma_start(wp[:, :], g.io["norm_post"]).then_inc(loaded, 16)
            for t in range(TT):
                sp.wait_ge(added, 2 * t + 2)
                sp.dma_start(g.io["out"][t * P:t * P + P, :], res[:, t, :]).then_inc(stored, 16)
            sp.wait_ge(stored, 16 * TT)
            for j in range(RAW):
                sp.wait_ge(g.raw_loaded[j], 16 * (g.total // RAW))

        @block.scalar
        def _(act):
            for q in range(2 * TT):
                act.activation(junk[:, :], banks[q][:, :], ACT.Square, accum_out=ss[:, q // 2, q % 2:q % 2 + 1])\
                   .then_inc(summed, 1)
                act.wait_ge(summed, q + 1)
            act.wait_ge(root, 3)
            act.activation(st[:, 2, :], st[:, 1, :], ACT.Sqrt).then_inc(root, 1)

        @block.vector
        def _(dve):
            dve.wait_ge(summed, 2 * TT)
            dve.tensor_reduce(st[:, 0, :], ss[:, :, :], AX.X, ALU.add).then_inc(root, 1)
            dve.wait_ge(root, 1)
            dve.tensor_scalar(st[:, 0, :], st[:, 0, :], 1.0 / D, EPS, ALU.mult, ALU.add).then_inc(root, 1)
            dve.wait_ge(root, 2)
            dve.reciprocal(st[:, 1, :], st[:, 0, :]).then_inc(root, 1)
            dve.wait_ge(root, 4)
            n = refine_root(dve, st[:, 2, :], st[:, 0, :], st[:, 3, :], root, 4)
            dve.wait_ge(root, n)
            dve.wait_ge(loaded, 16)
            for q in range(2 * TT):
                t, w = q // 2, slice(q % 2 * 512, q % 2 * 512 + 512)
                dve.scalar_tensor_tensor(out=res[:, t, w], in0=banks[q][:, :], scalar=st[:, 2, t:t + 1],
                                         in1=wp[:, w], op0=ALU.mult, op1=ALU.mult).then_inc(scaled, 1)
            for q in range(2 * TT):
                t, w = q // 2, slice(q % 2 * 512, q % 2 * 512 + 512)
                dve.wait_ge(scaled, q + 1)
                dve.tensor_tensor(res[:, t, w], res[:, t, w], g.h[:, t, w], ALU.add).then_inc(added, 1)


def build(nc, io, until=99):
    g = Program(nc, io)
    setup(g)
    with ExitStack() as block1:
        act1 = g.act1 = g.at("act1", R, [P, N_PROJ1, S])
        rows1 = g.banks(block1, 1, "rows1")[0]
        g.run(normed_columns, "mix_norm", small=(io["w_ba"], rows1[0:64, :]))
        g.run(project, act1, N_PROJ1, ((4, ACT.Copy, 1.0), (8, ACT.Silu, 1.0)), "conv1")
        g.run(delta_rows, act1, rows1)
    if until > 2:
        g.run(delta_rule, act1)
        g.run(delta_norm, act1)
    if until > 3:
        g.run(pool_mix, act1)
        g.run(merge, (g.ph, g.pl), len(POOL_WINDOWS), (g.yh, g.yl), io["x"])
        with ExitStack() as stack:
            g.run(mix_out, stack)
    if until > 4:
        g.run(normed_columns, "ffn_norm")
        g.run(peer_scores)
    if until > 5:
        g.run(peer_pick)
        g.run(peer_gates)
    if until > 6:
        g.run(peer_experts)
    if until > 7:
        rows2 = nc.dram_tensor("rows2", [S, D], F32, kind="Internal").ap()
        with ExitStack() as stack:
            dt_ps = g.banks(stack, 1, "dt")[0]
            g.run(normed_columns, "pre2", (io["w_dt"], dt_ps[0:SSD_HEADS, :]), io["final_norm"], rows2)
            act2 = g.at("act2a", R, [P, N_PROJ2A, S])
            g.run(project, act2, N_PROJ2A, ((8, ACT.Silu, 1.0),), "conv2", "conv2_b")
            g.run(ssd_rows, dt_ps)
        g.run(ssd, act2)
        g.run(ssd_norm, act2)
    if until > 8:
        act2 = g.at("act2b", R, [P, N_PROJ2B, S])
        g.run(project, act2, N_PROJ2B, ((8, ACT.Copy, 64 ** -0.5), (16, ACT.Copy, 1.0), (8, ACT.Silu, 1.0)))
        g.run(stick_breaking, act2)
    if until > 9:
        g.run(merge, (g.yh, g.yl), DC, (g.oh, g.ol), rows2, "gate2_b")
        with ExitStack() as stack:
            g.run(finish, g.run(mix_out, stack))
    if until < 99:
        with nc.Block() as block:
            @block.sync
            def _(sp):
                for j in range(RAW):
                    sp.wait_ge(g.raw_loaded[j], 16 * (g.base // RAW + 1))
    return g



def _tiles(w):
    k, n = w.shape
    t = w.reshape(k // P, P, n // P, P).transpose(2, 1, 0, 3).reshape(n // P, P, k)
    return np.pad(t, ((0, 0), (0, 0), (0, TILE - k)))


def _columns(v):
    return np.asarray(v).reshape(-1, P).T


def layout(a):
    a = {k: np.asarray(v) for k, v in a.items()}
    w1, w2 = a["w_in"][0], a["w_in_2"][0]
    t1, lg = 512 + 4096, 512 + 4096 + 16
    stream = [_tiles(w1[:, 0:512]), _tiles(w1[:, 512 + 3072:t1]), _tiles(w1[:, 512:512 + 3072])]
    ga, gb = _tiles(w1[:, lg:lg + D]), _tiles(w1[:, lg + D:])
    stream.append(np.stack([ga, _tiles(a["w_pool_up"][0]), gb, _tiles(a["w_dn_up"][0])], 1).reshape(-1, P, TILE))
    stream.append(a["w_mix_out"][0].reshape(DC, P, D))
    stream.append(_tiles(a["peer_w_query"][0]))
    down = _tiles(a["peer_down"][0].T)
    up = a["peer_up"][0].reshape(N_KEYS, P, D)
    stream.append(np.stack([down.reshape(-1, 4, P, TILE), up.reshape(-1, 4, P, TILE)], 1).reshape(-1, P, TILE))
    z, xbc, dt, q = 1024, 2560, 2576, 2576 + 1024
    stream += [_tiles(w2[:, 0:z]), _tiles(w2[:, z:xbc]), _tiles(w2[:, dt:dt + 4096])]
    g0 = dt + 4096
    stream.append(np.stack([_tiles(w2[:, g0:g0 + D]), _tiles(a["w_ssd_proj_2"][0]), _tiles(w2[:, g0 + D:]),
                            _tiles(a["w_sb_proj_2"][0])], 1).reshape(-1, P, TILE))
    stream.append(a["w_out_2"][0].reshape(DC, P, D))
    stream = np.concatenate(stream)
    assert len(stream) == N_TILES

    def taps(w):
        return w.reshape(TAPS, -1, P).transpose(2, 1, 0).reshape(P, -1)

    cols = np.concatenate([
        _columns(a["mix_norm_w"]), _columns(a["ffn_norm_w"]), _columns(a["norm_pre_2"]), _columns(a["pool_scale"]),
        taps(a["conv_w"][0]), _columns(a["dn_norm_w"]), taps(a["conv_w_2"][0]), _columns(a["conv_b_2"]),
        _columns(a["ssd_norm_2"]), _columns(a["b_gate_2"]), _columns(np.repeat(a["d_skip_2"][0], 64))], 1)
    assert cols.shape == (P, N_COLS)
    heads = np.zeros((SSD_HEADS, 4), np.float32)
    heads[:8, 0], heads[:8, 1] = a["a_log"][0], a["dt_bias"][0]
    heads[:, 2], heads[:, 3] = a["a_log_2"][0], a["dt_bias_2"][0]
    ba = np.zeros((P, DC, 64), np.float32)
    ba[:, :, 0:8] = w1[:, t1 + 8:lg].reshape(DC, P, 8).transpose(1, 0, 2)
    ba[:, :, 32:40] = w1[:, t1:t1 + 8].reshape(DC, P, 8).transpose(1, 0, 2)
    keys = np.stack([a["peer_keys_1"][0], a["peer_keys_2"][0]], 1).reshape(16, N_KEYS, P)
    return {
        "x": a["x"][0], "stream": stream, "cols": cols, "heads": heads, "w_ba": ba,
        "w_dt": w2[:, xbc:dt].reshape(DC, P, 16).transpose(1, 0, 2),
        "pool_w": a["pool_w"][0].transpose(1, 0, 2), "keys": keys.transpose(2, 0, 1),
        "final_norm": np.tile(a["final_norm_w"], (P, 1)), "norm_post": np.tile(a["norm_post_2"][0], (P, 1)),
    }


def program(nc, shapes, until=99):
    io = {k: nc.dram_tensor(f"in_{k}", s, F32, kind="ExternalInput").ap() for k, s in shapes.items()}
    io["out"] = nc.dram_tensor("out", [S, D], F32, kind="ExternalOutput").ap()
    return build(nc, io, until)


def kernel(**inputs):
    import concourse.bacc as _bacc
    from concourse.bass_utils import run_bass_kernel_spmd as _run

    arrays = {k: np.ascontiguousarray(v) for k, v in layout(inputs).items()}
    nc = _bacc.Bacc("TRN2", target_bir_lowering=False, num_devices=1)
    program(nc, {k: v.shape for k, v in arrays.items()})
    r = _run(nc, [{f"in_{k}": v for k, v in arrays.items()}], core_ids=[0])
    return r.results[0]["out"].reshape(1, S, D)
```

```python
from contextlib import ExitStack, contextmanager

import numpy as np

import concourse.bass as bass
from concourse import mybir

ALU = mybir.AluOpType
ACT = mybir.ActivationFunctionType
AX = mybir.AxisListType
F32 = mybir.dt.float32
F32R = mybir.dt.float32r
U32 = mybir.dt.uint32

P = 128
D = 1024
S = 512
DC = D // P
TT = S // P
EPS = 1e-6
RAW = 4
TILE = 1024

POOL_WINDOWS = (2, 4, 8, 16)
HEADS = 8
TAPS = 4
TOPK = 16
N_KEYS = 128
SSD_HEADS = 16
SB_HEADS = 16
LEVELS = 7

N_PROJ1 = 36
N_MERGE = 32
N_OUT = 8
N_QUERY = 16
EARLY = 24
N_PEER = 2 * N_KEYS
N_PROJ2A = 20
N_SSD = 8
N_PROJ2B = 24
N_TILES = N_PROJ1 + N_MERGE + N_OUT + N_QUERY + N_PEER + N_PROJ2A + N_SSD + N_PROJ2B + N_MERGE + N_OUT

COLS = {}


def _col(name, n):
    COLS[name] = (sum(w for _, w in COLS.values()), n)


for _name, _n in (("mix_norm", 8), ("ffn_norm", 8), ("pre2", 8), ("pool_scale", 4), ("conv1", 24 * TAPS),
                  ("dn_norm", 1), ("conv2", 12 * TAPS), ("conv2_b", 12), ("ssd_norm", 8), ("gate2_b", 16),
                  ("d_skip", 8)):
    _col(_name, _n)
N_COLS = sum(w for _, w in COLS.values())


PAGE = 2048
SBUF_FROM = 16512
MISC, RAW_AT, SPLIT_AT, X_AT, R = 0, 6, 14, 22, 38
H_AT = R + 57
N_PAGES = R + 65


class Program:

    def __init__(self, nc, io):
        self.nc, self.io = nc, io
        self.base = 0
        self.total = io["stream"].shape[0]
        self.names = 0
        self.consts_end = 0

    def at(self, name, page, shape, dt=F32):
        self.names += 1
        assert page + int(np.prod(shape[1:])) * 4 / PAGE <= N_PAGES, (name, page, shape)
        return self.nc.alloc_sbuf_tensor_at(f"{name}_{self.names}", list(shape), dt,
                                            offset=SBUF_FROM + int(page * PAGE))

    def const(self, name, shape, dt=F32):
        at = self.consts_end
        self.consts_end += -(-int(np.prod(shape[1:])) * 4 // 32) * 32
        assert self.consts_end <= RAW_AT * PAGE, self.consts_end
        return self.at(name, MISC + at / PAGE, shape, dt)

    def banks(self, stack, n, name="bank"):
        self.names += 1
        return [stack.enter_context(self.nc.psum_tensor(f"{name}{b}_{self.names}", [P, 512], F32)) for b in range(n)]

    def sem(self, name):
        self.names += 1
        return self.nc.alloc_semaphore(f"{name}_{self.names}")

    def run(self, stage, *args, **kw):
        before = self.nc.snapshot_sems()
        result = stage(self, *args, **kw)
        self.nc.clear_and_free_semaphores(self.nc.allocated_since(before))
        self.nc.all_engine_barrier()
        return result

    def col(self, name, i=0):
        at = COLS[name][0] + i
        return self.cols[:, at:at + 1]


@contextmanager
def steps(eng, start, end, step):
    with eng.Fori(start // step, end // step) as k:
        yield k * step



def stream_load(g, sp, n):
    base = g.base
    n = min(n, g.total - RAW - base)
    if n <= 0:
        return
    with steps(sp, 0, n, RAW) as i:
        for j in range(RAW):
            sp.wait_ge(g.high_split, i + (base + j + 1))
            sp.wait_ge(g.low_split, i + (base + j + 1))
            sp.dma_start(g.raw[:, j, :], g.io["stream"][i + (base + RAW + j)]).then_inc(g.raw_loaded[j], 16)


def split_high(g, act, i, j, slots=2):
    t = g.base + j
    act.wait_ge(g.raw_loaded[t % RAW], 4 * i + 16 * (t // RAW + 1))
    act.wait_ge(g.tile_used, i + (t + 3 - slots))
    act.activation(g.high[t % slots], g.raw[:, t % RAW, :], ACT.Copy).then_inc(g.high_split, 1)


def split_low(g, dve, i, j, slots=2):
    t = g.base + j
    dve.wait_ge(g.raw_loaded[t % RAW], 4 * i + 16 * (t // RAW + 1))
    dve.wait_ge(g.high_split, i + (t + 1))
    dve.tensor_tensor(g.low[t % slots], g.raw[:, t % RAW, :], g.high[t % slots], ALU.subtract).then_inc(g.low_split, 1)


def tile_done(g, eng, i, j):
    eng.wait_ge(g.tile_used, i + (g.base + j + 3))


def mm_columns(g, pe, t, out, chunks=DC, x=None, start=0, stop=None):
    xh, xl = x or (g.xh, g.xl)
    hi, lo = g.high[t % 2], g.low[t % 2]
    for c in range(start, stop or chunks):
        w = slice(c * P, c * P + P)
        pe.matmul(out, hi[:, w], xh[:, c, :], start=(c == 0), stop=False)
        pe.matmul(out, hi[:, w], xl[:, c, :], start=False, stop=False)
        last = pe.matmul(out, lo[:, w], xh[:, c, :], start=False, stop=(c == chunks - 1))
    return last


def setup(g):
    nc, io = g.nc, g.io
    g.h = g.at("h", H_AT, [P, TT, D])
    g.xh = g.at("xh", X_AT, [P, DC, S], F32R)
    g.xl = g.at("xl", X_AT + 8, [P, DC, S], F32R)
    g.raw = g.at("raw", RAW_AT, [P, RAW, TILE])
    hl = g.at("split", SPLIT_AT, [P, 2, 2, TILE], F32R)
    g.high = [hl[:, s, 0, :] for s in range(2)]
    g.low = [hl[:, s, 1, :] for s in range(2)]
    g.cols = g.const("cols", [P, N_COLS])
    g.heads = g.const("heads", [SSD_HEADS, 4])
    g.ident = g.const("ident", [P, P])
    g.ones = g.const("ones", [P, P])
    g.upto = g.const("upto", [P, P])
    g.neg_from = g.const("neg_from", [P, P])
    g.neg_ones = g.const("neg_ones", [P, P])
    g.last_row = g.const("last_row", [P, P])
    g.to_row = g.const("to_row", [P, HEADS, 32])
    g.head_mask = g.const("head_mask", [P, SSD_HEADS])
    g.level = g.const("level", [P, LEVELS, P])
    g.raw_loaded = [g.sem(f"raw_loaded{j}") for j in range(RAW)]
    g.high_split = g.sem("high_split")
    g.low_split = g.sem("low_split")
    g.tile_used = g.sem("tile_used")
    cols_loaded, heads_loaded = g.sem("cols_loaded"), g.sem("heads_loaded")
    rows_loaded = g.sem("rows_loaded")
    consts = g.sem("consts")
    with nc.Block() as block:
        @block.sync
        def _(sp):
            sp.dma_start(g.h[:, :, :], io["x"].rearrange("(t p) d -> p t d", p=P)).then_inc(rows_loaded, 16)
            for j in range(RAW):
                sp.dma_start(g.raw[:, j, :], io["stream"][j]).then_inc(g.raw_loaded[j], 16)
            sp.wait_ge(rows_loaded, 16)

        @block.scalar
        def _(act):
            act.dma_start(g.cols[:, :], io["cols"]).then_inc(cols_loaded, 16)
            act.dma_start(g.heads[:, :], io["heads"]).then_inc(heads_loaded, 16)
            act.sem_inc(g.tile_used, 2)
            for j in range(2):
                split_high(g, act, 0, j)
            act.wait_ge(cols_loaded, 16)
            act.wait_ge(heads_loaded, 16)

        @block.vector
        def _(dve):
            for j in range(2):
                split_low(g, dve, 0, j)

        @block.gpsimd
        def _(pool):
            for b, v in ((g.ident, 0.0), (g.ones, 1.0), (g.upto, 1.0), (g.neg_from, -1.0), (g.neg_ones, -1.0),
                         (g.last_row, 1.0)):
                pool.memset(b[:, :], v).then_inc(consts, 1)
            pool.memset(g.to_row[:, :, :], 0.0).then_inc(consts, 1)
            pool.memset(g.head_mask[:, :], 0.0).then_inc(consts, 1)
            pool.memset(g.level[:, :, :], 0.0).then_inc(consts, 1)
            pool.wait_ge(consts, 9)
            for h in range(HEADS):
                pool.memset(g.to_row[:, h, h:h + 1], 1.0)
            for lv in range(LEVELS):
                w = 1 << lv
                pool.memset(g.level[:, lv, :].rearrange("p (b r) -> p b r", r=2 * w)[:, :, w:], 1.0).then_inc(consts, 1)
            n = 9 + LEVELS
            pool.wait_ge(consts, n)

            def select(view, compare, fill, base, pattern, mult):
                nonlocal n
                pool.affine_select(out=view, in_=view, compare_op=compare, fill=fill, base=base, pattern=pattern,
                                   channel_multiplier=mult).then_inc(consts, 1)
                n += 1

            select(g.ident[:, :], ALU.not_equal, 1.0, 0, [[-1, P]], 1)
            select(g.upto[:, :], ALU.is_ge, 0.0, 0, [[1, P]], -1)
            select(g.neg_from[:, :], ALU.is_ge, 0.0, 0, [[-1, P]], 1)
            select(g.last_row[:, :], ALU.is_ge, 0.0, 1 - P, [[0, P]], 1)
            for lv in range(LEVELS):
                w = 1 << lv
                v = g.level[:, lv, :].rearrange("p (b r) -> p b r", r=2 * w)
                select(v, ALU.is_ge, 0.0, 0, [[-2 * w, P // (2 * w)], [0, 2 * w]], 1)
                pool.wait_ge(consts, n)
                select(v, ALU.is_ge, 0.0, w - 1, [[2 * w, P // (2 * w)], [0, 2 * w]], -1)
            for q in range(4):
                pool.wait_ge(consts, n)
                select(g.head_mask[:, :], ALU.not_equal, 1.0, -32 * q, [[-1, SSD_HEADS]], 1)
            pool.wait_ge(consts, n)


def refine_root(dve, r, v, t, done, n):
    dve.tensor_tensor(t, r, r, ALU.mult).then_inc(done, 1)
    dve.wait_ge(done, n + 1)
    dve.tensor_tensor(t, t, v, ALU.mult).then_inc(done, 1)
    dve.wait_ge(done, n + 2)
    dve.tensor_scalar(t, t, -0.5, 1.5, ALU.mult, ALU.add).then_inc(done, 1)
    dve.wait_ge(done, n + 3)
    dve.tensor_tensor(r, r, t, ALU.mult).then_inc(done, 1)
    return n + 4


def normed_columns(g, weight, small=None, first_weight=None, rows_to=None):
    nc = g.nc
    with ExitStack() as stack:
        junk = g.at("junk", R, [P, D])
        rows = g.at("rows", R + 2, [P, TT, D])
        col = g.at("col", R + 10, [P, 2, S])
        wn = g.at("wn", R + 12, [P, D])
        ws = g.at("ws", R + 14, [P, DC, 64])
        ss = g.at("ss", R + 15, [P, 2, TT])
        rs = g.at("rs", R + 15.25, [P, 2, TT])
        var = g.at("var", R + 15.5, [P, 2, TT])
        tmp = g.at("tmp", R + 15.75, [P, 2, TT])
        turned_ps = g.banks(stack, 4, "turned")
        m = small[0].shape[2] if small else 0
        small_loaded, norm_loaded = g.sem("small_loaded"), g.sem("norm_loaded")
        summed, rooted, scaled, turned, columned, high, low = (
            g.sem(x) for x in ("summed", "rooted", "scaled", "turned", "columned", "x_high", "x_low"))
        small_used = g.sem("small_used")
        rounds = 2 if first_weight is not None else 1
        with nc.Block() as block:
            @block.sync
            def _(sp):
                if first_weight is not None:
                    sp.dma_start(wn[:, :], first_weight).then_inc(norm_loaded, 16)
                if rows_to is not None:
                    sp.wait_ge(scaled, TT)
                    sp.dma_start(rows_to.rearrange("(t p) d -> p t d", p=P), g.h[:, :, :]).then_inc(norm_loaded, 16)
                    sp.wait_ge(norm_loaded, 32)
                if small:
                    sp.dma_start(ws[:, :, 0:m], small[0]).then_inc(small_loaded, 16)

            @block.scalar
            def _(act):
                for r in range(rounds):
                    for t in range(TT):
                        if r == 1:
                            act.wait_ge(scaled, t + 1)
                        act.activation(junk[:, :], g.h[:, t, :], ACT.Square,
                                       accum_out=ss[:, r, t:t + 1]).then_inc(summed, 1)
                        act.wait_ge(summed, TT * r + t + 1)
                    act.wait_ge(rooted, 7 * r + 2)
                    act.activation(rs[:, r, :], rs[:, r, :], ACT.Sqrt).then_inc(rooted, 1)
                for c in range(DC):
                    act.wait_ge(columned, c + 1)
                    act.activation(g.xh[:, c, :], col[:, c % 2, :], ACT.Copy).then_inc(high, 1)

            @block.vector
            def _(dve):
                for r in range(rounds):
                    dve.wait_ge(summed, TT * (r + 1))
                    dve.tensor_scalar(var[:, r, :], ss[:, r, :], 1.0 / D, EPS, ALU.mult, ALU.add).then_inc(rooted, 1)
                    dve.wait_ge(rooted, 7 * r + 1)
                    dve.reciprocal(rs[:, r, :], var[:, r, :]).then_inc(rooted, 1)
                    dve.wait_ge(rooted, 7 * r + 3)
                    n = refine_root(dve, rs[:, r, :], var[:, r, :], tmp[:, r, :], rooted, 7 * r + 3)
                    dve.wait_ge(rooted, n)
                    if r == 0 and first_weight is not None:
                        dve.wait_ge(norm_loaded, 16)
                        for t in range(TT):
                            dve.scalar_tensor_tensor(out=g.h[:, t, :], in0=g.h[:, t, :], scalar=rs[:, 0, t:t + 1],
                                                     in1=wn[:, :], op0=ALU.mult, op1=ALU.mult).then_inc(scaled, 1)
                        dve.wait_ge(scaled, TT)
                for t in range(TT):
                    dve.tensor_scalar(rows[:, t, :], g.h[:, t, :], rs[:, rounds - 1, t:t + 1], None,
                                      ALU.mult).then_inc(scaled, 1)
                for c in range(DC + 1):
                    if c < DC:
                        dve.wait_ge(turned, c + 1)
                        if c >= 2:
                            dve.wait_ge(high, c - 1)
                            dve.wait_ge(low, c - 1)
                            if small:
                                dve.wait_ge(small_used, c - 1)
                        dve.tensor_scalar(col[:, c % 2, :], turned_ps[c % 4][:, :], g.col(weight, c), None,
                                          ALU.mult).then_inc(columned, 1)
                    if c:
                        dve.wait_ge(high, c)
                        dve.tensor_tensor(g.xl[:, c - 1, :], col[:, (c - 1) % 2, :], g.xh[:, c - 1, :],
                                          ALU.subtract).then_inc(low, 1)

            @block.tensor
            def _(pe):
                def narrow(c):
                    pe.wait_ge(columned, c + 1)
                    pe.matmul(small[1], ws[:, c, 0:m], col[:, c % 2, :], start=(c == 0),
                              stop=(c == DC - 1)).then_inc(small_used, 1)

                pe.wait_ge(scaled, TT * rounds)
                if small:
                    pe.wait_ge(small_loaded, 16)
                for c in range(DC):
                    if c >= 4:
                        pe.wait_ge(columned, c - 3)
                    for t in range(TT):
                        last = pe.transpose(turned_ps[c % 4][:, t * P:t * P + P], rows[:, t, c * P:c * P + P],
                                            g.ident[:, :])
                    last.then_inc(turned, 1)
                    if small and c >= 1:
                        narrow(c - 1)
                if small:
                    narrow(DC - 1)


def project(g, act_buf, n_tiles, plain, conv=None, conv_bias=None):
    nc = g.nc
    with ExitStack() as stack:
        out = g.banks(stack, 4, "proj")
        pre = g.at("pre", R + 40, [P, 2, 3 + S])
        mixed = g.at("conv", R + 43, [P, 2, S])
        read, summed, done = (g.sem(x) for x in ("bank_read", "conv_step", "conv_out"))
        cleared, silu = g.sem("pad_cleared"), g.sem("silu_done")
        base = g.base
        n_plain = sum(p[0] for p in plain)
        with nc.Block() as block:
            @block.sync
            def _(sp):
                stream_load(g, sp, n_tiles)

            @block.tensor
            def _(pe):
                with steps(pe, 0, n_tiles, 4) as i:
                    for j in range(4):
                        pe.wait_ge(g.low_split, i + (base + j + 1))
                        pe.wait_ge(read, i + (j + 1))
                        mm_columns(g, pe, base + j, out[j][:, :]).then_inc(g.tile_used, 1)

            @block.scalar
            def _(act):
                act.sem_inc(read, 4)
                at = 0
                for n, place, func, scale in plain:
                    with steps(act, at, at + n, 4) as i:
                        for j in range(4):
                            split_high(g, act, i, j + 2)
                            tile_done(g, act, i, j)
                            act.activation(act_buf[:, i + (j + place - at), :], out[j][:, :], func, scale=scale)\
                               .then_inc(read, 1)
                    at += n
                if n_tiles > n_plain:
                    def take(i, j):
                        split_high(g, act, i, j + 2)
                        tile_done(g, act, i, j)
                        act.wait_ge(done, i + (j + 1 - n_plain))
                        act.activation(pre[:, j % 2, 3:], out[j % 4][:, :], ACT.Copy).then_inc(read, 1)

                    def finish(i, j):
                        act.wait_ge(done, i + (j + 3 - n_plain))
                        b = 0.0
                        if conv_bias:
                            b = g.cols[:, bass.ds(i + (COLS[conv_bias][0] + j - n_plain), 1)]
                        act.activation(act_buf[:, bass.ds(i + j, 1), :].rearrange("p o s -> p (o s)"),
                                       mixed[:, j % 2, :], ACT.Silu, bias=b).then_inc(silu, 1)

                    act.wait_ge(cleared, 1)
                    take(n_plain, 0)
                    with steps(act, n_plain, n_tiles - 4, 4) as i:
                        for j in range(4):
                            take(i, j + 1)
                            finish(i, j)
                    for j in range(4):
                        if j < 3:
                            take(n_tiles - 4, j + 1)
                        finish(n_tiles - 4, j)

            @block.vector
            def _(dve):
                with steps(dve, 0, n_plain, 4) as i:
                    for j in range(4):
                        split_low(g, dve, i, j + 2)
                if n_tiles > n_plain:
                    dve.memset(pre[:, :, 0:3], 0.0).then_inc(cleared, 1)
                    dve.sem_inc(done, 2)
                    with steps(dve, n_plain, n_tiles, 4) as i:
                        for j in range(4):
                            split_low(g, dve, i, j + 2)
                            w = COLS[conv][0]
                            dve.wait_ge(read, i + (j + 5))
                            b = j % 2
                            for k in range(TAPS):
                                tap = g.cols[:, bass.ds(4 * i + (w + 4 * (j - n_plain) + k), 1)]
                                if k == 0:
                                    if j >= 2:
                                        dve.wait_ge(silu, i + (j - 1 - n_plain))
                                    ins = dve.tensor_scalar(mixed[:, b, :], pre[:, b, 0:S], tap, None, ALU.mult)
                                else:
                                    dve.wait_ge(summed, 3 * i + (3 * (j - n_plain) + k))
                                    ins = dve.scalar_tensor_tensor(out=mixed[:, b, :], in0=pre[:, b, k:k + S],
                                                                   scalar=tap, in1=mixed[:, b, :], op0=ALU.mult,
                                                                   op1=ALU.add)
                                ins.then_inc(summed if k < 3 else done, 1)
    g.base += n_tiles


XA, Z, Q, K, V = 0, 4, 12, 20, 28


def delta_rows(g, act_buf, rows_ps):
    nc = g.nc
    g.rows = g.at("rows", R + 62, [P, S])
    v = g.at("v", R + 58, [P, S])
    t = g.at("t", R + 59, [P, S])
    u = g.at("u", R + 60, [P, S])
    sq = g.at("sq", R + 56, [P, 2, S])
    neg_a = g.const("neg_a", [P, 1])
    g.sum_c = g.const("sum_c", [P, HEADS, TT])
    g.beta_c = g.const("beta_c", [P, HEADS, TT])
    g.nbeg_c = g.const("nbeg_c", [P, HEADS, TT])
    g.left_c = g.const("left_c", [P, HEADS, TT])
    g.last_c = g.const("last_c", [P, HEADS, TT])
    eg = g.const("eg", [P, HEADS, TT])
    cleared, squared, summed, root, soft, turned, spread, tail = (g.sem(x) for x in (
        "rows_cleared", "squared", "norms_summed", "root", "softplus", "rows_turned", "last_spread",
        "scalars"))
    with ExitStack() as stack:
        cols_ps = g.banks(stack, 1, "cols")[0]
        last_ps = g.banks(stack, 1, "last")[0]
        with nc.Block() as block:
            @block.scalar
            def _(act):
                act.wait_ge(soft, 1)
                act.activation(t[0:8, :], v[0:8, :], ACT.Abs).then_inc(soft, 1)
                act.wait_ge(soft, 2)
                act.activation(t[0:8, :], t[0:8, :], ACT.Exp, scale=-1.0).then_inc(soft, 1)
                act.activation(neg_a[0:8, :], g.heads[0:8, 0:1], ACT.Exp)
                act.wait_ge(soft, 3)
                act.activation(t[0:8, :], t[0:8, :], ACT.Ln, bias=1.0).then_inc(soft, 1)
                act.wait_ge(cleared, 1)
                act.activation(g.rows[32:40, :], rows_ps[32:40, :], ACT.Sigmoid).then_inc(soft, 1)
                for n in range(2 * HEADS):
                    if n >= 2:
                        act.wait_ge(summed, n - 1)
                    act.activation(sq[:, n % 2, :], act_buf[:, (K if n < HEADS else Q) + n % HEADS, :],
                                   ACT.Square).then_inc(squared, 1)
                act.wait_ge(root, 2)
                act.activation(g.rows[64:, :], t[64:, :], ACT.Sqrt).then_inc(root, 1)
                act.wait_ge(tail, 2)
                act.activation(eg[:, :, :], g.sum_c[:, :, :], ACT.Exp).then_inc(tail, 1)
                act.wait_ge(spread, 1)
                act.activation(g.last_c[:, :, :], last_ps[:, 0:32].rearrange("p (h c) -> p h c", c=TT),
                               ACT.Exp).then_inc(tail, 1)
                act.wait_ge(tail, 5)
                act.activation(g.left_c[:, :, :], g.left_c[:, :, :], ACT.Exp).then_inc(tail, 1)

            @block.tensor
            def _(pe):
                for n in range(2 * HEADS):
                    pe.wait_ge(squared, n + 1)
                    q = 64 if n < HEADS else 96
                    pe.matmul(rows_ps[q:q + 32, :], g.to_row[:, n % HEADS, :], sq[:, n % 2, :],
                              start=(n % HEADS == 0), stop=(n % HEADS == HEADS - 1)).then_inc(summed, 1)
                pe.wait_ge(soft, 11)
                for c in range(TT):
                    pe.transpose(cols_ps[:, c * P:c * P + 64], g.rows[0:64, c * P:c * P + P], g.ident[0:64, 0:64])\
                      .then_inc(turned, 1)
                pe.wait_ge(tail, 2)
                pe.matmul(last_ps[:, 0:32], g.last_row[:, :], g.sum_c[:, :, :].rearrange("p h c -> p (h c)"),
                          start=True, stop=True).then_inc(spread, 1)

            @block.vector
            def _(dve):
                dve.tensor_scalar(v[0:8, :], rows_ps[0:8, :], g.heads[0:8, 1:2], None, ALU.add).then_inc(soft, 1)
                dve.memset(g.rows[:, :], 0.0).then_inc(cleared, 1)
                dve.wait_ge(soft, 5)
                dve.scalar_tensor_tensor(out=u[0:8, :], in0=v[0:8, :], scalar=0.0, in1=t[0:8, :], op0=ALU.max,
                                         op1=ALU.add).then_inc(soft, 1)
                dve.wait_ge(soft, 6)
                dve.tensor_scalar(u[0:8, :], u[0:8, :], neg_a[0:8, :], -1.0, ALU.mult, ALU.mult).then_inc(soft, 1)
                dve.wait_ge(soft, 7)
                for c in range(TT):
                    w = slice(c * P, c * P + P)
                    dve.tensor_tensor_scan(out=g.rows[0:8, w], data0=g.ones[0:8, :], data1=u[0:8, w], initial=0.0,
                                           op0=ALU.mult, op1=ALU.add).then_inc(soft, 1)
                dve.wait_ge(summed, 2 * HEADS)
                dve.tensor_scalar(v[64:, :], rows_ps[64:, :], EPS, None, ALU.add).then_inc(root, 1)
                dve.wait_ge(root, 1)
                dve.reciprocal(t[64:, :], v[64:, :]).then_inc(root, 1)
                dve.wait_ge(root, 3)
                n = refine_root(dve, g.rows[64:, :], v[64:, :], t[64:, :], root, 3)
                dve.wait_ge(root, n)
                dve.tensor_scalar(g.rows[96:, :], g.rows[96:, :], P ** -0.5, None, ALU.mult).then_inc(root, 1)
                dve.wait_ge(turned, TT)
                cols = cols_ps[:, :].rearrange("p (c n) -> p n c", n=P)
                dve.tensor_copy(g.sum_c[:, :, :], cols[:, 0:8, :]).then_inc(tail, 1)
                dve.tensor_copy(g.beta_c[:, :, :], cols[:, 32:40, :]).then_inc(tail, 1)
                dve.wait_ge(tail, 3)
                dve.scalar_tensor_tensor(out=g.nbeg_c[:, :, :], in0=eg[:, :, :], scalar=-1.0, in1=g.beta_c[:, :, :],
                                         op0=ALU.mult, op1=ALU.mult)
                dve.wait_ge(spread, 1)
                dve.wait_ge(tail, 4)
                dve.tensor_tensor(g.left_c[:, :, :], last_ps[:, 0:32].rearrange("p (h c) -> p h c", c=TT),
                                  g.sum_c[:, :, :], ALU.subtract).then_inc(tail, 1)
                dve.wait_ge(root, n + 1)


SLOTS = 2


def nth(i, s, per, k=0):
    return per * i + (SLOTS * k + s + 1)


def delta_rule(g, act_buf):
    nc = g.nc

    def tile(name, page):
        return g.at(name, page, [P, TT, P])

    bufs = []
    for s in range(SLOTS):
        a = R + 36 + 13 * s
        b = {n: tile(n, a + k) for k, n in enumerate(
            ("kn", "qn", "dec", "db", "d", "attn", "x", "kb", "kd", "qg", "sel", "vb"))}
        b["inv"], b["inv_t"], b["part"], b["w"] = b["kn"], b["qn"], b["db"], b["sel"]
        b["vn"] = g.at("vn", a + 12, [P, P])
        b["st"] = g.at("st", a + 12.25, [P, P])
        bufs.append(b)
    names = ("selected", "spread", "k_normed", "q_normed", "diffed", "decayed", "masked", "grown", "betad", "grams",
             "lowered", "attended", "v_copied", "rows_turned", "v_scaled", "k_scaled", "k_left", "q_scaled",
             "part_made", "first_t", "crossed", "cross_read", "product_made", "inv_made", "inv_t_made",
             "w_made", "w_read", "new_made", "new_read", "out_made", "state_made", "state_added", "head_done")
    m = {n: g.sem(n) for n in names}

    def per(b):
        return b[:, :, :].rearrange("p c n -> p (c n)")

    with ExitStack() as stack:
        banks = [g.banks(stack, 4, "delta") for _ in range(SLOTS)]

        def ps(s, k):
            return banks[s][k][:, :].rearrange("p (c n) -> p c n", n=P)

        with nc.Block() as block:
            @block.tensor
            def _(pe):
                with steps(pe, 0, HEADS, SLOTS) as i:
                    for s in range(SLOTS):
                        b = bufs[s]
                        pe.wait_ge(m["selected"], i + (s + 1))
                        for q in range(4):
                            last = pe.matmul(banks[s][q][:, :], g.ones[32 * q:32 * q + 32, :],
                                             per(b["sel"])[32 * q:32 * q + 32, :], start=True, stop=True)
                        last.then_inc(m["spread"], 1)
                    for s in range(SLOTS):
                        b = bufs[s]
                        pe.wait_ge(m["k_normed"], i + (s + 1))
                        pe.wait_ge(m["q_normed"], i + (s + 1))
                        for c in range(TT):
                            pe.matmul(ps(s, 2)[:, c, :], b["kn"][:, c, :], b["kn"][:, c, :], start=True, stop=True)
                        for c in range(TT):
                            last = pe.matmul(ps(s, 3)[:, c, :], b["kn"][:, c, :], b["qn"][:, c, :], start=True,
                                             stop=True)
                        last.then_inc(m["grams"], 1)
                    for s in range(SLOTS):
                        b = bufs[s]
                        pe.wait_ge(m["v_copied"], i + (s + 1))
                        pe.wait_ge(m["grown"], i + (s + 1))
                        pe.wait_ge(m["diffed"], i + (s + 1))
                        pe.wait_ge(m["betad"], i + (s + 1))
                        for c in range(TT):
                            pe.transpose(ps(s, 0)[:, c, :], b["kn"][:, c, :], g.ident[:, :])
                        for c in range(TT):
                            last = pe.transpose(ps(s, 1)[:, c, :], b["x"][:, c, :], g.ident[:, :])
                        last.then_inc(m["rows_turned"], 1)
                    for s in range(SLOTS):
                        b = bufs[s]
                        pe.wait_ge(m["part_made"], nth(i, s, LEVELS))
                        pe.wait_ge(m["lowered"], i + (s + 1))
                        for c in range(TT):
                            last = pe.matmul(ps(s, 2)[:, c, :], b["part"][:, c, :], g.ident[:, :], start=True,
                                             stop=True)
                        last.then_inc(m["first_t"], 1)
                    for lv in range(1, LEVELS):
                        for s in range(SLOTS):
                            b = bufs[s]
                            pe.wait_ge(m["part_made"], nth(i, s, LEVELS, lv))
                            pe.wait_ge(m["inv_made"], nth(i, s, LEVELS - 1, lv - 1))
                            for c in range(TT):
                                last = pe.matmul(ps(s, 2)[:, c, :], b["part"][:, c, :], b["inv"][:, c, :],
                                                 start=True, stop=True)
                            last.then_inc(m["crossed"], 1)
                        for s in range(SLOTS):
                            b = bufs[s]
                            pe.wait_ge(m["cross_read"], nth(i, s, LEVELS - 1, lv - 1))
                            pe.wait_ge(m["inv_t_made"], nth(i, s, LEVELS, lv - 1))
                            if lv == 1:
                                pe.wait_ge(m["attended"], i + (s + 1))
                                pe.wait_ge(m["k_left"], i + (s + 1))
                            if lv < LEVELS - 1:
                                for c in range(TT):
                                    pe.matmul(ps(s, 3)[:, c, :], b["inv_t"][:, c, :], b["x"][:, c, :],
                                              start=True, stop=True)
                            for c in range(TT):
                                last = pe.matmul(ps(s, 0)[:, c, :], b["x"][:, c, :], b["inv_t"][:, c, :],
                                                 start=True, stop=True)
                            last.then_inc(m["product_made"], 1)
                    for s in range(SLOTS):
                        b = bufs[s]
                        pe.wait_ge(m["inv_t_made"], nth(i, s, LEVELS, LEVELS - 1))
                        pe.wait_ge(m["k_scaled"], i + (s + 1))
                        for c in range(TT):
                            last = pe.matmul(ps(s, 2)[:, c, :], b["kb"][:, c, :], b["inv_t"][:, c, :], start=True,
                                             stop=True)
                        last.then_inc(m["w_made"], 1)
                    for c in range(TT):
                        for s in range(SLOTS):
                            b = bufs[s]
                            if c == 0:
                                pe.wait_ge(m["v_scaled"], i + (s + 1))
                                pe.wait_ge(m["w_read"], i + (s + 1))
                            else:
                                pe.wait_ge(m["state_added"], nth(i, s, TT - 1, c - 1))
                            last = pe.matmul(ps(s, 3)[:, c, :], b["inv_t"][:, c, :], b["vb"][:, c, :], start=True,
                                             stop=(c == 0))
                            if c:
                                last = pe.matmul(ps(s, 3)[:, c, :], b["w"][:, c, :], b["st"][:, :], start=False,
                                                 stop=True)
                            last.then_inc(m["new_made"], 1)
                        for s in range(SLOTS):
                            b = bufs[s]
                            pe.wait_ge(m["new_read"], nth(i, s, TT, c))
                            if c == 0:
                                pe.wait_ge(m["q_scaled"], i + (s + 1))
                            if c < TT - 1:
                                pe.matmul(ps(s, 0)[:, c, :], b["kd"][:, c, :], b["vn"][:, :], start=True,
                                          stop=True).then_inc(m["state_made"], 1)
                            if c:
                                pe.matmul(ps(s, 1)[:, c, :], b["st"][:, :], b["qg"][:, c, :], start=True, stop=False)
                            pe.matmul(ps(s, 1)[:, c, :], b["vn"][:, :], b["attn"][:, c, :], start=(c == 0),
                                      stop=True).then_inc(m["out_made"], 1)

            @block.scalar
            def _(act):
                act.sem_inc(m["head_done"], SLOTS)
                with steps(act, 0, HEADS, SLOTS) as i:
                    for s in range(SLOTS):
                        b = bufs[s]
                        act.wait_ge(m["spread"], i + (s + 1))
                        act.activation(per(b["qg"]), banks[s][0][:, :], ACT.Exp).then_inc(m["grown"], 1)
                        act.activation(per(b["x"]), act_buf[:, i + (V + s), :], ACT.Copy).then_inc(m["v_copied"], 1)
                        act.wait_ge(m["diffed"], i + (s + 1))
                        act.activation(per(b["dec"]), per(b["dec"]), ACT.Exp).then_inc(m["decayed"], 1)
                    for lv in range(1, LEVELS):
                        for s in range(SLOTS):
                            b = bufs[s]
                            act.wait_ge(m["crossed"], nth(i, s, LEVELS - 1, lv - 1))
                            act.activation(per(b["x"]), banks[s][2][:, :], ACT.Copy).then_inc(m["cross_read"], 1)
                    for s in range(SLOTS):
                        b = bufs[s]
                        act.wait_ge(m["w_made"], i + (s + 1))
                        act.activation(per(b["w"]), banks[s][2][:, :], ACT.Copy).then_inc(m["w_read"], 1)
                    for c in range(TT):
                        for s in range(SLOTS):
                            b = bufs[s]
                            act.wait_ge(m["new_made"], nth(i, s, TT, c))
                            act.activation(b["vn"][:, :], ps(s, 3)[:, c, :], ACT.Copy).then_inc(m["new_read"], 1)
                    for s in range(SLOTS):
                        act.wait_ge(m["out_made"], nth(i, s, TT, TT - 1))
                        act.activation(act_buf[:, i + (Q + s), :], banks[s][1][:, :],
                                       ACT.Copy).then_inc(m["head_done"], 1)

            @block.gpsimd
            def _(pool):
                with steps(pool, 0, HEADS, SLOTS) as i:
                    for s in range(SLOTS):
                        b = bufs[s]
                        pool.wait_ge(m["decayed"], i + (s + 1))
                        pool.tensor_tensor(b["dec"][:, :, :], b["dec"][:, :, :],
                                           g.upto[:, :].unsqueeze(1).to_broadcast([P, TT, P]),
                                           ALU.mult).then_inc(m["masked"], 1)
                    for lv in range(LEVELS):
                        for s in range(SLOTS):
                            b = bufs[s]
                            if lv == 0:
                                pool.wait_ge(m["lowered"], i + (s + 1))
                            elif lv == 1:
                                pool.wait_ge(m["first_t"], i + (s + 1))
                                pool.wait_ge(m["inv_t_made"], nth(i, s, LEVELS))
                            else:
                                pool.wait_ge(m["crossed"], nth(i, s, LEVELS - 1, lv - 2))
                            pool.tensor_tensor(b["part"][:, :, :], b["d"][:, :, :],
                                               g.level[:, lv, :].unsqueeze(1).to_broadcast([P, TT, P]),
                                               ALU.mult).then_inc(m["part_made"], 1)

            @block.vector
            def _(dve):
                def scaled(out, src, cols, h, sem):
                    dve.tensor_tensor(out[:, :, :], src, cols[:, bass.ds(h, 1), :].rearrange("p o c -> p (o c)")
                                      .unsqueeze(2).to_broadcast([P, TT, P]), ALU.mult).then_inc(sem, 1)

                with steps(dve, 0, HEADS, SLOTS) as i:
                    for s in range(SLOTS):
                        b = bufs[s]
                        dve.wait_ge(m["head_done"], i + (s + 1))
                        dve.tensor_scalar(per(b["sel"]), g.rows[:, :], g.head_mask[:, bass.ds(i + s, 1)], None,
                                          ALU.mult).then_inc(m["selected"], 1)
                    for s in range(SLOTS):
                        b = bufs[s]
                        h = i + s
                        dve.wait_ge(m["grown"], i + (s + 1))
                        for c in range(TT):
                            ins = dve.tensor_scalar(b["dec"][:, c, :], ps(s, 0)[:, c, :],
                                                    g.sum_c[:, bass.ds(h, 1), c], 0.0, ALU.subtract, ALU.min)
                        ins.then_inc(m["diffed"], 1)
                        dve.tensor_tensor(per(b["kn"]), act_buf[:, i + (K + s), :], banks[s][2][:, :],
                                          ALU.mult).then_inc(m["k_normed"], 1)
                        dve.tensor_tensor(per(b["qn"]), act_buf[:, i + (Q + s), :], banks[s][3][:, :],
                                          ALU.mult).then_inc(m["q_normed"], 1)
                        dve.wait_ge(m["grown"], i + (s + 1))
                        dve.wait_ge(m["q_normed"], i + (s + 1))
                        dve.tensor_tensor(per(b["qg"]), per(b["qg"]), per(b["qn"]), ALU.mult).then_inc(m["q_scaled"], 1)
                    for s in range(SLOTS):
                        b = bufs[s]
                        dve.wait_ge(m["masked"], i + (s + 1))
                        dve.tensor_tensor(per(b["db"]), per(b["dec"]), banks[s][1][:, :],
                                          ALU.mult).then_inc(m["betad"], 1)
                        dve.wait_ge(m["grams"], i + (s + 1))
                        dve.wait_ge(m["betad"], i + (s + 1))
                        dve.tensor_tensor(per(b["d"]), banks[s][2][:, :], per(b["db"]),
                                          ALU.mult).then_inc(m["lowered"], 1)
                        dve.tensor_tensor(per(b["attn"]), banks[s][3][:, :], per(b["dec"]),
                                          ALU.mult).then_inc(m["attended"], 1)
                    ident = g.ident[:, :].unsqueeze(1).to_broadcast([P, TT, P])
                    for s in range(SLOTS):
                        b = bufs[s]
                        h = i + s
                        dve.wait_ge(m["rows_turned"], i + (s + 1))
                        scaled(b["vb"], ps(s, 1), g.beta_c, h, m["v_scaled"])
                        scaled(b["kb"], ps(s, 0), g.nbeg_c, h, m["k_scaled"])
                        scaled(b["kd"], ps(s, 0), g.left_c, h, m["k_left"])
                    for s in range(SLOTS):
                        b = bufs[s]
                        dve.wait_ge(m["part_made"], nth(i, s, LEVELS))
                        dve.tensor_tensor(b["inv_t"][:, :, :], ident, b["part"][:, :, :],
                                          ALU.subtract).then_inc(m["inv_t_made"], 1)
                        dve.wait_ge(m["first_t"], i + (s + 1))
                        dve.tensor_tensor(b["inv"][:, :, :], ident, ps(s, 2),
                                          ALU.subtract).then_inc(m["inv_made"], 1)
                    for lv in range(1, LEVELS):
                        for s in range(SLOTS):
                            b = bufs[s]
                            dve.wait_ge(m["product_made"], nth(i, s, LEVELS - 1, lv - 1))
                            if lv < LEVELS - 1:
                                dve.wait_ge(m["inv_made"], nth(i, s, LEVELS - 1, lv - 1))
                                dve.tensor_tensor(per(b["inv"]), per(b["inv"]), banks[s][3][:, :],
                                                  ALU.subtract).then_inc(m["inv_made"], 1)
                            dve.wait_ge(m["inv_t_made"], nth(i, s, LEVELS, lv - 1))
                            dve.tensor_tensor(per(b["inv_t"]), per(b["inv_t"]), banks[s][0][:, :],
                                              ALU.subtract).then_inc(m["inv_t_made"], 1)
                    for c in range(TT - 1):
                        for s in range(SLOTS):
                            b = bufs[s]
                            dve.wait_ge(m["state_made"], nth(i, s, TT - 1, c))
                            if c == 0:
                                dve.tensor_copy(b["st"][:, :], ps(s, 0)[:, c, :]).then_inc(m["state_added"], 1)
                            else:
                                dve.wait_ge(m["out_made"], nth(i, s, TT, c))
                                dve.scalar_tensor_tensor(
                                    out=b["st"][:, :], in0=b["st"][:, :], scalar=g.last_c[:, bass.ds(i + s, 1), c],
                                    in1=ps(s, 0)[:, c, :], op0=ALU.mult, op1=ALU.add).then_inc(m["state_added"], 1)


def windows(g, pool, act_buf):
    pad = max(POOL_WINDOWS)
    a = g.at("win_a", R + 20, [P, pad + S])
    b = g.at("win_b", R + 22, [P, pad + S])
    rate = g.at("rate", R + 33, [P, pad])
    step = g.sem("window_step")
    n = 0

    def did(ins):
        nonlocal n
        ins.then_inc(step, 1)
        n += 1
        pool.wait_ge(step, n)

    did(pool.memset(a[:, 0:pad], 0.0))
    did(pool.memset(b[:, 0:pad], 0.0))
    for k in range(pad):
        pool.memset(rate[:, k:k + 1], 1.0 / (k + 1))
    for q, win in enumerate(POOL_WINDOWS):
        x = act_buf[:, XA + q, :]
        out = g.pooled[:, q, :]
        did(pool.tensor_copy(a[:, pad:], x))
        src, dst, lag = a, b, 1
        while lag < win:
            did(pool.tensor_tensor(dst[:, pad:], src[:, pad:], src[:, pad - lag:pad - lag + S], ALU.add))
            src, dst, lag = dst, src, 2 * lag
        did(pool.tensor_scalar(out, src[:, pad:], 1.0 / win, None, ALU.mult))
        did(pool.tensor_tensor(out[:, 0:win], src[:, pad:pad + win], rate[:, 0:win], ALU.mult))
        did(pool.tensor_tensor(out, out, x, ALU.subtract))


def delta_norm(g, act_buf):
    nc = g.nc
    g.pooled = g.at("pooled", R + 24, [P, len(POOL_WINDOWS), S])
    g.yh = g.at("yh", R + 36, [P, HEADS, S], F32R)
    g.yl = g.at("yl", R + 44, [P, HEADS, S], F32R)
    sq = g.at("sq", R + 52, [P, 2, S])
    v = g.at("v", R + 54, [32, S])
    t = g.at("t", R + 55, [32, S])
    rr = g.at("rr", R + 56, [32, S])
    y = g.at("y", R + 57, [P, 3, S])
    squared, summed, root, spread, normed, gated, high, low = (g.sem(x) for x in (
        "squared", "summed", "root", "spread", "normed", "gated", "y_high", "y_low"))
    with ExitStack() as stack:
        rows_ps = g.banks(stack, 1, "rows")[0]
        wide = g.banks(stack, 4, "wide")
        with nc.Block() as block:
            @block.gpsimd
            def _(pool):
                windows(g, pool, act_buf)

            @block.scalar
            def _(act):
                for h in range(HEADS):
                    if h >= 2:
                        act.wait_ge(summed, h - 1)
                    act.activation(sq[:, h % 2, :], act_buf[:, Q + h, :], ACT.Square).then_inc(squared, 1)
                act.wait_ge(root, 2)
                act.activation(rr[:, :], t[:, :], ACT.Sqrt).then_inc(root, 1)
                for h in range(HEADS):
                    act.wait_ge(gated, h + 1)
                    act.activation(g.yh[:, h, :], y[:, h % 3, :], ACT.Copy).then_inc(high, 1)

            @block.tensor
            def _(pe):
                for h in range(HEADS):
                    pe.wait_ge(squared, h + 1)
                    pe.matmul(rows_ps[0:32, :], g.to_row[:, h, :], sq[:, h % 2, :], start=(h == 0),
                              stop=(h == HEADS - 1)).then_inc(summed, 1)
                pe.wait_ge(root, 7)
                for h in range(HEADS):
                    if h >= 4:
                        pe.wait_ge(normed, h - 3)
                    pe.matmul(wide[h % 4][:, :], g.head_mask[0:32, h:h + 1].to_broadcast([32, P]), rr[:, :],
                              start=True, stop=True).then_inc(spread, 1)

            @block.vector
            def _(dve):
                dve.wait_ge(summed, HEADS)
                dve.tensor_scalar(v[:, :], rows_ps[0:32, :], 1.0 / P, EPS, ALU.mult, ALU.add).then_inc(root, 1)
                dve.wait_ge(root, 1)
                dve.reciprocal(t[:, :], v[:, :]).then_inc(root, 1)
                dve.wait_ge(root, 3)
                refine_root(dve, rr[:, :], v[:, :], t[:, :], root, 3)
                for h in range(HEADS + 2):
                    if h < HEADS:
                        dve.wait_ge(spread, h + 1)
                        if h >= 3:
                            dve.wait_ge(low, h - 2)
                        dve.tensor_tensor(y[:, h % 3, :], act_buf[:, Q + h, :], wide[h % 4][:, :],
                                          ALU.mult).then_inc(normed, 1)
                    if 1 <= h <= HEADS:
                        dve.wait_ge(normed, h)
                        dve.scalar_tensor_tensor(out=y[:, (h - 1) % 3, :], in0=y[:, (h - 1) % 3, :],
                                                 scalar=g.col("dn_norm"), in1=act_buf[:, Z + h - 1, :], op0=ALU.mult,
                                                 op1=ALU.mult).then_inc(gated, 1)
                    if h >= 2:
                        dve.wait_ge(high, h - 1)
                        dve.tensor_tensor(g.yl[:, h - 2, :], y[:, (h - 2) % 3, :], g.yh[:, h - 2, :],
                                          ALU.subtract).then_inc(low, 1)


def pool_mix(g):
    nc = g.nc
    n_groups = len(POOL_WINDOWS)
    g.ph = g.at("ph", R + 12, [P, n_groups, S], F32R)
    g.pl = g.at("pl", R + 16, [P, n_groups, S], F32R)
    y = g.at("pool_y", R + 28, [P, n_groups, S])
    w = g.at("pool_w", R + 32, [P, n_groups, P])
    loaded, mixed, scaled, high, low = (g.sem(x) for x in ("pool_w_loaded", "mixed", "pool_scaled", "p_high", "p_low"))
    with ExitStack() as stack:
        banks = g.banks(stack, n_groups, "mixed")
        with nc.Block() as block:
            @block.sync
            def _(sp):
                sp.dma_start(w[:, :, :], g.io["pool_w"]).then_inc(loaded, 16)

            @block.vector
            def _(dve):
                for q in range(n_groups):
                    dve.wait_ge(mixed, q + 1)
                    dve.tensor_scalar(y[:, q, :], banks[q][:, :], g.col("pool_scale", q), None,
                                      ALU.mult).then_inc(scaled, 1)
                for q in range(n_groups):
                    dve.wait_ge(high, q + 1)
                    dve.tensor_tensor(g.pl[:, q, :], y[:, q, :], g.ph[:, q, :], ALU.subtract).then_inc(low, 1)

            @block.tensor
            def _(pe):
                pe.wait_ge(loaded, 16)
                for q in range(n_groups):
                    pe.matmul(banks[q][:, :], w[:, q, :], g.pooled[:, q, :], start=True, stop=True).then_inc(mixed, 1)

            @block.scalar
            def _(act):
                for q in range(n_groups):
                    act.wait_ge(scaled, q + 1)
                    act.activation(g.ph[:, q, :], y[:, q, :], ACT.Copy).then_inc(high, 1)


def merge(g, a, a_chunks, b, rows_from, bias=None):
    nc, base = g.nc, g.base
    g.mh = g.at("mh", R + 20, [P, DC, S], F32R)
    g.ml = g.at("ml", R + 28, [P, DC, S], F32R)
    gate = g.at("gate", R + 52, [P, 2, S])
    m = g.at("merged", R + 54, [P, 3, S])
    gated, first, second, both, high, low = (g.sem(x) for x in (
        "gated", "a_gated", "b_gated", "merged", "m_high", "m_low"))
    rows = g.sem("rows_loaded")
    with ExitStack() as stack:
        banks = g.banks(stack, 4, "merge")
        with nc.Block() as block:
            @block.sync
            def _(sp):
                sp.dma_start(g.h[:, :, :], rows_from.rearrange("(t p) d -> p t d", p=P)).then_inc(rows, 16)
                stream_load(g, sp, N_MERGE)
                sp.wait_ge(rows, 16)

            @block.tensor
            def _(pe):
                with steps(pe, 0, N_MERGE, 4) as i:
                    for j, (x, chunks) in enumerate(((None, DC), (a, a_chunks), (None, DC), (b, DC))):
                        pe.wait_ge(g.low_split, i + (base + j + 1))
                        if j % 2 == 0:
                            pe.wait_ge(gated, i // 2 + (j // 2 + 1))
                        else:
                            pe.wait_ge(first if j == 1 else second, i // 4 + 1)
                        mm_columns(g, pe, base + j, banks[j][:, :], chunks, x).then_inc(g.tile_used, 1)

            @block.scalar
            def _(act):
                act.sem_inc(gated, 2)
                with steps(act, 0, N_MERGE, 4) as i:
                    for j in range(4):
                        split_high(g, act, i, j + 2)
                        if j % 2 == 0:
                            tile_done(g, act, i, j)
                            act.wait_ge(first if j == 0 else second, i // 4 + 1)
                            b = 0.0
                            if bias:
                                b = g.cols[:, bass.ds(i // 4 + (COLS[bias][0] + DC * (j // 2)), 1)]
                            act.activation(gate[:, j // 2, :], banks[j][:, :], ACT.Sigmoid, bias=b).then_inc(gated, 1)
                    act.wait_ge(both, i // 4 + 1)
                    act.activation(g.mh[:, i // 4, :], m[:, 2, :], ACT.Copy).then_inc(high, 1)

            @block.vector
            def _(dve):
                dve.sem_inc(first, 1)
                dve.sem_inc(second, 1)
                with steps(dve, 0, N_MERGE, 4) as i:
                    for j in range(4):
                        split_low(g, dve, i, j + 2)
                        if j % 2:
                            dve.wait_ge(gated, i // 2 + (j // 2 + 3))
                            tile_done(g, dve, i, j)
                            dve.tensor_tensor(m[:, j // 2, :], gate[:, j // 2, :], banks[j][:, :],
                                              ALU.mult).then_inc(first if j == 1 else second, 1)
                    dve.wait_ge(first, i // 4 + 2)
                    dve.wait_ge(second, i // 4 + 2)
                    dve.tensor_tensor(m[:, 2, :], m[:, 0, :], m[:, 1, :], ALU.add).then_inc(both, 1)
                    dve.wait_ge(high, i // 4 + 1)
                    dve.tensor_tensor(g.ml[:, i // 4, :], m[:, 2, :], g.mh[:, i // 4, :],
                                      ALU.subtract).then_inc(low, 1)
    g.base += N_MERGE


def mm_rows(pe, hi, lo, bank, xh, xl, half, start, stop):
    w = slice(half * 512, half * 512 + 512)
    pe.matmul(bank, xh, hi[:, w], start=start, stop=False, skip_group_check=True)
    pe.matmul(bank, xh, lo[:, w], start=False, stop=False, skip_group_check=True)
    return pe.matmul(bank, xl, hi[:, w], start=False, stop=stop, skip_group_check=True)


def mix_out(g, stack):
    nc, base = g.nc, g.base
    banks = g.banks(stack, 2 * TT, "out")
    last = base + N_OUT == g.total
    done = g.sem("out_done")
    added = g.sem("rows_added")
    with nc.Block() as block:
        @block.sync
        def _(sp):
            stream_load(g, sp, N_OUT)

        @block.tensor
        def _(pe):
            for c in range(N_OUT):
                t = base + c
                pe.wait_ge(g.low_split, t + 1)
                for q in range(2 * TT):
                    w = slice(q // 2 * P, q // 2 * P + P)
                    ins = mm_rows(pe, g.high[t % 2], g.low[t % 2], banks[q][:, :], g.mh[:, c, w], g.ml[:, c, w],
                                  q % 2, c == 0, c == N_OUT - 1)
                    if c == N_OUT - 1:
                        ins.then_inc(done, 1)
                if c < N_OUT - 1:
                    ins.then_inc(g.tile_used, 1)
            pe.wait_ge(done, 2 * TT)
            pe.sem_inc(g.tile_used, 1)

        @block.scalar
        def _(act):
            for c in range(N_OUT - 2 * last):
                split_high(g, act, 0, c + 2)

        @block.vector
        def _(dve):
            for c in range(N_OUT - 2 * last):
                split_low(g, dve, 0, c + 2)
            if not last:
                for q in range(2 * TT):
                    dve.wait_ge(done, q + 1)
                    rows = g.h[:, q // 2, q % 2 * 512:q % 2 * 512 + 512]
                    dve.tensor_tensor(rows, rows, banks[q][:, :], ALU.add).then_inc(added, 1)
    g.base += N_OUT
    return banks


def past(eng, sem, count, passed):
    eng.wait_ge(sem, count)
    eng.sem_inc(passed, 1)


def top16(dve, n, values, work, best, at, picked, passed, count, meanwhile=None):
    for r in range(n):
        dve.max(best[:, r, 0:8], values(r)).then_inc(picked, 1)
    if meanwhile:
        meanwhile()
    past(dve, picked, count + n, passed)
    for r in range(n):
        dve.match_replace(work(r), best[:, r, 0:8], values(r), -3.0e38).then_inc(picked, 1)
    for r in range(n):
        dve.max_index(at[:, r, 0:8], best[:, r, 0:8], values(r)).then_inc(picked, 1)
    past(dve, picked, count + 2 * n, passed)
    for r in range(n):
        dve.max(best[:, r, 8:16], work(r)).then_inc(picked, 1)
    past(dve, picked, count + 4 * n, passed)
    for r in range(n):
        dve.max_index(at[:, r, 8:16], best[:, r, 8:16], work(r)).then_inc(picked, 1)
    return count + 5 * n


def peer_scores(g):
    nc, base = g.nc, g.base
    n_halves = 2 * HEADS
    keys = g.at("keys", R, [P, n_halves, N_KEYS])
    query = g.at("query", R + 4, [P, 2, S])
    score = g.at("score", R + 6, [P, 2, TT, N_KEYS])
    work = g.at("work", R + 8, [P, TT, N_KEYS])
    g.vals = g.at("vals", R + 10, [P, TT, n_halves, TOPK])
    g.keyno = g.at("keyno", R + 12, [P, TT, n_halves, TOPK])
    best = g.at("best", R + 14, [P, 2, TT, TOPK])
    where = g.at("where", R + 15, [P, 2, TT, TOPK], U32)
    per_tile = 5 * TT
    FIRST = 3
    passed, pool_passed = g.sem("passed"), g.sem("pool_passed")
    keys_loaded, q_read, scored, s_read, picked, kept = (g.sem(x) for x in (
        "keys_loaded", "query_read", "scored", "score_read", "picked", "kept"))
    with ExitStack() as stack:
        qb = g.banks(stack, 4, "query")
        sb = g.banks(stack, 4, "score")
        with nc.Block() as block:
            @block.sync
            def _(sp):
                sp.dma_start(keys[:, :, :], g.io["keys"]).then_inc(keys_loaded, 16)
                stream_load(g, sp, N_QUERY)

            @block.tensor
            def _(pe):
                def score_tile(i, j):
                    pe.wait_ge(q_read, i + (j + 1))
                    pe.wait_ge(s_read, i + (j + 1))
                    for t in range(TT):
                        last = pe.matmul(sb[j][:, t * P:t * P + P], query[:, j % 2, t * P:t * P + P],
                                         keys[:, bass.ds(i + j, 1), :].rearrange("p o k -> p (o k)"),
                                         start=True, stop=True)
                    last.then_inc(scored, 1)

                pe.wait_ge(keys_loaded, 16)
                with steps(pe, 0, N_QUERY, 4) as i:
                    for j in range(4):
                        pe.wait_ge(g.low_split, i + (base + j + 1))
                        mm_columns(g, pe, base + j, qb[j][:, :], stop=FIRST)
                        if j:
                            score_tile(i, j - 1)
                        mm_columns(g, pe, base + j, qb[j][:, :], start=FIRST).then_inc(g.tile_used, 1)
                    score_tile(i, 3)

            @block.scalar
            def _(act):
                act.sem_inc(s_read, 4)
                with steps(act, 0, N_QUERY, 4) as i:
                    for j in range(4):
                        split_high(g, act, i, j + 2)
                        tile_done(g, act, i, j)
                        act.wait_ge(scored, i + (j + 1))
                        act.activation(query[:, j % 2, :], qb[j][:, :], ACT.Copy).then_inc(q_read, 1)

            @block.gpsimd
            def _(pool):
                pool.sem_inc(kept, 3)
                with steps(pool, 0, N_QUERY, 4) as i:
                    for j in range(4):
                        past(pool, picked, per_tile * i + per_tile * (j + 1), pool_passed)
                        for to, src in ((g.vals, best), (g.keyno, where)):
                            pool.tensor_copy(to[:, :, bass.ds(i + j, 1), :].rearrange("p t o k -> p t (o k)"),
                                             src[:, j % 2, :, :]).then_inc(kept, 1)

            @block.vector
            def _(dve):
                dve.sem_inc(scored, 2)
                with steps(dve, 0, N_QUERY, 4) as i:
                    for j in range(4):
                        s = j % 2
                        dve.wait_ge(scored, i + (j + 3))
                        dve.wait_ge(kept, 2 * i + (2 * j + 1))
                        dve.tensor_copy(score[:, s, :, :].rearrange("p t k -> p (t k)"), sb[j][:, :])\
                           .then_inc(s_read, 1)
                        past(dve, s_read, i + (j + 5), passed)
                        top16(dve, TT, lambda r: score[:, s, r, :], lambda r: work[:, r, :], best[:, s, :, :],
                              where[:, s, :, :], picked, passed, per_tile * i + per_tile * j,
                              meanwhile=lambda: split_low(g, dve, i, j + 2))
    g.base += N_QUERY


QUAD = 4
AHEAD = 4 * QUAD


def peer_pick(g):
    nc, base = g.nc, g.base
    g.early = g.at("early", R + 29, [P, EARLY, S])
    hk = HEADS * TOPK
    g.first = g.at("first", R + 17, [P, S])
    g.gate = g.at("gate", R + 18, [P, S])
    g.second = g.at("second", R + 19, [P, S + AHEAD])
    g.count = g.at("count", R + 20.25, [P, N_KEYS])
    cand = g.at("cand", R + 21, [P, HEADS, TOPK, TOPK])
    work = g.at("work", R + 25, [P, HEADS, TOPK, TOPK])
    hot = g.at("hot", R, [P, 2, HEADS, TOPK, TOPK])
    best = g.at("best", R + 14, [P, HEADS, TOPK])
    where = g.at("where", R + 14.25, [P, HEADS, TOPK], U32)
    part = g.at("part", R + 14.5, [P, 2, hk], U32)
    partf = g.at("partf", R + 15, [P, 2, hk])
    res = g.at("res", R + 15.5, [P, 3, hk])
    total = g.at("total", R + 16.25, [P, 2, HEADS])
    passed = g.sem("passed")
    ready, counted, picked, step, grown, turned, kept, hot_made = (g.sem(x) for x in (
        "summed", "counted", "picked", "pick_step", "exp_done", "turned", "kept", "hot_made"))
    per_pick = 5 * HEADS

    def wide(v, axis):
        return v.unsqueeze(axis).to_broadcast([P, HEADS, TOPK, TOPK])

    def heads(v):
        return v.rearrange("p (h k) -> p h k", k=TOPK)

    with ExitStack() as stack:
        bank = g.banks(stack, 1, "turned")[0]
        down = g.banks(stack, 4, "down")
        activated = g.sem("activated")
        PER = EARLY // TT
        with nc.Block() as block:
            @block.gpsimd
            def _(pool):
                pool.memset(g.second[:, S:], 0.0)
                pool.iota(g.count[:, :], pattern=[[1, N_KEYS]], base=0, channel_multiplier=0,
                          allow_small_or_imprecise_dtypes=True).then_inc(counted, 1)
                with steps(pool, 0, EARLY, 2 * PER) as i:
                    for j in range(2 * PER):
                        split_low(g, pool, i, j + 2)

            @block.sync
            def _(sp):
                stream_load(g, sp, EARLY)

            @block.scalar
            def _(act):
                act.sem_inc(activated, 4)
                with steps(act, 0, EARLY, 2 * PER) as i:
                    t = i // PER
                    for j in range(2 * PER):
                        split_high(g, act, i, j + 2)
                        act.activation(g.early[:, i + j, :], down[j % 4][:, :], ACT.Gelu).then_inc(activated, 1)
                        if j % PER == PER - 2:
                            act.wait_ge(step, 10 * t + (10 * (j // PER) + 6))
                            act.activation(res[:, 2, :], res[:, 2, :], ACT.Exp).then_inc(grown, 1)

            @block.tensor
            def _(pe):
                with steps(pe, 0, EARLY, 2 * PER) as i:
                    t = i // PER
                    for j in range(2 * PER):
                        pe.wait_ge(g.low_split, i + (base + j + 1))
                        pe.wait_ge(activated, i + (j + 1))
                        mm_columns(g, pe, base + j, down[j % 4][:, :]).then_inc(g.tile_used, 1)
                        if j % PER == PER - 1:
                            pe.wait_ge(step, 10 * t + (10 * (j // PER) + 10))
                            for r in range(3):
                                last = pe.transpose(bank[:, r * P:r * P + P], res[:, r, :], g.ident[:, :])
                            last.then_inc(turned, 1)

            @block.vector
            def _(dve):
                dve.wait_ge(counted, 1)
                dve.sem_inc(kept, 1)
                with steps(dve, 0, TT, 1) as t:
                    def halves(buf, half):
                        return buf[:, bass.ds(t, 1), half::2, :].rearrange("p o h k -> p (o h) k")

                    dve.wait_ge(kept, 3 * t + 1)
                    dve.tensor_tensor(cand[:, :, :, :], wide(halves(g.vals, 0), 3), wide(halves(g.vals, 1), 2),
                                      ALU.add).then_inc(ready, 1)
                    past(dve, ready, t + 1, passed)
                    top16(dve, HEADS, lambda h: cand[:, h, :, :].rearrange("p a b -> p (a b)"),
                          lambda h: work[:, h, :, :].rearrange("p a b -> p (a b)"), best, where, picked,
                          passed, per_pick * t)
                    dve.wait_ge(picked, per_pick * t + per_pick)
                    flat = where[:, :, :].rearrange("p h k -> p (h k)")
                    dve.tensor_scalar(part[:, 0, :], flat, 4, None, ALU.logical_shift_right).then_inc(step, 1)
                    dve.tensor_scalar(part[:, 1, :], flat, TOPK - 1, None, ALU.bitwise_and).then_inc(step, 1)
                    dve.wait_ge(step, 10 * t + 2)
                    dve.tensor_copy(partf[:, :, :], part[:, :, :]).then_inc(step, 1)
                    dve.wait_ge(step, 10 * t + 3)
                    for k in range(2):
                        dve.tensor_tensor(hot[:, k, :, :, :], wide(heads(partf[:, k, :]), 3),
                                          g.count[:, 0:TOPK].unsqueeze(1).unsqueeze(1)
                                          .to_broadcast([P, HEADS, TOPK, TOPK]), ALU.is_equal).then_inc(step, 1)
                    dve.tensor_tensor(heads(res[:, 2, :]), best[:, :, :],
                                      best[:, :, 0:1].to_broadcast([P, HEADS, TOPK]), ALU.subtract).then_inc(step, 1)
                    dve.wait_ge(step, 10 * t + 6)
                    for k in range(2):
                        dve.tensor_tensor(hot[:, k, :, :, :], hot[:, k, :, :, :], wide(halves(g.keyno, k), 2),
                                          ALU.mult).then_inc(hot_made, 1)
                    dve.wait_ge(grown, t + 1)
                    dve.tensor_reduce(total[:, 0, :], heads(res[:, 2, :]), AX.X, ALU.add).then_inc(step, 1)
                    for k in range(2):
                        dve.wait_ge(hot_made, 2 * t + (k + 1))
                        ins = dve.tensor_reduce(heads(res[:, k, :]), hot[:, k, :, :, :], AX.X, ALU.add)
                    ins.then_inc(step, 1)
                    dve.wait_ge(step, 10 * t + 8)
                    dve.reciprocal(total[:, 1, :], total[:, 0, :]).then_inc(step, 1)
                    dve.wait_ge(step, 10 * t + 9)
                    dve.tensor_tensor(heads(res[:, 2, :]), heads(res[:, 2, :]),
                                      total[:, 1, :].unsqueeze(2).to_broadcast([P, HEADS, TOPK]),
                                      ALU.mult).then_inc(step, 1)
                    dve.wait_ge(turned, t + 1)
                    for r, out in enumerate((g.first, g.second, g.gate)):
                        dve.tensor_copy(out[:, bass.ds(t * P, P)], bank[:, r * P:r * P + P]).then_inc(kept, 1)
    g.base += EARLY


GROUP = 32


def peer_gates(g):
    nc = g.nc
    BY_POOL = 2
    n_groups = S // GROUP
    g.gates = nc.dram_tensor("gates", [n_groups, P, N_KEYS, GROUP], F32, kind="Internal").ap()
    hot2 = g.at("hot2", R + 21, [P, 4, QUAD, N_KEYS])
    hot1 = g.at("hot1", R + 25, [P, 4, QUAD, N_KEYS])
    now = g.at("now", R + 16.5, [P, 4 * QUAD])
    now_read, passed = g.sem("now_read"), g.sem("passed")
    stage = [g.at(f"stage{s}", R + 8 * s, [P, N_KEYS, GROUP]) for s in range(2)]
    second_made, first_made, third_made, product, read, apart, act_passed = (g.sem(x) for x in (
        "second_hot", "first_hot", "second_hot_by_act", "product", "read", "apart", "act_passed"))
    stored = [g.sem(f"stored{s}") for s in range(2)]
    quads = GROUP // QUAD
    with ExitStack() as stack:
        banks = g.banks(stack, 4, "gates")

        with nc.Block() as block:
            @block.gpsimd
            def _(pool):
                pool.sem_inc(product, 4)
                pool.sem_inc(second_made, 1)
                with steps(pool, 0, S // QUAD, 4) as i:
                    pool.wait_ge(second_made, i + 1)
                    pool.tensor_copy(now[:, :], g.second[:, bass.ds(i * QUAD, 4 * QUAD)]).then_inc(now_read, 1)
                    pool.wait_ge(now_read, i // 4 + 1)
                    for j in range(4):
                        pool.wait_ge(product, i + (j + 1))
                        pool.sem_inc(passed, 1)
                        for k in range(BY_POOL):
                            n = j * QUAD + k
                            ins = pool.tensor_scalar(hot2[:, j, k, :], g.count[:, :], now[:, n:n + 1], None,
                                                     ALU.is_equal)
                        ins.then_inc(second_made, 1)

            @block.vector
            def _(dve):
                with steps(dve, 0, S // QUAD, 4) as i:
                    for j in range(4):
                        dve.wait_ge(product, i + (j + 1))
                        for k in range(QUAD):
                            t = i * QUAD + (j * QUAD + k)
                            ins = dve.tensor_scalar(hot1[:, j, k, :], g.count[:, :], g.first[:, bass.ds(t, 1)],
                                                    g.gate[:, bass.ds(t, 1)], ALU.is_equal, ALU.mult)
                        for k in range(BY_POOL, QUAD - 1):
                            t = i * QUAD + (j * QUAD + k)
                            ins = dve.tensor_scalar(hot2[:, j, k, :], g.count[:, :], g.second[:, bass.ds(t, 1)],
                                                    None, ALU.is_equal)
                        ins.then_inc(first_made, 1)

            @block.tensor
            def _(pe):
                with steps(pe, 0, S // QUAD, 4) as i:
                    for j in range(4):
                        pe.wait_ge(second_made, i + (j + 2))
                        pe.wait_ge(first_made, i + (j + 1))
                        pe.wait_ge(third_made, i + (j + 1))
                        pe.wait_ge(read, i + (j + 1))
                        for k in range(QUAD):
                            ins = pe.matmul(banks[j][:, k * P:k * P + P], hot2[:, j, k, :], hot1[:, j, k, :],
                                            start=True, stop=True)
                        ins.then_inc(product, 1)

            @block.scalar
            def _(act):
                def distance(n, j):
                    t = n * QUAD + (j * QUAD + QUAD - 1)
                    act.activation(hot2[:, j % 4, QUAD - 1, :], g.count[:, :], ACT.Abs, scale=-1.0,
                                   bias=g.second[:, bass.ds(t, 1)]).then_inc(apart, 1)

                def last_row(n, j):
                    act.wait_ge(apart, n + (j + 1))
                    hot = hot2[:, j % 4, QUAD - 1, :]
                    act.activation(hot, hot, ACT.Relu, scale=-1.0, bias=1.0).then_inc(third_made, 1)

                act.sem_inc(read, 4)
                for s in range(2):
                    act.sem_inc(stored[s], 16)
                for j in range(4):
                    distance(0, j)
                    last_row(0, j)
                with steps(act, 0, n_groups, 2) as i:
                    for s in range(2):
                        act.wait_ge(stored[s], 8 * i + 16)
                        with steps(act, 0, quads, 4) as q:
                            n = i * quads + q
                            for j in range(4):
                                past(act, product, n + (s * quads + j + 5), act_passed)
                                distance(n, s * quads + j + 4)
                                act.activation(
                                    stage[s][:, :, bass.ds(q * QUAD + j * QUAD, QUAD)],
                                    banks[j][:, :].rearrange("p (t e) -> p e t", e=N_KEYS), ACT.Copy).then_inc(read, 1)
                                last_row(n, s * quads + j + 4)

            @block.sync
            def _(sp):
                with steps(sp, 0, n_groups, 2) as i:
                    for s in range(2):
                        sp.wait_ge(read, i * quads + ((s + 1) * quads + 4))
                        sp.dma_start(g.gates[i + s], stage[s][:, :, :]).then_inc(stored[s], 16)
                for s in range(2):
                    sp.wait_ge(stored[s], 16 * n_groups // 2 + 16)


def up_free(n, n_up, n_banks):
    before = n - n_banks if n >= n_banks else max(m for m in range(n_up) if m % n_banks == n) - n_up
    return n_banks + before + 1


def mm_up(g, pe, out, wh, wl, pair, q):
    rows = slice(q // 2 * P, q // 2 * P + P)
    for k in range(2):
        e = 2 * pair + k
        last = mm_rows(pe, g.high[e], g.low[e], out, wh[:, e, rows], wl[:, e, rows], q % 2, k == 0, k == 1)
    return last


def four_slots(g):
    more = g.at("split2", R + 4, [P, 2, 2, TILE], F32R)
    g.high += [more[:, s, 0, :] for s in range(2)]
    g.low += [more[:, s, 1, :] for s in range(2)]


def two_slots(g):
    del g.high[2:], g.low[2:]


def peer_early(g):
    nc, base = g.nc, g.base
    SL, B, UP = 4, 4, 6
    four_slots(g)
    gate = g.at("gate", R, [P, S // GROUP, B, GROUP])
    w = g.at("weight", R + 14, [P, 2, S])
    wh = g.at("weight_high", R + 16, [P, B, S], F32R)
    wl = g.at("weight_low", R + 20, [P, B, S], F32R)
    gates_loaded, weighed, w_high, w_low, up_done, added = (g.sem(x) for x in (
        "gates_loaded", "weighed", "w_high", "w_low", "up_done", "added"))
    halves = 2 * TT
    with ExitStack() as stack:
        up = g.banks(stack, UP, "up")
        with nc.Block() as block:
            @block.sync
            def _(sp):
                with steps(sp, 0, EARLY, B) as b:
                    sp.wait_ge(weighed, b + 1)
                    sp.dma_start(gate[:, :, :, :], g.gates[:, :, bass.ds(b, B), :]
                                 .rearrange("n p e t -> p n e t")).then_inc(gates_loaded, 16)
                    for j in range(B):
                        sp.wait_ge(g.high_split, b + (base + j + 1))
                        sp.wait_ge(g.low_split, b + (base + j + 1))
                        sp.dma_start(g.raw[:, j, :], g.io["stream"][b + (base + RAW + j)]).then_inc(g.raw_loaded[j], 16)

            @block.tensor
            def _(pe):
                with steps(pe, 0, EARLY, B) as b:
                    for pair in range(2):
                        pe.wait_ge(g.low_split, b + (base + 2 * pair + 2))
                        pe.wait_ge(w_low, b + (2 * pair + 2))
                        for q in range(halves):
                            n = halves * pair + q
                            pe.wait_ge(added, 4 * b + up_free(n, 2 * halves, UP))
                            last = mm_up(g, pe, up[n % UP][:, :], wh, wl, pair, q)
                            if q < halves - 1:
                                last.then_inc(up_done, 1)
                            else:
                                last.then_inc(g.tile_used, 2)

            @block.scalar
            def _(act):
                def high(b, j):
                    act.wait_ge(weighed, b + (j + 2))
                    act.activation(wh[:, j, :], w[:, j % 2, :], ACT.Copy).then_inc(w_high, 1)

                for j in range(B):
                    if j == 0:
                        split_high(g, act, 0, 2, SL)
                        split_high(g, act, 0, 3, SL)
                    high(0, j)
                with steps(act, 0, EARLY - B, B) as b:
                    for pair in range(2):
                        for t in range(2):
                            split_high(g, act, b, B + 2 * pair + t, SL)
                        for j in range(2):
                            high(b + B, 2 * pair + j)
                for t in range(2):
                    split_high(g, act, EARLY - B, B + t, SL)

            @block.vector
            def _(dve):
                def weights(b, j):
                    if not (isinstance(b, int) and j < 2):
                        dve.wait_ge(w_low, b + (j - 1))
                    dve.tensor_tensor(w[:, j % 2, :].rearrange("p (n t) -> p n t", t=GROUP),
                                      g.early[:, bass.ds(b + j, 1), :].rearrange("p o (n t) -> p (o n) t", t=GROUP),
                                      gate[:, :, j, :], ALU.mult).then_inc(weighed, 1)
                    dve.wait_ge(w_high, b + (j + 1))
                    dve.tensor_tensor(wl[:, j, :], w[:, j % 2, :], wh[:, j, :], ALU.subtract).then_inc(w_low, 1)

                def add(b, pair):
                    for q in range(halves):
                        n = halves * pair + q
                        if q < halves - 1:
                            dve.wait_ge(up_done, b // B * (2 * (halves - 1)) + (pair * (halves - 1) + q + 1))
                        else:
                            tile_done(g, dve, b, 2 * pair + 1)
                        rows = g.h[:, q // 2, q % 2 * 512:q % 2 * 512 + 512]
                        dve.tensor_tensor(rows, rows, up[n % UP][:, :], ALU.add).then_inc(added, 1)

                dve.sem_inc(added, UP)
                dve.sem_inc(weighed, 1)
                split_low(g, dve, 0, 2, SL)
                split_low(g, dve, 0, 3, SL)
                dve.wait_ge(gates_loaded, 16)
                for j in range(B):
                    weights(0, j)
                with steps(dve, 0, EARLY - B, B) as b:
                    for pair in range(2):
                        add(b, pair)
                        for t in range(2):
                            split_low(g, dve, b, B + 2 * pair + t, SL)
                        if pair == 0:
                            dve.wait_ge(gates_loaded, b // B * 16 + 32)
                        for j in range(2):
                            weights(b + B, 2 * pair + j)
                add(EARLY - B, 0)
                for t in range(2):
                    split_low(g, dve, EARLY - B, B + t, SL)
                add(EARLY - B, 1)
    two_slots(g)
    g.base += EARLY


def peer_experts(g):
    nc, base = g.nc, g.base
    SL, B, UP = 4, 4, 6
    n_blocks = N_KEYS - EARLY
    four_slots(g)
    halves = 2 * TT
    gate = g.at("gate", R, [P, S // GROUP, B, GROUP])
    gelu = g.at("gelu", R + 12, [P, 2, S])
    w = g.at("weight", R + 14, [P, 2, S])
    wh = g.at("weight_high", R + 16, [P, B, S], F32R)
    wl = g.at("weight_low", R + 20, [P, B, S], F32R)
    gates_loaded, activated, weighed, w_high, w_low, up_done, added = (g.sem(x) for x in (
        "gates_loaded", "activated", "weighed", "w_high", "w_low", "up_done", "added"))
    with ExitStack() as stack:
        down = g.banks(stack, 2, "down")
        up = g.banks(stack, UP, "up")
        with nc.Block() as block:
            @block.sync
            def _(sp):
                with steps(sp, 0, n_blocks, B) as b:
                    i = 2 * b
                    for j in range(2 * B):
                        if j == 0:
                            sp.wait_ge(weighed, b + 2)
                            sp.dma_start(gate[:, :, :, :], g.gates[:, :, bass.ds(b + EARLY, B), :]
                                         .rearrange("n p e t -> p n e t")).then_inc(gates_loaded, 16)
                        sp.wait_ge(g.high_split, i + (base + j + 1))
                        sp.wait_ge(g.low_split, i + (base + j + 1))
                        sp.dma_start(g.raw[:, j % RAW, :], g.io["stream"][i + (base + RAW + j)])\
                          .then_inc(g.raw_loaded[j % RAW], 16)

            @block.tensor
            def _(pe):
                with steps(pe, 0, n_blocks, B) as b:
                    i = 2 * b
                    for j in range(B):
                        pe.wait_ge(g.low_split, i + (base + j + 1))
                        pe.wait_ge(activated, b + (j + 1))
                        hi, lo = g.high[j], g.low[j]
                        for c in range(DC):
                            k = slice(c * P, c * P + P)
                            pe.matmul(down[j % 2][:, :], hi[:, k], g.xh[:, c, :], start=(c == 0), stop=False)
                            pe.matmul(down[j % 2][:, :], hi[:, k], g.xl[:, c, :], start=False, stop=False)
                            last = pe.matmul(down[j % 2][:, :], lo[:, k], g.xh[:, c, :], start=False,
                                             stop=(c == DC - 1))
                        last.then_inc(g.tile_used, 1)
                    for pair in range(2):
                        pe.wait_ge(g.low_split, i + (base + B + 2 * pair + 2))
                        pe.wait_ge(w_low, b + (2 * pair + 2))
                        for q in range(halves):
                            n = halves * pair + q
                            pe.wait_ge(added, 4 * b + up_free(n, 2 * halves, UP))
                            last = mm_up(g, pe, up[n % UP][:, :], wh, wl, pair, q)
                            if q < halves - 1:
                                last.then_inc(up_done, 1)
                            else:
                                last.then_inc(g.tile_used, 2)

            @block.scalar
            def _(act):
                act.sem_inc(activated, 2)
                with steps(act, 0, n_blocks, B) as b:
                    i = 2 * b
                    for j in range(B):
                        for t in ((2, 3), (4,), (5,), ())[j]:
                            split_high(g, act, i, t, SL)
                        tile_done(g, act, i, j)
                        act.wait_ge(weighed, b + (j + 1))
                        act.activation(gelu[:, j % 2, :], down[j % 2][:, :], ACT.Gelu).then_inc(activated, 1)
                        act.wait_ge(weighed, b + (j + 3))
                        act.wait_ge(g.tile_used, i + (base + 2))
                        act.activation(wh[:, j, :], w[:, j % 2, :], ACT.Copy).then_inc(w_high, 1)
                    for t in (6, 7, 8, 9):
                        split_high(g, act, i, t, SL)

            @block.vector
            def _(dve):
                dve.sem_inc(weighed, 2)
                dve.sem_inc(added, UP)
                with steps(dve, 0, n_blocks, B) as b:
                    i = 2 * b
                    dve.wait_ge(gates_loaded, b // B * 16 + 16)
                    for j in range(B):
                        for t in ((2, 3), (4,), (5,), ())[j]:
                            split_low(g, dve, i, t, SL)
                        dve.wait_ge(activated, b + (j + 3))
                        dve.tensor_tensor(w[:, j % 2, :].rearrange("p (n t) -> p n t", t=GROUP),
                                          gelu[:, j % 2, :].rearrange("p (n t) -> p n t", t=GROUP),
                                          gate[:, :, j, :], ALU.mult).then_inc(weighed, 1)
                        dve.wait_ge(w_high, b + (j + 1))
                        dve.tensor_tensor(wl[:, j, :], w[:, j % 2, :], wh[:, j, :], ALU.subtract).then_inc(w_low, 1)
                    for pair in range(2):
                        for t in ((6, 7), (8, 9))[pair]:
                            split_low(g, dve, i, t, SL)
                        for q in range(halves):
                            n = halves * pair + q
                            if q < halves - 1:
                                dve.wait_ge(up_done, b // B * (2 * (halves - 1)) + (pair * (halves - 1) + q + 1))
                            else:
                                tile_done(g, dve, i, B + 2 * pair + 1)
                            rows = g.h[:, q // 2, q % 2 * 512:q % 2 * 512 + 512]
                            dve.tensor_tensor(rows, rows, up[n % UP][:, :], ALU.add).then_inc(added, 1)
    two_slots(g)
    g.base += 2 * n_blocks


SZ, SX, SB_, SC = 0, 8, 16, 18
AQ, AK, AV, AZ = 0, 8, 20, 28
SSD_GROUPS = 2


def ssd_rows(g, rows_ps):
    nc = g.nc
    nh = SSD_HEADS
    g.rows = g.at("ssd_rows", R + 52, [64, S])
    v = g.at("v", R + 53, [nh, S])
    t = g.at("t", R + 54, [nh, S])
    dt = g.at("dt", R + 55, [nh, S])
    da = g.at("da", R + 56, [nh, S])
    neg_a = g.at("neg_a", R + 57, [nh, 1])
    g.sum_c = g.at("ssd_sum", R + 57.25, [P, nh, TT])
    g.dt_c = g.at("ssd_dt", R + 57.5, [P, nh, TT])
    g.left_c = g.at("ssd_left", R + 57.75, [P, nh, TT])
    g.last_c = g.at("ssd_last", R + 58, [P, nh, TT])
    soft, turned, tail, spread, rate = (g.sem(x) for x in ("softplus", "turned", "scalars", "last_spread", "rate"))
    with ExitStack() as stack:
        cols_ps = g.banks(stack, 1, "cols")[0]
        last_ps = g.banks(stack, 1, "last")[0]
        with nc.Block() as block:
            @block.scalar
            def _(act):
                act.activation(neg_a[:, :], g.heads[:, 2:3], ACT.Exp).then_inc(rate, 1)
                act.wait_ge(soft, 2)
                act.activation(t[:, :], v[:, :], ACT.Abs).then_inc(soft, 1)
                act.wait_ge(soft, 3)
                act.activation(t[:, :], t[:, :], ACT.Exp, scale=-1.0).then_inc(soft, 1)
                act.wait_ge(soft, 4)
                act.activation(t[:, :], t[:, :], ACT.Ln, bias=1.0).then_inc(soft, 1)
                act.wait_ge(spread, 1)
                act.activation(g.last_c[:, :, :], last_ps[:, 0:TT * nh].rearrange("p (h c) -> p h c", c=TT),
                               ACT.Exp).then_inc(tail, 1)
                act.wait_ge(tail, 4)
                act.activation(g.left_c[:, :, :], g.left_c[:, :, :], ACT.Exp).then_inc(tail, 1)

            @block.tensor
            def _(pe):
                pe.wait_ge(soft, 12)
                for c in range(TT):
                    pe.transpose(cols_ps[:, c * P:c * P + 64], g.rows[:, c * P:c * P + P], g.ident[0:64, 0:64])\
                      .then_inc(turned, 1)
                pe.wait_ge(tail, 2)
                pe.matmul(last_ps[:, 0:TT * nh], g.last_row[:, :], g.sum_c[:, :, :].rearrange("p h c -> p (h c)"),
                          start=True, stop=True).then_inc(spread, 1)

            @block.vector
            def _(dve):
                dve.memset(g.rows[:, :], 0.0).then_inc(soft, 1)
                dve.tensor_scalar(v[:, :], rows_ps[0:nh, :], g.heads[:, 3:4], None, ALU.add).then_inc(soft, 1)
                dve.wait_ge(soft, 5)
                dve.scalar_tensor_tensor(out=dt[:, :], in0=v[:, :], scalar=0.0, in1=t[:, :], op0=ALU.max,
                                         op1=ALU.add).then_inc(soft, 1)
                dve.wait_ge(soft, 6)
                dve.wait_ge(rate, 1)
                dve.tensor_scalar(da[:, :], dt[:, :], neg_a[:, :], -1.0, ALU.mult, ALU.mult).then_inc(soft, 1)
                dve.tensor_copy(g.rows[32:32 + nh, :], dt[:, :]).then_inc(soft, 1)
                dve.wait_ge(soft, 8)
                for c in range(TT):
                    w = slice(c * P, c * P + P)
                    dve.tensor_tensor_scan(out=g.rows[0:nh, w], data0=g.ones[0:nh, :], data1=da[:, w], initial=0.0,
                                           op0=ALU.mult, op1=ALU.add).then_inc(soft, 1)
                dve.wait_ge(turned, TT)
                cols = cols_ps[:, :].rearrange("p (c n) -> p n c", n=P)
                dve.tensor_copy(g.sum_c[:, :, :], cols[:, 0:nh, :]).then_inc(tail, 1)
                dve.tensor_copy(g.dt_c[:, :, :], cols[:, 32:32 + nh, :]).then_inc(tail, 1)
                dve.wait_ge(tail, 3)
                dve.tensor_tensor(g.left_c[:, :, :], last_ps[:, 0:TT * nh].rearrange("p (h c) -> p h c", c=TT),
                                  g.sum_c[:, :, :], ALU.subtract).then_inc(tail, 1)
                dve.wait_ge(tail, 5)
                dve.tensor_tensor(g.left_c[:, :, :], g.left_c[:, :, :], g.dt_c[:, :, :], ALU.mult).then_inc(tail, 1)
                dve.wait_ge(tail, 6)


def ssd(g, act_buf, v_buf):
    nc, base = g.nc, g.base

    def tile(name, page):
        return g.at(name, R + page, [P, TT, P])

    def flat(b):
        return b[:, :, :].rearrange("p c n -> p (c n)")

    sel = [g.at(f"sel{s}", R + 28 + s, [SSD_HEADS, S]) for s in range(2)]
    grown = [tile(f"grown{s}", 30 + s) for s in range(2)]
    dec = [tile(f"dec{s}", 32 + s) for s in range(2)]
    attn = [tile(f"attn{s}", 34 + s) for s in range(2)]
    cg = [tile(f"cg{s}", 36 + s) for s in range(2)]
    x = tile("x", 38)
    xdt, xleft = tile("xdt", 39), tile("xleft", 40)
    st = g.at("st", R + 41, [P, TT - 1, P])
    y = g.at("y", R + 42, [P, S])
    scores = [tile(f"scores{q}", 43 + q) for q in range(SSD_GROUPS)]
    b_rows = [tile(f"b_rows{q}", 45 + q) for q in range(SSD_GROUPS)]
    m = {n: g.sem(n) for n in ("prepared", "scores_read", "b_read", "selected", "spread", "exp_made", "x_copied",
                               "diffed", "decayed", "masked", "attended", "c_scaled", "x_turned", "x_scaled",
                               "states_made", "states_added", "y_made", "y_read", "v_read")}
    pairs = SSD_HEADS // 2 // SSD_GROUPS
    n_pairs = SSD_GROUPS * pairs
    BEFORE = 2
    with ExitStack() as stack:
        wide = g.banks(stack, 2, "wide")
        prep = g.banks(stack, 2, "prep")
        xb, sb, yb = g.banks(stack, 3, "ssd")

        def chunks(b):
            return b[:, :].rearrange("p (c n) -> p c n", n=P)

        with nc.Block() as block:
            @block.sync
            def _(sp):
                stream_load(g, sp, N_SSD)

            @block.tensor
            def _(pe):
                for q in range(SSD_GROUPS):
                    if q:
                        pe.wait_ge(m["scores_read"], q)
                        pe.wait_ge(m["b_read"], q)
                    for c in range(TT):
                        w = slice(c * P, c * P + P)
                        pe.matmul(prep[0][:, w], act_buf[:, SB_ + q, w], act_buf[:, SC + q, w], start=True, stop=True)
                    for c in range(TT):
                        w = slice(c * P, c * P + P)
                        last = pe.transpose(prep[1][:, w], act_buf[:, SB_ + q, w], g.ident[:, :])
                    last.then_inc(m["prepared"], 1)
                def spread(n):
                    pe.wait_ge(m["selected"], 2 * n + 2)
                    pe.wait_ge(m["diffed"], 2 * n)
                    for s in range(2):
                        pe.matmul(wide[s][:, :], g.ones[0:SSD_HEADS, :], sel[s][:, :], start=True,
                                  stop=True).then_inc(m["spread"], 1)

                def turn(n):
                    pe.wait_ge(m["x_copied"], n + 1)
                    pe.wait_ge(m["x_scaled"], 2 * n)
                    for c in range(TT):
                        last = pe.transpose(chunks(xb)[:, c, :], x[:, c, :], g.ident[:, :])
                    last.then_inc(m["x_turned"], 1)

                def states(n, q):
                    pe.wait_ge(m["x_scaled"], 2 * n + 2)
                    for c in range(TT - 1):
                        last = pe.matmul(chunks(sb)[:, c, :], b_rows[q][:, c, :], xleft[:, c, :], start=True,
                                         stop=True)
                    last.then_inc(m["states_made"], 1)

                def output(n):
                    pe.wait_ge(m["states_added"], 5 * n + 5)
                    pe.wait_ge(m["attended"], 2 * n + 2)
                    pe.wait_ge(m["c_scaled"], 2 * n + 2)
                    pe.wait_ge(m["y_read"], n)
                    for s in range(2):
                        half = slice(64 * s, 64 * s + 64)
                        for c in range(TT):
                            last = pe.matmul(chunks(yb)[half, c, :], xdt[:, c, half], attn[s][:, c, :],
                                             start=True, stop=(c == 0))
                            if c:
                                last = pe.matmul(chunks(yb)[half, c, :], st[:, c - 1, half], cg[s][:, c, :],
                                                 start=False, stop=True)
                    last.then_inc(m["y_made"], 1)

                def v_tile(n, start, stop):
                    t = base + n
                    if start == 0:
                        pe.wait_ge(g.low_split, t + 1)
                        if n < 2:
                            pe.wait_ge(m["scores_read"], SSD_GROUPS)
                            pe.wait_ge(m["b_read"], SSD_GROUPS)
                        else:
                            pe.wait_ge(m["v_read"], n - 1)
                    last = mm_columns(g, pe, t, prep[n % 2][:, :], start=start, stop=stop)
                    if stop == DC:
                        last.then_inc(g.tile_used, 1)

                spread(0)
                turn(0)
                v_tile(0, 0, BEFORE)
                states(0, 0)
                v_tile(0, BEFORE, DC)
                for n in range(1, n_pairs):
                    spread(n)
                    turn(n)
                    v_tile(n, 0, BEFORE)
                    output(n - 1)
                    v_tile(n, BEFORE, DC)
                    states(n, n // pairs)
                output(n_pairs - 1)

            @block.scalar
            def _(act):
                for q in range(SSD_GROUPS):
                    act.wait_ge(m["prepared"], q + 1)
                    act.activation(flat(scores[q]), prep[0][:, :], ACT.Copy).then_inc(m["scores_read"], 1)
                    act.activation(flat(b_rows[q]), prep[1][:, :], ACT.Copy).then_inc(m["b_read"], 1)
                for n in range(n_pairs):
                    act.wait_ge(m["x_turned"], n)
                    act.activation(flat(x), act_buf[:, n + SX, :], ACT.Copy).then_inc(m["x_copied"], 1)
                    act.wait_ge(m["c_scaled"], 2 * n)
                    act.wait_ge(m["spread"], 2 * n + 2)
                    for s in range(2):
                        act.activation(flat(grown[s]), wide[s][:, :], ACT.Exp).then_inc(m["exp_made"], 1)
                    for s in range(2):
                        act.wait_ge(m["diffed"], 2 * n + (s + 1))
                        act.activation(flat(dec[s]), flat(dec[s]), ACT.Exp).then_inc(m["decayed"], 1)
                    split_high(g, act, 0, n + 2)
                    act.activation(v_buf[:, AV + n, :], prep[n % 2][:, :], ACT.Copy).then_inc(m["v_read"], 1)

            @block.gpsimd
            def _(pool):
                for n in range(n_pairs):
                    for s in range(2):
                        pool.wait_ge(m["decayed"], 2 * n + (s + 1))
                        pool.tensor_tensor(dec[s][:, :, :], dec[s][:, :, :],
                                           g.upto[:, :].unsqueeze(1).to_broadcast([P, TT, P]),
                                           ALU.mult).then_inc(m["masked"], 1)
                    split_low(g, pool, 0, n + 2)

            @block.vector
            def _(dve):
                def select(n):
                    for s in range(2):
                        dve.tensor_scalar(sel[s][:, :], g.rows[0:SSD_HEADS, :],
                                          g.head_mask[0:SSD_HEADS, bass.ds(2 * n + s, 1)], None,
                                          ALU.mult).then_inc(m["selected"], 1)

                def decays(n, first=False):
                    if not first:
                        dve.wait_ge(m["attended"], 2 * n)
                    for s in range(2):
                        dve.wait_ge(m["exp_made"], 2 * n + (s + 1))
                        for c in range(TT):
                            ins = dve.tensor_scalar(dec[s][:, c, :], chunks(wide[s])[:, c, :],
                                                    g.sum_c[:, bass.ds(2 * n + s, 1), c], 0.0, ALU.subtract,
                                                    ALU.min)
                        ins.then_inc(m["diffed"], 1)

                def prepare(n, q, last=False):
                    dve.wait_ge(m["x_turned"], n + 1)
                    for out, cols in ((xleft, g.left_c), (xdt, g.dt_c)):
                        for s in range(2):
                            src = xb[:, :].rearrange("p (c h d) -> p h c d", h=2, d=64)[:, s, :, :]
                            dst = out[:, :, :].rearrange("p c (h d) -> p h c d", d=64)[:, s, :, :]
                            ins = dve.tensor_tensor(
                                dst, src, cols[:, bass.ds(2 * n + s, 1), :].rearrange("p o c -> p (o c)")
                                .unsqueeze(2).to_broadcast([P, TT, 64]), ALU.mult)
                        ins.then_inc(m["x_scaled"], 1)
                    for s in range(2):
                        dve.tensor_tensor(flat(cg[s]), flat(grown[s]), act_buf[:, SC + q, :],
                                          ALU.mult).then_inc(m["c_scaled"], 1)
                    if not last:
                        dve.wait_ge(m["spread"], 2 * n + 2)
                        select(n + 1)
                    dve.wait_ge(m["states_made"], n + 1)
                    dve.tensor_copy(st[:, 0, :], chunks(sb)[:, 0, :]).then_inc(m["states_added"], 1)
                    for c in range(1, TT - 1):
                        dve.wait_ge(m["states_added"], 5 * n + (2 * c - 1))
                        for s in range(2):
                            half = slice(64 * s, 64 * s + 64)
                            dve.scalar_tensor_tensor(
                                out=st[:, c, half], in0=st[:, c - 1, half],
                                scalar=g.last_c[:, bass.ds(2 * n + s, 1), c], in1=chunks(sb)[:, c, half],
                                op0=ALU.mult, op1=ALU.add).then_inc(m["states_added"], 1)
                    for s in range(2):
                        dve.wait_ge(m["masked"], 2 * n + (s + 1))
                        dve.tensor_tensor(flat(attn[s]), flat(dec[s]), flat(scores[q]),
                                          ALU.mult).then_inc(m["attended"], 1)

                def finish_y(n):
                    dve.wait_ge(m["y_made"], n + 1)
                    dve.scalar_tensor_tensor(out=y[:, :], in0=act_buf[:, bass.ds(n + SX, 1), :]
                                             .rearrange("p o s -> p (o s)"),
                                             scalar=g.cols[:, bass.ds(n + COLS["d_skip"][0], 1)], in1=yb[:, :],
                                             op0=ALU.mult, op1=ALU.add).then_inc(m["y_read"], 1)
                    dve.wait_ge(m["y_read"], n + 1)
                    z = act_buf[:, bass.ds(n + SZ, 1), :].rearrange("p o s -> p (o s)")
                    dve.tensor_tensor(z, y[:, :], z, ALU.mult)

                select(0)
                decays(0, first=True)
                dve.wait_ge(m["scores_read"], 1)
                prepare(0, 0)
                for n in range(1, n_pairs):
                    decays(n)
                    finish_y(n - 1)
                    dve.wait_ge(m["scores_read"], n // pairs + 1)
                    prepare(n, n // pairs, last=(n == n_pairs - 1))
                finish_y(n_pairs - 1)
    g.base += N_SSD


def ssd_norm(g, act_buf):
    nc = g.nc
    g.yh = g.at("yh", R + 36, [P, DC, S], F32R)
    g.yl = g.at("yl", R + 44, [P, DC, S], F32R)
    sq = g.at("sq", R + 52, [P, 2, S])
    v = g.at("v", R + 54, [P, SSD_GROUPS, S])
    t = g.at("t", R + 56, [P, SSD_GROUPS, S])
    r = g.at("r", R + 58, [P, SSD_GROUPS, S])
    y = g.at("y", R + 60, [P, 2, S])
    squared, summed, root, scaled, high, low = (g.sem(x) for x in (
        "squared", "summed", "root", "scaled", "y_high", "y_low"))
    per = DC // SSD_GROUPS
    with ExitStack() as stack:
        banks = g.banks(stack, SSD_GROUPS, "mean")
        with nc.Block() as block:
            @block.scalar
            def _(act):
                for n in range(DC):
                    if n >= 2:
                        act.wait_ge(summed, n - 1)
                    act.activation(sq[:, n % 2, :], act_buf[:, SZ + n, :], ACT.Square).then_inc(squared, 1)
                act.wait_ge(root, 3)
                act.activation(r[:, :, :], t[:, :, :], ACT.Sqrt).then_inc(root, 1)
                for n in range(DC):
                    act.wait_ge(scaled, n + 1)
                    act.activation(g.yh[:, n, :], y[:, n % 2, :], ACT.Copy).then_inc(high, 1)

            @block.tensor
            def _(pe):
                for n in range(DC):
                    pe.wait_ge(squared, n + 1)
                    pe.matmul(banks[n // per][:, :], g.ones[:, :], sq[:, n % 2, :], start=(n % per == 0),
                              stop=(n % per == per - 1)).then_inc(summed, 1)

            @block.vector
            def _(dve):
                for q in range(SSD_GROUPS):
                    dve.wait_ge(summed, per * (q + 1))
                    dve.tensor_scalar(v[:, q, :], banks[q][:, :], 1.0 / (per * P), EPS, ALU.mult,
                                      ALU.add).then_inc(root, 1)
                dve.wait_ge(root, 2)
                dve.reciprocal(t[:, :, :], v[:, :, :]).then_inc(root, 1)
                dve.wait_ge(root, 4)
                n = refine_root(dve, r[:, :, :], v[:, :, :], t[:, :, :], root, 4)
                dve.wait_ge(root, n)
                for n in range(DC + 1):
                    if n < DC:
                        if n >= 2:
                            dve.wait_ge(low, n - 1)
                        dve.scalar_tensor_tensor(out=y[:, n % 2, :], in0=act_buf[:, SZ + n, :],
                                                 scalar=g.col("ssd_norm", n), in1=r[:, n // per, :], op0=ALU.mult,
                                                 op1=ALU.mult).then_inc(scaled, 1)
                    if n:
                        dve.wait_ge(high, n)
                        dve.tensor_tensor(g.yl[:, n - 1, :], y[:, (n - 1) % 2, :], g.yh[:, n - 1, :],
                                          ALU.subtract).then_inc(low, 1)


def stick_breaking(g, act_buf):
    nc = g.nc
    OFF = (0, 512, 1024, 896)
    WIDE = 1280
    g.oh = g.at("oh", R + AQ, [P, DC, S], F32R)
    g.ol = g.at("ol", R + AK, [P, DC, S], F32R)
    ks, qs, vs = (g.at(n, R + 16 + k, [P, S]) for k, n in enumerate(("ks", "qs", "vs")))
    vr = g.at("v_rows", R + 19, [P, TT, P])
    tmp = g.at("tmp", R + 52, [P, WIDE])
    soft = [g.at(f"soft{s}", R + 54.5 + 2.5 * s, [P, WIDE]) for s in range(2)]
    weight = [g.at(f"weight{s}", R + 59.5 + 2.5 * s, [P, WIDE]) for s in range(2)]
    m = {n: g.sem(n) for n in ("qk_copied", "v_copied", "v_turned", "v_read", "logits", "abs_made", "exp_made",
                               "log_made", "softened", "soft_masked", "summed", "weights", "masked", "out_made",
                               "out_gated", "o_high", "pool_passed")}
    with ExitStack() as stack:
        lg = [stack.enter_context(nc.psum_tensor(f"logits{s}", [P, 3 * 512], F32)) for s in range(2)]
        vb, ob = g.banks(stack, 2, "attn")
        pairs = SB_HEADS // 2

        def kb_of(buf, kb, qb=None):
            qb = kb if qb is None else qb
            return buf[:, OFF[kb] + (qb - kb) * P:OFF[kb] + (TT - kb) * P]

        with nc.Block() as block:
            @block.tensor
            def _(pe):
                def logits(s):
                    half = slice(64 * s, 64 * s + 64)
                    for kb in (0, 1, 3, 2):
                        last = pe.matmul(kb_of(lg[s], kb), ks[half, kb * P:kb * P + P],
                                         qs[half, kb * P:], start=(kb != 3), stop=True,
                                         skip_group_check=True)
                    last.then_inc(m["logits"], 1)

                def sums(n, s):
                    pe.wait_ge(m["soft_masked"], 2 * n + (s + 1))
                    for kb in range(TT):
                        for k2 in range(kb, TT):
                            last = pe.matmul(kb_of(lg[s], kb, k2), (g.neg_from if k2 == kb else g.neg_ones)[:, :],
                                             kb_of(soft[s], k2), start=False, stop=True, skip_group_check=True)
                    last.then_inc(m["summed"], 1)

                def turn_v(n):
                    pe.wait_ge(m["v_copied"], n + 1)
                    pe.wait_ge(m["v_read"], n + 1)
                    for c in range(TT):
                        last = pe.transpose(vb[:, c * P:c * P + P], vs[:, c * P:c * P + P], g.ident[:, :])
                    last.then_inc(m["v_turned"], 1)

                def output(n, s):
                    pe.wait_ge(m["masked"], 2 * n + (s + 1))
                    if s == 0:
                        pe.wait_ge(m["v_read"], n + 2)
                        pe.wait_ge(m["out_gated"], n + 1)
                    half = slice(64 * s, 64 * s + 64)
                    for kb in range(TT):
                        last = pe.matmul(ob[half, kb * P:], vr[:, kb, half], kb_of(weight[s], kb),
                                         start=(kb == 0), stop=(kb == TT - 1), skip_group_check=True)
                    last.then_inc(m["out_made"], 1)

                pe.wait_ge(m["qk_copied"], 2)
                logits(0)
                logits(1)
                sums(0, 0)
                with steps(pe, 0, pairs - 1, 1) as n:
                    turn_v(n)
                    pe.wait_ge(m["qk_copied"], 2 * n + 4)
                    for s in range(2):
                        pe.wait_ge(m["weights"], 2 * n + (s + 1))
                        logits(s)
                        sums(n + s, 1 - s)
                        output(n, s)
                turn_v(pairs - 1)
                sums(pairs - 1, 1)
                output(pairs - 1, 0)
                output(pairs - 1, 1)

            @block.scalar
            def _(act):
                def softplus(n, s):
                    act.wait_ge(m["logits"], 2 * n + (s + 1))
                    if not (isinstance(n, int) and n == 0 and s == 0):
                        act.wait_ge(m["softened"], 2 * n + s)
                    act.activation(tmp[:, :], lg[s][:, 0:WIDE], ACT.Abs).then_inc(m["abs_made"], 1)
                    act.wait_ge(m["abs_made"], 2 * n + (s + 1))
                    act.activation(tmp[:, :], tmp[:, :], ACT.Exp, scale=-1.0).then_inc(m["exp_made"], 1)
                    act.wait_ge(m["exp_made"], 2 * n + (s + 1))
                    act.activation(tmp[:, :], tmp[:, :], ACT.Ln, bias=1.0).then_inc(m["log_made"], 1)

                def weigh(n, s):
                    act.wait_ge(m["summed"], 2 * n + (s + 1))
                    act.activation(weight[s][:, :], lg[s][:, 0:WIDE], ACT.Exp).then_inc(m["weights"], 1)

                softplus(0, 0)
                softplus(0, 1)
                weigh(0, 0)
                with steps(act, 0, pairs - 1, 1) as n:
                    for s in range(2):
                        softplus(n + 1, s)
                        weigh(n + s, 1 - s)
                weigh(pairs - 1, 1)

            @block.gpsimd
            def _(pool):
                def mask(buf, ready, count, sem):
                    pool.wait_ge(ready, count)
                    pool.sem_inc(m["pool_passed"], 1)
                    for kb in range(TT):
                        v = buf[:, OFF[kb]:OFF[kb] + P]
                        ins = pool.affine_select(out=v, in_=v, compare_op=ALU.is_gt, fill=0.0, base=0,
                                                 pattern=[[1, P]], channel_multiplier=-1)
                    ins.then_inc(sem, 1)

                def mask_soft(n, s):
                    mask(soft[s], m["softened"], 2 * n + (s + 1), m["soft_masked"])

                def mask_weight(n, s):
                    mask(weight[s], m["weights"], 2 * n + (s + 1), m["masked"])

                mask_soft(0, 0)
                mask_soft(0, 1)
                mask_weight(0, 0)
                with steps(pool, 0, pairs - 1, 1) as n:
                    for s in range(2):
                        mask_soft(n + 1, s)
                        mask_weight(n + s, 1 - s)
                mask_weight(pairs - 1, 1)

            @block.vector
            def _(dve):
                def copy(n, dst, src, sem):
                    dve.tensor_copy(dst[:, :], act_buf[:, bass.ds(n + src, 1), :].rearrange("p o s -> p (o s)"))\
                       .then_inc(sem, 1)

                def soften(n, s):
                    dve.wait_ge(m["log_made"], 2 * n + (s + 1))
                    if not (isinstance(n, int) and n == 0):
                        dve.wait_ge(m["summed"], 2 * n + (s - 1))
                    dve.scalar_tensor_tensor(out=soft[s][:, :], in0=lg[s][:, 0:WIDE], scalar=0.0, in1=tmp[:, :],
                                             op0=ALU.max, op1=ALU.add).then_inc(m["softened"], 1)

                def v_rows(n):
                    dve.wait_ge(m["v_turned"], n + 1)
                    dve.tensor_copy(vr[:, :, :].rearrange("p c n -> p (c n)"), vb[:, :]).then_inc(m["v_read"], 1)

                def gate(n):
                    dve.wait_ge(m["out_made"], 2 * n + 2)
                    z, high, low = (buf[:, bass.ds(n + at, 1), :].rearrange("p o s -> p (o s)")
                                    for buf, at in ((act_buf, AZ), (g.oh, 0), (g.ol, 0)))
                    dve.tensor_tensor(z, ob[:, :], z, ALU.mult).then_inc(m["out_gated"], 1)
                    dve.wait_ge(m["out_gated"], n + 2)
                    dve.tensor_copy(high, z).then_inc(m["o_high"], 1)
                    dve.wait_ge(m["o_high"], n + 1)
                    dve.tensor_tensor(low, z, high, ALU.subtract)

                dve.sem_inc(m["v_read"], 1)
                dve.sem_inc(m["out_gated"], 1)
                copy(0, ks, AK, m["qk_copied"])
                copy(0, qs, AQ, m["qk_copied"])
                copy(0, vs, AV, m["v_copied"])
                soften(0, 0)
                soften(0, 1)
                with steps(dve, 0, pairs - 1, 1) as n:
                    dve.wait_ge(m["logits"], 2 * n + 2)
                    copy(n + 1, ks, AK, m["qk_copied"])
                    copy(n + 1, qs, AQ, m["qk_copied"])
                    v_rows(n)
                    copy(n + 1, vs, AV, m["v_copied"])
                    soften(n + 1, 0)
                    soften(n + 1, 1)
                    gate(n)
                v_rows(pairs - 1)
                gate(pairs - 1)


def finish(g, banks):
    nc = g.nc
    wp = g.at("norm_post", R, [P, D])
    junk = g.at("junk", R + 2, [P, 512])
    res = g.at("res", R + 3, [P, TT, D])
    ss = g.at("ss", R + 11, [P, TT, 2])
    st = g.at("stats", R + 11.5, [P, 4, TT])
    loaded, summed, root, scaled, added = (g.sem(x) for x in ("post_loaded", "summed", "root", "scaled", "added"))
    stored = g.sem("stored")
    with nc.Block() as block:
        @block.sync
        def _(sp):
            sp.dma_start(wp[:, :], g.io["norm_post"]).then_inc(loaded, 16)
            for t in range(TT):
                sp.wait_ge(added, 2 * t + 2)
                sp.dma_start(g.io["out"][t * P:t * P + P, :], res[:, t, :]).then_inc(stored, 16)
            sp.wait_ge(stored, 16 * TT)
            for j in range(RAW):
                sp.wait_ge(g.raw_loaded[j], 16 * (g.total // RAW))

        @block.scalar
        def _(act):
            for q in range(2 * TT):
                act.activation(junk[:, :], banks[q][:, :], ACT.Square, accum_out=ss[:, q // 2, q % 2:q % 2 + 1])\
                   .then_inc(summed, 1)
                act.wait_ge(summed, q + 1)
            act.wait_ge(root, 3)
            act.activation(st[:, 2, :], st[:, 1, :], ACT.Sqrt).then_inc(root, 1)

        @block.vector
        def _(dve):
            dve.wait_ge(summed, 2 * TT)
            dve.tensor_reduce(st[:, 0, :], ss[:, :, :], AX.X, ALU.add).then_inc(root, 1)
            dve.wait_ge(root, 1)
            dve.tensor_scalar(st[:, 0, :], st[:, 0, :], 1.0 / D, EPS, ALU.mult, ALU.add).then_inc(root, 1)
            dve.wait_ge(root, 2)
            dve.reciprocal(st[:, 1, :], st[:, 0, :]).then_inc(root, 1)
            dve.wait_ge(root, 4)
            n = refine_root(dve, st[:, 2, :], st[:, 0, :], st[:, 3, :], root, 4)
            dve.wait_ge(root, n)
            dve.wait_ge(loaded, 16)
            for q in range(2 * TT):
                t, w = q // 2, slice(q % 2 * 512, q % 2 * 512 + 512)
                dve.scalar_tensor_tensor(out=res[:, t, w], in0=banks[q][:, :], scalar=st[:, 2, t:t + 1],
                                         in1=wp[:, w], op0=ALU.mult, op1=ALU.mult).then_inc(scaled, 1)
            for q in range(2 * TT):
                t, w = q // 2, slice(q % 2 * 512, q % 2 * 512 + 512)
                dve.wait_ge(scaled, q + 1)
                dve.tensor_tensor(res[:, t, w], res[:, t, w], g.h[:, t, w], ALU.add).then_inc(added, 1)


def build(nc, io):
    g = Program(nc, io)
    setup(g)

    with ExitStack() as stack:
        act1 = g.at("act1", R, [P, N_PROJ1, S])
        rows1 = g.banks(stack, 1, "rows1")[0]
        g.run(normed_columns, "mix_norm", small=(io["w_ba"], rows1[0:64, :]))
        g.run(project, act1, N_PROJ1, ((4, XA, ACT.Copy, 1.0), (8, Z, ACT.Silu, 1.0)), "conv1")
        g.run(delta_rows, act1, rows1)
    g.run(delta_rule, act1)
    g.run(delta_norm, act1)
    g.run(pool_mix)
    g.run(merge, (g.ph, g.pl), len(POOL_WINDOWS), (g.yh, g.yl), io["x"])
    with ExitStack() as stack:
        g.run(mix_out, stack)

    g.run(normed_columns, "ffn_norm")
    g.run(peer_scores)
    g.run(peer_pick)
    g.run(peer_gates)
    g.run(peer_early)
    g.run(peer_experts)

    rows2 = nc.dram_tensor("rows2", [S, D], F32, kind="Internal").ap()
    with ExitStack() as stack:
        dt_ps = g.banks(stack, 1, "dt")[0]
        g.run(normed_columns, "pre2", (io["w_dt"], dt_ps[0:SSD_HEADS, :]), io["final_norm"], rows2)
        act2 = g.at("act2a", R, [P, N_PROJ2A, S])
        g.run(project, act2, N_PROJ2A, ((8, SZ, ACT.Silu, 1.0),), "conv2", "conv2_b")
        g.run(ssd_rows, dt_ps)
    act2b = g.at("act2b", R, [P, AZ + DC, S])
    g.run(ssd, act2, act2b)
    g.run(ssd_norm, act2)

    g.run(project, act2b, N_PROJ2B, ((8, AQ, ACT.Copy, 64 ** -0.5), (8, AK, ACT.Copy, 1.0), (8, AZ, ACT.Silu, 1.0)))
    g.run(stick_breaking, act2b)
    g.run(merge, (g.yh, g.yl), DC, (g.oh, g.ol), rows2, "gate2_b")
    with ExitStack() as stack:
        g.run(finish, g.run(mix_out, stack))
    assert g.base == g.total
    return g



def _tiles(w):
    k, n = w.shape
    t = w.reshape(k // P, P, n // P, P).transpose(2, 1, 0, 3).reshape(n // P, P, k)
    return np.pad(t, ((0, 0), (0, 0), (0, TILE - k)))


def _columns(v):
    return np.asarray(v).reshape(-1, P).T


def layout(a):
    a = {k: np.asarray(v) for k, v in a.items()}
    w1, w2 = a["w_in"][0], a["w_in_2"][0]
    t1, lg = 512 + 4096, 512 + 4096 + 16
    stream = [_tiles(w1[:, 0:512]), _tiles(w1[:, 512 + 3072:t1]), _tiles(w1[:, 512:512 + 3072])]
    ga, gb = _tiles(w1[:, lg:lg + D]), _tiles(w1[:, lg + D:])
    stream.append(np.stack([ga, _tiles(a["w_pool_up"][0]), gb, _tiles(a["w_dn_up"][0])], 1).reshape(-1, P, TILE))
    stream.append(a["w_mix_out"][0].reshape(DC, P, D))
    stream.append(_tiles(a["peer_w_query"][0]))
    down = _tiles(a["peer_down"][0].T)
    up = a["peer_up"][0].reshape(N_KEYS, P, D)
    stream += [down[:EARLY], up[:EARLY]]
    stream.append(np.stack([down[EARLY:].reshape(-1, 4, P, TILE), up[EARLY:].reshape(-1, 4, P, TILE)], 1)
                  .reshape(-1, P, TILE))
    z, xbc, dt, q = 1024, 2560, 2576, 2576 + 1024
    stream += [_tiles(w2[:, 0:z]), _tiles(w2[:, z:xbc]), _tiles(w2[:, dt + 2048:dt + 3072]),
               _tiles(w2[:, dt:dt + 2048]), _tiles(w2[:, dt + 3072:dt + 4096])]
    g0 = dt + 4096
    stream.append(np.stack([_tiles(w2[:, g0:g0 + D]), _tiles(a["w_ssd_proj_2"][0]), _tiles(w2[:, g0 + D:]),
                            _tiles(a["w_sb_proj_2"][0])], 1).reshape(-1, P, TILE))
    stream.append(a["w_out_2"][0].reshape(DC, P, D))
    stream = np.concatenate(stream)
    assert len(stream) == N_TILES

    def taps(w):
        return w.reshape(TAPS, -1, P).transpose(2, 1, 0).reshape(P, -1)

    cols = np.concatenate([
        _columns(a["mix_norm_w"]), _columns(a["ffn_norm_w"]), _columns(a["norm_pre_2"]), _columns(a["pool_scale"]),
        taps(a["conv_w"][0]), _columns(a["dn_norm_w"]), taps(a["conv_w_2"][0]), _columns(a["conv_b_2"]),
        _columns(a["ssd_norm_2"]), _columns(a["b_gate_2"]), _columns(np.repeat(a["d_skip_2"][0], 64))], 1)
    assert cols.shape == (P, N_COLS)
    heads = np.zeros((SSD_HEADS, 4), np.float32)
    heads[:8, 0], heads[:8, 1] = a["a_log"][0], a["dt_bias"][0]
    heads[:, 2], heads[:, 3] = a["a_log_2"][0], a["dt_bias_2"][0]
    ba = np.zeros((P, DC, 64), np.float32)
    ba[:, :, 0:8] = w1[:, t1 + 8:lg].reshape(DC, P, 8).transpose(1, 0, 2)
    ba[:, :, 32:40] = w1[:, t1:t1 + 8].reshape(DC, P, 8).transpose(1, 0, 2)
    keys = np.stack([a["peer_keys_1"][0], a["peer_keys_2"][0]], 1).reshape(16, N_KEYS, P)
    return {
        "x": a["x"][0], "stream": stream, "cols": cols, "heads": heads, "w_ba": ba,
        "w_dt": w2[:, xbc:dt].reshape(DC, P, 16).transpose(1, 0, 2),
        "pool_w": a["pool_w"][0].transpose(1, 0, 2), "keys": keys.transpose(2, 0, 1),
        "final_norm": np.tile(a["final_norm_w"], (P, 1)), "norm_post": np.tile(a["norm_post_2"][0], (P, 1)),
    }


def program(nc, shapes):
    io = {k: nc.dram_tensor(f"in_{k}", s, F32, kind="ExternalInput").ap() for k, s in shapes.items()}
    io["out"] = nc.dram_tensor("out", [S, D], F32, kind="ExternalOutput").ap()
    return build(nc, io)


def kernel(**inputs):
    import concourse.bacc as _bacc
    from concourse.bass_utils import run_bass_kernel_spmd as _run

    arrays = {k: np.ascontiguousarray(v) for k, v in layout(inputs).items()}
    nc = _bacc.Bacc("TRN2", target_bir_lowering=False, num_devices=1)
    program(nc, {k: v.shape for k, v in arrays.items()})
    r = _run(nc, [{f"in_{k}": v for k, v in arrays.items()}], core_ids=[0])
    return r.results[0]["out"].reshape(1, S, D)
```
